# Optimizing a Trainium2 kernel written in Bass

```python
import math
import jax, jax.numpy as jnp
from jax import lax
import numpy as np

D_MODEL = 1024
BATCH = 1
SEQ = 512
DEPTH = 2

N_MEM = 256
HEAD_DIM = 64
DSA_HEADS = 6
GDN_HEADS = 6
MEM_HEADS = 4
DSA_W = DSA_HEADS * HEAD_DIM
GDN_W = GDN_HEADS * HEAD_DIM
MEM_W = MEM_HEADS * HEAD_DIM
MIX_W = DSA_W + GDN_W + MEM_W
IDX_HEADS = 8
IDX_DIM = 32
TOPK_MAX = 256
Q_BLOCK = 128
GDN_CHUNK = 64
CONV_WIDTH = 4
NUM_BUCKETS = 32
MAX_DISTANCE = 128
D_FF = 2816
EPS = 1e-6
IN_SPLIT_SIZES = (
    DSA_W, DSA_W, DSA_W,
    IDX_HEADS * IDX_DIM, IDX_DIM, IDX_HEADS,
    GDN_W, GDN_W, GDN_W, GDN_W,
    GDN_HEADS, GDN_HEADS,
    MEM_W,
)
IN_W = sum(IN_SPLIT_SIZES)

kernel_name = 'hybrid_dsa_gdn_memory_macaron'

def rms_norm(x, gain):
    xf = x.astype(jnp.float32)
    y = xf * lax.rsqrt(jnp.mean(xf * xf, axis=-1, keepdims=True) + EPS)
    return (y * gain.astype(jnp.float32)).astype(x.dtype)

def l2_norm(x):
    return x * lax.rsqrt(jnp.sum(x * x, axis=-1, keepdims=True) + EPS)

def swiglu(h, w_gate, w_up, w_down):
    return (jax.nn.silu(h @ w_gate) * (h @ w_up)) @ w_down

def split_columns(p):
    offsets, acc = [], 0
    for s in IN_SPLIT_SIZES[:-1]:
        acc += s
        offsets.append(acc)
    return jnp.split(p, offsets, axis=-1)

def t5_bucket(dist):
    n = jnp.maximum(dist, 0)
    max_exact = NUM_BUCKETS // 2
    nf = jnp.maximum(n, 1).astype(jnp.float32)
    large = max_exact + (jnp.log(nf / max_exact) / math.log(MAX_DISTANCE / max_exact)
                         * (NUM_BUCKETS - max_exact)).astype(jnp.int32)
    large = jnp.minimum(large, NUM_BUCKETS - 1)
    return jnp.where(n < max_exact, n, large)

def dsa_attention(q, k, v, q_idx, k_idx, w_idx, rel_bias):
    B, T, H, dh = q.shape
    top_k = min(TOPK_MAX, T // 4)
    nb = T // Q_BLOCK
    key_pos = jnp.arange(T, dtype=jnp.int32)
    gather = jax.vmap(lambda src, idx: src[idx])

    def blocks(a):
        return jnp.moveaxis(a.reshape(B, nb, Q_BLOCK, *a.shape[2:]), 1, 0)

    def one_block(args):
        blk, qb, qib, wb = args
        q_pos = blk * Q_BLOCK + jnp.arange(Q_BLOCK, dtype=jnp.int32)
        admissible = key_pos[None, :] <= q_pos[:, None]
        head_scores = jax.nn.relu(jnp.einsum('bqhd,bsd->bqhs', qib, k_idx).astype(jnp.float32))
        score = jnp.einsum('bqhs,bqh->bqs', head_scores, wb.astype(jnp.float32))
        score = jnp.where(admissible[None], score, -jnp.inf)
        _, sel = lax.top_k(score, top_k)
        k_sel = gather(k, sel)
        v_sel = gather(v, sel)
        logits = jnp.einsum('bqhd,bqkhd->bhqk', qb, k_sel).astype(jnp.float32) * dh ** -0.5
        dist = q_pos[None, :, None] - sel
        bias = rel_bias.astype(jnp.float32)[t5_bucket(dist)]
        logits = logits + jnp.moveaxis(bias, 3, 1)
        logits = jnp.where((dist >= 0)[:, None], logits, -jnp.inf)
        p = jax.nn.softmax(logits, axis=-1).astype(v.dtype)
        return jnp.einsum('bhqk,bqkhd->bqhd', p, v_sel)

    out = lax.map(one_block, (jnp.arange(nb, dtype=jnp.int32), blocks(q), blocks(q_idx), blocks(w_idx)))
    return jnp.moveaxis(out, 0, 1).reshape(B, T, H, dh)

def causal_depthwise_conv(x, w):
    C = x.shape[-1]
    return lax.conv_general_dilated(
        x, w[:, None, :].astype(x.dtype), window_strides=(1,),
        padding=[(CONV_WIDTH - 1, 0)], dimension_numbers=('NWC', 'WIO', 'NWC'),
        feature_group_count=C)

def gated_delta_rule_chunked(q, k, v, g, beta):
    B, T, H, dk = q.shape
    dv = v.shape[-1]
    C = GDN_CHUNK
    N = T // C

    def to_chunks(a):
        return jnp.moveaxis(a.reshape(B, N, C, H, *a.shape[3:]), 3, 1)

    q, k, v, g, beta = (to_chunks(a) for a in (q, k, v, g, beta))
    g_cum = jnp.cumsum(g, axis=-1)
    causal = jnp.tril(jnp.ones((C, C), dtype=bool))
    strict = jnp.tril(jnp.ones((C, C), dtype=bool), -1)
    decay = jnp.exp(jnp.where(causal, g_cum[..., :, None] - g_cum[..., None, :], -jnp.inf))
    k_beta = k * beta[..., None]
    v_beta = v * beta[..., None]
    lower = jnp.where(strict, jnp.einsum('bhncd,bhnsd->bhncs', k_beta, k) * decay, 0.0)
    t_mat = jnp.eye(C, dtype=jnp.float32) + lower
    u = lax.linalg.triangular_solve(t_mat, v_beta, left_side=True, lower=True, unit_diagonal=True)
    w = lax.linalg.triangular_solve(t_mat, k_beta * jnp.exp(g_cum)[..., None],
                                    left_side=True, lower=True, unit_diagonal=True)
    attn_intra = jnp.where(causal, jnp.einsum('bhncd,bhnsd->bhncs', q, k) * decay, 0.0)

    def step(S, xs):
        q_c, k_c, u_c, w_c, g_c, a_c = xs
        v_new = u_c - jnp.einsum('bhcd,bhde->bhce', w_c, S)
        o = jnp.einsum('bhcd,bhde->bhce', q_c * jnp.exp(g_c)[..., None], S) \
            + jnp.einsum('bhcs,bhse->bhce', a_c, v_new)
        g_last = g_c[..., -1]
        S = S * jnp.exp(g_last)[..., None, None] + jnp.einsum(
            'bhcd,bhce->bhde', k_c * jnp.exp(g_last[..., None] - g_c)[..., None], v_new)
        return S, o

    xs = tuple(jnp.moveaxis(a, 2, 0) for a in (q, k, u, w, g_cum, attn_intra))
    S0 = jnp.zeros((B, H, dk, dv), jnp.float32)
    _, o = lax.scan(step, S0, xs)
    return jnp.transpose(o, (1, 0, 3, 2, 4)).reshape(B, T, H, dv)

def gdn_mixer(q, k, v, z, a, b_in, conv_w, A_log, dt_bias, out_gain):
    B, T, _ = q.shape
    qkv = jax.nn.silu(causal_depthwise_conv(jnp.concatenate([q, k, v], axis=-1), conv_w))
    q, k, v = jnp.split(qkv, 3, axis=-1)
    heads = lambda t: t.reshape(B, T, GDN_HEADS, HEAD_DIM).astype(jnp.float32)
    qh = l2_norm(heads(q)) * HEAD_DIM ** -0.5
    kh = l2_norm(heads(k))
    vh = heads(v)
    beta = jax.nn.sigmoid(b_in.astype(jnp.float32))
    g = -jnp.exp(A_log.astype(jnp.float32)) * jax.nn.softplus(a.astype(jnp.float32) + dt_bias.astype(jnp.float32))
    o = gated_delta_rule_chunked(qh, kh, vh, g, beta)
    o = rms_norm(o, out_gain) * jax.nn.silu(heads(z))
    return o.reshape(B, T, GDN_W).astype(z.dtype)

def memory_attention(q, mem_kv, q_gain, k_gain):
    B, T, _ = q.shape
    M = mem_kv.shape[1]
    qh = rms_norm(q.reshape(B, T, MEM_HEADS, HEAD_DIM), q_gain)
    km, vm = jnp.split(mem_kv, 2, axis=-1)
    kh = rms_norm(km.reshape(B, M, MEM_HEADS, HEAD_DIM), k_gain)
    vh = vm.reshape(B, M, MEM_HEADS, HEAD_DIM)
    logits = jnp.einsum('bthd,bmhd->bhtm', qh, kh).astype(jnp.float32) * HEAD_DIM ** -0.5
    p = jax.nn.softmax(logits, axis=-1).astype(vh.dtype)
    return jnp.einsum('bhtm,bmhd->bthd', p, vh).reshape(B, T, MEM_W)

def setup_inputs(seed: int = 0) -> dict:
    key = jax.random.key(seed)
    ks = jax.random.split(key, 24)
    nrm = lambda k, shape, scale: jax.random.normal(k, shape, jnp.float32) * scale
    gain = lambda k, shape: 1.0 + 0.05 * jax.random.normal(k, shape, jnp.float32)
    return {
        'x': nrm(ks[0], (BATCH, SEQ, D_MODEL), 1.0),
        'mem': nrm(ks[1], (BATCH, N_MEM, D_MODEL), 1.0),
        'ffn1_norm': gain(ks[2], (DEPTH, D_MODEL)),
        'ffn1_w_gate': nrm(ks[3], (DEPTH, D_MODEL, D_FF), D_MODEL ** -0.5),
        'ffn1_w_up': nrm(ks[4], (DEPTH, D_MODEL, D_FF), D_MODEL ** -0.5),
        'ffn1_w_down': nrm(ks[5], (DEPTH, D_FF, D_MODEL), D_FF ** -0.5),
        'mix_norm': gain(ks[6], (DEPTH, D_MODEL)),
        'w_in': nrm(ks[7], (DEPTH, D_MODEL, IN_W), D_MODEL ** -0.5),
        'dsa_q_norm': gain(ks[8], (DEPTH, HEAD_DIM)),
        'dsa_k_norm': gain(ks[9], (DEPTH, HEAD_DIM)),
        'rel_bias': nrm(ks[10], (NUM_BUCKETS, DSA_HEADS), 0.5),
        'gdn_conv': nrm(ks[11], (DEPTH, CONV_WIDTH, 3 * GDN_W), CONV_WIDTH ** -0.5),
        'gdn_A_log': jnp.log(jax.random.uniform(ks[12], (DEPTH, GDN_HEADS), jnp.float32, 1.0, 16.0)),
        'gdn_dt_bias': nrm(ks[13], (DEPTH, GDN_HEADS), 0.1),
        'gdn_out_norm': gain(ks[14], (DEPTH, HEAD_DIM)),
        'mem_norm': gain(ks[15], (DEPTH, D_MODEL)),
        'w_mem_kv': nrm(ks[16], (DEPTH, D_MODEL, 2 * MEM_W), D_MODEL ** -0.5),
        'mem_q_norm': gain(ks[17], (DEPTH, HEAD_DIM)),
        'mem_k_norm': gain(ks[18], (DEPTH, HEAD_DIM)),
        'w_out': nrm(ks[19], (DEPTH, MIX_W, D_MODEL), MIX_W ** -0.5),
        'ffn2_norm': gain(ks[20], (DEPTH, D_MODEL)),
        'ffn2_w_gate': nrm(ks[21], (DEPTH, D_MODEL, D_FF), D_MODEL ** -0.5),
        'ffn2_w_up': nrm(ks[22], (DEPTH, D_MODEL, D_FF), D_MODEL ** -0.5),
        'ffn2_w_down': nrm(ks[23], (DEPTH, D_FF, D_MODEL), D_FF ** -0.5),
    }

def reference(x, mem, ffn1_norm, ffn1_w_gate, ffn1_w_up, ffn1_w_down, mix_norm, w_in,
              dsa_q_norm, dsa_k_norm, rel_bias, gdn_conv, gdn_A_log, gdn_dt_bias,
              gdn_out_norm, mem_norm, w_mem_kv, mem_q_norm, mem_k_norm, w_out,
              ffn2_norm, ffn2_w_gate, ffn2_w_up, ffn2_w_down):
    B, T, _ = x.shape
    for l in range(DEPTH):
        x = x + 0.5 * swiglu(rms_norm(x, ffn1_norm[l]), ffn1_w_gate[l], ffn1_w_up[l], ffn1_w_down[l])
        h = rms_norm(x, mix_norm[l])
        (dq, dk, dv, iq, ik, iw, gq, gk, gv, gz, ga, gb, mq) = split_columns(h @ w_in[l])
        qa = rms_norm(dq.reshape(B, T, DSA_HEADS, HEAD_DIM), dsa_q_norm[l])
        ka = rms_norm(dk.reshape(B, T, DSA_HEADS, HEAD_DIM), dsa_k_norm[l])
        va = dv.reshape(B, T, DSA_HEADS, HEAD_DIM)
        q_idx = iq.reshape(B, T, IDX_HEADS, IDX_DIM) * IDX_DIM ** -0.5
        w_idx = iw * IDX_HEADS ** -0.5
        out_a = dsa_attention(qa, ka, va, q_idx, ik, w_idx, rel_bias).reshape(B, T, DSA_W)
        out_b = gdn_mixer(gq, gk, gv, gz, ga, gb, gdn_conv[l], gdn_A_log[l], gdn_dt_bias[l], gdn_out_norm[l])
        mem_kv = rms_norm(mem, mem_norm[l]) @ w_mem_kv[l]
        out_c = memory_attention(mq, mem_kv, mem_q_norm[l], mem_k_norm[l])
        x = x + jnp.concatenate([out_a, out_b, out_c], axis=-1) @ w_out[l]
        x = x + 0.5 * swiglu(rms_norm(x, ffn2_norm[l]), ffn2_w_gate[l], ffn2_w_up[l], ffn2_w_down[l])
    return x


_drawn_inputs = setup_inputs


def setup_inputs(seed=0):
    import zlib

    import numpy as np

    out = dict(_drawn_inputs(seed))
    spreads = {}
    factors = {'dsa_q_norm': 6.141,
     'dsa_k_norm': 5.895,
     'gdn_dt_bias': 5.069,
     'mem_norm': 7.448,
     'mem_q_norm': 8.0,
     'mem_k_norm': 8.0}
    for name, (base, spread) in spreads.items():
        noise = np.random.default_rng([zlib.crc32(name.encode()), seed]).standard_normal(out[name].shape)
        drawn = base * np.exp(spread * noise) if base else spread * noise
        out[name] = __import__('jax').numpy.asarray(drawn.astype(out[name].dtype))
    for name, factor in factors.items():
        out[name] = (out[name] * factor).astype(out[name].dtype)
    return out
```

```python
import math
from contextlib import ExitStack

import numpy as np

import concourse.bass as bass
from concourse import mybir

F32 = mybir.dt.float32
F32R = mybir.dt.float32r
ALU = mybir.AluOpType
ACT = mybir.ActivationFunctionType
AX = mybir.AxisListType

P = 128
EPS = 1e-6
T = 512
D = 1024
KD = D // P
NM = 256
DH = 64
FF = 2816
NF = FF // P
H_A, H_B, H_M = 6, 6, 4
H_I, D_I = 8, 32
TOPK = 128
NB = T // P
BUCKETS = 32
MAX_DIST = 128
CONV = 4
NEG = -1.0e30
GONE = -3.0e38
WA, WB, WM = H_A * DH, H_B * DH, H_M * DH
UNIT_COLS = 256
UNIT = KD * UNIT_COLS

O_DQ, O_DV = 0, 2 * WA
O_IQ = 3 * WA
O_IK = O_IQ + H_I * D_I
O_IW = O_IK + D_I
O_G = O_IW + H_I
O_GA = O_G + 4 * WB
O_MQ = O_GA + 2 * H_B
SM = H_I + 2 * H_B

PARTS = [(0, 8), (8, 15), (15, NF)]
GU_UNITS = 2 * (FF // UNIT_COLS)
DN_UNITS = len(PARTS) * (D // UNIT_COLS)
MIX_UNITS = 20
U_FFN = [0, GU_UNITS + DN_UNITS + MIX_UNITS]
U_MIX = GU_UNITS + DN_UNITS
LAYER_UNITS = 2 * (GU_UNITS + DN_UNITS) + MIX_UNITS

MIX_SRC = (["iq", (O_DQ, 256), "small", (O_DQ + 256, 256), (O_DQ + 512, 256), (O_DV, 256), (O_DV + 256, 128)]
           + [(O_MQ, 256)] + ["mk", "mv"] + [(O_G + 256 * i, 256) for i in range(6)]
           + [("out", i) for i in range(4)])
assert len(MIX_SRC) == MIX_UNITS
SMALL_UNIT = U_MIX + 2
SMALL_DMAS = P // D_I + 2


def unit_dmas(v):
    return SMALL_DMAS if v == SMALL_UNIT else 1


def landed_value(v):
    return 16 * sum(unit_dmas(w) for w in range(2, v + 1) if w % 2 == v % 2)


COL_DMAS = 4 + 2 * 5 + 3

GROUPS = []


def _groups():
    def g(name, u, kind, **kw):
        GROUPS.append(dict(name=name, unit=U_MIX + u, kind=kind, **kw))
    for c in range(2):
        g("iq", 0, "T", c=c, col=128 * c)
    for c in range(2):
        g("dq", 1, "T", c=c, col=128 * c, norm=True)
    g("ik", 2, "T", c=0, col=0)
    g("sm", 2, "S")
    for c in range(2, 6):
        g("dq" if c < 3 else "dk", 2 + c // 2, "T", c=c % 3, col=128 * (c % 2), norm=True)
    for b in range(NB):
        g("va", 5, "N", b=b, n=256)
    for b in range(NB):
        g("vb", 6, "N", b=b, n=128)
    for c in range(2):
        g("mq", 7, "T", c=c, col=128 * c, norm=True)
    for c in range(2):
        g("mk", 8, "M", c=c, col=128 * c, norm=True)
    for b in range(2):
        g("mv", 9, "V", b=b)
    for c in range(12):
        g(("gq", "gk", "gv", "gz")[c // 3], 10 + c // 2, "T", c=c % 3, col=128 * (c % 2))


_groups()
N_GROUPS = len(GROUPS)
GATE_GROUP = 5
FIRST_CONV = 24
NORM_OF = {i: sum(1 for x in GROUPS[:i] if x.get("norm")) for i, g in enumerate(GROUPS) if g.get("norm")}
N_NORM_A = sum(1 for g in GROUPS if g.get("norm"))
LAST_OF_UNIT = {g["unit"]: i for i, g in enumerate(GROUPS)}

LEVELS = 6
(S_ROWS, S_DECAY, S_KK, S_QK, S_INV) = range(5)
S_LEVEL = 5
S_UW = S_LEVEL + 2 * (LEVELS - 1)
S_REC = S_UW + 1
S_OUT = S_REC + 4
N_STEPS = S_OUT + 3

JOBS = H_A + H_M
SLOTS = JOBS + 2
JOB_SLOT = {1 + (n * (N_STEPS - 2)) // SLOTS: n for n in range(SLOTS)}
assert len(JOB_SLOT) == SLOTS

N_PE, N_ACT, N_DVE, N_POOL = 26, 12, 25, 3


def t5_bucket():
    n = np.arange(0, T)
    exact = BUCKETS // 2
    nf = np.maximum(n, 1).astype(np.float32)
    large = exact + (np.log(nf / np.float32(exact)) / np.float32(math.log(MAX_DIST / exact))
                     * np.float32(BUCKETS - exact)).astype(np.int32)
    return np.where(n < exact, n, np.minimum(large, BUCKETS - 1))


def constants():
    p = np.arange(P)[:, None]
    c = np.arange(P)[None, :]
    c64 = np.arange(DH)[None, :]
    f = {}
    f["ident"] = (p == c)
    f["ones"] = np.ones((P, P))
    f["same64"] = (p // 64 == c // 64)
    f["prefix"] = (p // 64 == c // 64) & (p <= c)
    f["suffix"] = (p // 64 == c // 64) & (p > c)
    f["causal"] = np.where(c > p, NEG, 0.0)
    f["upper64"] = (p % 64) <= c64
    f["ident64"] = (p % 64) == c64
    for j in range(LEVELS):
        m = 1 << j
        s = p % 64
        f[f"level{j}"] = (s // (2 * m) == c64 // (2 * m)) & (s % (2 * m) < m) & (c64 % (2 * m) >= m)
    sel = np.zeros((P, 3 * P))
    for pair in range(3):
        for m in range(P):
            sel[2 * pair + m // 64, pair * P + m] = 1.0
    f["pairsel"] = sel
    f["eps"] = np.full((P, 1), EPS)
    f["one"] = np.ones((P, 1))
    f["zero"] = np.zeros((P, 1))
    return {k: np.ascontiguousarray(v, dtype=np.float32) for k, v in f.items()}


def bucket_rows():
    hot = np.zeros((BUCKETS, 384), np.float32)
    bucket = t5_bucket()
    for i in range(384):
        hot[bucket[max(255 - i, 0)], i] += 1.0
        hot[BUCKETS - 1, i] -= 1.0
    return hot


CONSTS = constants()
CONST_AT, _at = {}, 0
for _k, _v in CONSTS.items():
    CONST_AT[_k] = (_at, _v.shape[1])
    _at += _v.shape[1]
N_CONST = _at


class Chain:

    def __init__(self, eng, sem):
        self.eng, self.sem, self.n = eng, sem, 0

    def step(self, ins):
        ins.then_inc(self.sem, 1)
        self.n += 1

    def join(self):
        self.eng.wait_ge(self.sem, self.n)


def bcast(ap, axis, n):
    shape = list(ap.shape)
    return ap.unsqueeze(axis).to_broadcast(shape[:axis] + [n] + shape[axis:])


SEMAPHORES = """
landed0 landed1 w_hi w_lo w_used
sq_done ss_done r_done xn_done xh_done xl_done x_up
gate_done up_done g_free u_free hh_done hl_done dn_done
act_chain dve_chain pool_chain
cols_in region_in mem_in strip_in
pj_done ev_done sc_done relu_done acc_done top_done
mem_sq mem_r mem_n mem_t mem_hi mem_lo
nq_sq nq_ss nq_r nq_done conv_in conv_done silu_done
v_t v_done sm_ready sp_e sp_b g_ready gc_ps gc_ready row_ps row_ready
gd_pe gd_act gd_dve gd_pool
jl_done jt_done jm_done je_done jtr_done jp_done jv_done
o_ev o_t o_hi o_lo
out_in
""".split()


def hybrid_trunk(nc, x, mem, ffn1_norm, ffn1_w_gate, ffn1_w_up, ffn1_w_down, mix_norm, w_in,
                 dsa_q_norm, dsa_k_norm, rel_bias, gdn_conv, gdn_A_log, gdn_dt_bias,
                 gdn_out_norm, mem_norm, w_mem_kv, mem_q_norm, mem_k_norm, w_out,
                 ffn2_norm, ffn2_w_gate, ffn2_w_up, ffn2_w_down, consts, hot_rows, out):
    depth = w_in.shape[0]
    ffn_w = [(ffn1_w_gate, ffn1_w_up, ffn1_w_down), (ffn2_w_gate, ffn2_w_up, ffn2_w_down)]
    norm_w = [ffn1_norm, mix_norm, ffn2_norm]

    with ExitStack() as ctx:
        ctx.enter_context(nc.allow_non_contiguous_dma("gains and other small columns"))

        def sb(name, shape, dt=F32, stack=ctx):
            return stack.enter_context(nc.sbuf_tensor(name, shape, dt))

        xT = sb("xT", [P, KD, T])
        XH = sb("XH", [P, KD, T], F32R)
        XL = sb("XL", [P, KD, T], F32R)
        raw = [sb(f"raw{i}", [P, KD, UNIT_COLS]) for i in range(2)]
        wh = [sb(f"wh{i}", [P, KD, UNIT_COLS], F32R) for i in range(2)]
        wl = [sb(f"wl{i}", [P, KD, UNIT_COLS], F32R) for i in range(2)]
        cst = sb("cst", [P, N_CONST])

        def const(name):
            a, n = CONST_AT[name]
            return cst[:, a:a + n]

        eps, one, zero = const("eps"), const("one"), const("zero")
        far = sb("far", [P, H_A])
        gain = sb("gain", [P, 4, KD])
        hgain = sb("hgain", [P, 5])
        convw = sb("convw", [P, CONV, 9])
        gdnp = sb("gdnp", [P, 2, H_B])

        ffn_mem = ExitStack()
        HH = sb("HH", [P, NF, T], F32R, ffn_mem)
        HL = sb("HL", [P, NF, T], F32R, ffn_mem)
        sg = [sb(f"sg{i}", [P, T], F32, ffn_mem) for i in range(2)]
        hf = [sb(f"hf{i}", [P, T], F32, ffn_mem) for i in range(2)]
        ffn_mem.close()
        prep_mem = ExitStack()
        sqt = [sb(f"sqt{i}", [P, T], F32, prep_mem) for i in range(2)]
        xn = [sb(f"xn{i}", [P, T], F32, prep_mem) for i in range(2)]
        rB = sb("rB", [P, T], F32, prep_mem)
        prep_mem.close()
        io_mem = ExitStack()
        xnat = sb("xnat", [P, NB, D], F32, io_mem)
        hot = sb("hot", [BUCKETS, 384], F32, io_mem)
        relb = sb("relb", [BUCKETS, H_A], F32, io_mem)
        rowsb = sb("rowsb", [H_A, 384], F32, io_mem)
        io_mem.close()
        dqT = sb("dqT", [P, 3, T])
        dkT = sb("dkT", [P, 3, T])
        dvN = sb("dvN", [P, NB, WA])
        mqT = sb("mqT", [P, 2, T])
        mkT = sb("mkT", [P, 2, NM])
        mvN = sb("mvN", [P, 2, WM])
        gqT = sb("gqT", [P, 3, T])
        gkT = sb("gkT", [P, 3, T])
        gzT = sb("gzT", [P, 3, T])
        gvN = sb("gvN", [P, NB, WB])
        unsel = [None] + [sb(f"unsel{b}", [P, P * (b + 1)]) for b in range(1, NB)]
        sm = sb("sm", [P, NB, SM])
        wI = sb("wI", [P, NB, H_I])
        gcol = sb("gcol", [P, 8, NB, H_B])
        beta, gdec, gcum, bg, kdec, tmpa, tmpb, tmpc = (gcol[:, i] for i in range(8))
        rowb = sb("rowb", [H_B, T])
        rowg = sb("rowg", [H_B, T])
        m8 = sb("m8", [P, 8])
        mxs = sb("mxs", [P, 2, 2])
        rsum = sb("rsum", [P, JOBS])
        rrec = sb("rrec", [P, JOBS])
        memr = sb("memr", [P, 2])
        oss = sb("oss", [P, H_B])

        t_mem = ExitStack()
        acc = [None] + [sb(f"acc{b}", [P, P * (b + 1)], F32, t_mem) for b in range(1, NB)]
        wrk = sb("wrk", [P, T], F32, t_mem)
        MH = sb("MH", [P, KD, NM], F32R, t_mem)
        ML = sb("ML", [P, KD, NM], F32R, t_mem)
        nsq = [sb(f"nsq{i}", [P, T], F32, t_mem) for i in range(2)]
        nrr = [sb(f"nrr{i}", [P, T], F32, t_mem) for i in range(2)]
        idx_mem = ExitStack()
        iqT = sb("iqT", [P, 2, T], F32, idx_mem)
        ikT = sb("ikT", [P, T], F32, idx_mem)
        rl = [sb(f"rl{i}", [P, T], F32, idx_mem) for i in range(2)]
        idx_mem.close()
        tok_mem = ExitStack()
        memN = sb("memN", [P, 2, D], F32, tok_mem)
        tok_mem.close()
        cv = [sb(f"cv{i}", [P, CONV - 1 + T], F32, t_mem) for i in range(2)]
        gvT = sb("gvT", [P, 3, T], F32, t_mem)
        t_mem.close()

        a_mem = ExitStack()

        def ab(name, shape):
            return sb(name, shape, F32, a_mem)
        at = [ab(f"at{i}", [P, T]) for i in range(2)]
        pT = [ab(f"pT{i}", [P, T]) for i in range(2)]
        oA = ab("oA", [P, WA])
        kbT = ab("kbT", [P, 3, P])
        EGr = ab("EGr", [P, 3, P])
        TG = ab("TG", [P, 2, 3, DH])
        DT = ab("DT", [P, 2, 3, DH])
        LT = ab("LT", [P, 2, 3, DH])
        AT = ab("AT", [P, 2, 3, DH])
        X = ab("X", [P, 2, 3, DH])
        XT = ab("XT", [P, 2, 3, DH])
        Y = ab("Y", [P, 2, 3, DH])
        BT = ab("BT", [P, 2, 3, DH])
        kbg = ab("kbg", [P, H_B, DH])
        kdc = ab("kdc", [P, H_B, DH])
        U = ab("U", [P, H_B, DH])
        WT = ab("WT", [P, 2, 3, DH])
        Sbd = ab("Sbd", [P, 3, P])
        Sdec = ab("Sdec", [P, 3, P])
        oG = ab("oG", [P, H_B, DH])
        strips = ab("strips", [P, H_A, 256])
        a_mem.close()

        bank = [ctx.enter_context(nc.psum_tensor(f"bank{i}", [P, T], F32)) for i in range(8)]
        strip_dram = nc.dram_tensor("bias_rows", [H_A, P, 384], F32).ap()

        S = {n: ctx.enter_context(nc.semaphore(n)) for n in SEMAPHORES}
        setup = [ctx.enter_context(nc.semaphore(f"setup_{n}"))
                 for n in ("cst", "x", "w", "pe", "xt", "rows", "hi", "lo", "out")]
        landed = [S["landed0"], S["landed1"]]

        def unit_src(v, L):
            if v in (0, 1):
                return [(ffn_w[0][v][L].rearrange("(k p) f -> p k f", p=P)[:, :, 0:UNIT_COLS], raw[v][:, :, :])]
            m = v - U_MIX
            dst = raw[v % 2]
            w = w_in[L].rearrange("(k p) n -> p k n", p=P)
            src = MIX_SRC[m]
            if src == "iq":
                return [(w[:, :, O_IQ:O_IQ + 256], dst[:, :, :])]
            if src == "small":
                reps = [(w[:, :, O_IK:O_IK + D_I], dst[:, :, D_I * r:D_I * (r + 1)]) for r in range(P // D_I)]
                return reps + [(w[:, :, O_IW:O_IW + H_I], dst[:, :, P:P + H_I]),
                               (w[:, :, O_GA:O_GA + 2 * H_B], dst[:, :, P + H_I:P + SM])]
            if src in ("mk", "mv"):
                kv = w_mem_kv[L].rearrange("(k p) n -> p k n", p=P)
                return [(kv[:, :, WM * (src == "mv"):WM * (1 + (src == "mv"))], dst[:, :, :])]
            if src[0] == "out":
                wo = w_out[L].rearrange("(k p) n -> p k n", p=P)
                return [(wo[:, :, 256 * src[1]:256 * src[1] + 256], dst[:, :, :])]
            return [(w[:, :, src[0]:src[0] + src[1]], dst[:, :, 0:src[1]])]

        (s_cst, s_x, s_w, s_pe, s_cp, s_rows, s_hi, s_lo, s_out) = setup
        with nc.Block() as block:
            @block.sync
            def _(sp):
                for v in range(2):
                    for src, dst in unit_src(v, 0):
                        sp.dma_start(dst, src).then_inc(s_w, 16)
                sp.dma_start(xnat[:, :, :], x[0].rearrange("(b p) d -> p b d", p=P)).then_inc(s_x, 16)
                sp.wait_ge(s_rows, 1)
                sp.dma_start(strip_dram, rowsb[:, None, :].to_broadcast([H_A, P, 384])).then_inc(s_out, 16)
                sp.wait_ge(s_out, 16)

            @block.gpsimd
            def _(pool):
                pool.dma_start(cst[:, :], consts).then_inc(s_cst, 16)
                pool.dma_start(hot[:, :], hot_rows).then_inc(s_cst, 16)
                pool.dma_start(relb[:, :], rel_bias).then_inc(s_cst, 16)
                pool.dma_start(far[:, :], rel_bias[BUCKETS - 1, :].partition_broadcast(P)).then_inc(s_cst, 16)

            @block.tensor
            def _(pe):
                pe.wait_ge(s_cst, 64)
                pe.wait_ge(s_x, 16)
                for k in range(KD):
                    if k >= 2:
                        pe.wait_ge(s_cp, k - 1)
                    for b in range(NB):
                        mm = pe.transpose(bank[k % 2][:, b * P:(b + 1) * P], xnat[:, b, k * P:(k + 1) * P],
                                          const("ident"))
                    mm.then_inc(s_pe, 1)
                pe.matmul(bank[2][0:H_A, 0:384], relb[:, :], hot[:, :], start=True, stop=True).then_inc(s_pe, 1)

            @block.scalar
            def _(act):
                act.wait_ge(s_w, 32)
                for v in range(2):
                    act.activation(wh[v][:, :, :], raw[v][:, :, :], ACT.Copy).then_inc(s_hi, 1)

            @block.vector
            def _(dve):
                for k in range(KD):
                    dve.wait_ge(s_pe, k + 1)
                    dve.tensor_copy(xT[:, k, :], bank[k % 2][:, :]).then_inc(s_cp, 1)
                dve.wait_ge(s_pe, KD + 1)
                dve.tensor_copy(rowsb[:, :], bank[2][0:H_A, 0:384]).then_inc(s_rows, 1)
                for v in range(2):
                    dve.wait_ge(s_hi, v + 1)
                    dve.tensor_tensor(wl[v][:, :, :], raw[v][:, :, :], wh[v][:, :, :].bitcast(F32),
                                      ALU.subtract).then_inc(s_lo, 1)

        with nc.Fori(0, depth) as L:
            with nc.Block() as block:

                @block.sync
                def _(sp):
                    def load(v, pairs, slot):
                        for src, dst in pairs:
                            sp.dma_start(dst, src).then_inc(landed[slot], 16)

                    def ffn_units(q):
                        w_gate, w_up, w_down = ffn_w[q]
                        ub = U_FFN[q]
                        gu = [w[L].rearrange("(k p) (c n) -> p k c n", p=P, n=UNIT_COLS) for w in (w_gate, w_up)]
                        dn = w_down[L].rearrange("(f p) (c n) -> p f c n", p=P, n=UNIT_COLS)
                        with sp.Fori(1 - q, NF // 2) as i:
                            for j in range(2):
                                sp.wait_ge(S["w_lo"], ub + 2 * i + j - 1)
                                sp.dma_start(raw[j][:, :, :], gu[j][:, :, i, :]).then_inc(landed[j], 16)
                        with sp.Fori(0, 2) as i:
                            for r in range(DN_UNITS // 2):
                                f0, f1 = PARTS[r % 3]
                                sp.wait_ge(S["w_lo"], ub + GU_UNITS + 6 * i + (r - 1))
                                sp.dma_start(raw[r % 2][:, 0:f1 - f0, :],
                                             dn[:, f0:f1, 2 * i + r // 3, :]).then_inc(landed[r % 2], 16)

                    ffn_units(0)
                    for v in range(U_MIX, U_MIX + MIX_UNITS):
                        sp.wait_ge(S["w_lo"], v - 1)
                        load(v, unit_src(v, L), v % 2)
                        if v == U_MIX + 17:
                            sp.wait_ge(S["v_done"], NB)
                            sp.wait_ge(S["nq_done"], N_NORM_A + 6)
                            sp.dma_start(strips[:, :, :], bass.AP(
                                tensor=strip_dram.tensor, offset=strip_dram.offset + P - 1,
                                ap=[[384 - 1, P], [P * 384, H_A], [1, 256]])).then_inc(S["strip_in"], 16)
                        if v == U_MIX + 4:
                            sp.wait_ge(S["sc_done"], 24)
                            sp.wait_ge(S["acc_done"], 24)
                            sp.dma_start(memN[:, :, :], mem[0].rearrange("(m p) d -> p m d", p=P)
                                         ).then_inc(S["mem_in"], 16)
                    ffn_units(1)
                    nxt = (L + 1) % depth
                    for v in range(2):
                        sp.wait_ge(S["w_lo"], LAYER_UNITS + v - 1)
                        load(v, unit_src(v, nxt), v)

                @block.gpsimd
                def _(pool):
                    pool.wait_ge(S["acc_done"], 24)
                    pool.wait_ge(S["mem_lo"], 4)
                    for i in range(2):
                        pool.memset(cv[i][:, 0:CONV - 1], 0.0).then_inc(S["pool_chain"], 1)
                    pool.wait_ge(S["v_done"], NB)
                    pool.wait_ge(S["nq_done"], N_NORM_A + 6)
                    pool.memset(Sbd[:, :, :], 0.0).then_inc(S["pool_chain"], 1)
                    for b in range(NB):
                        tok = slice(b * P, (b + 1) * P)
                        e_pe, e_act, e_dve = b * N_PE, b * N_ACT, b * N_DVE
                        pool.wait_ge(S["gd_pe"], e_pe + 5)
                        pool.wait_ge(S["gd_act"], e_act + 1)
                        pool.tensor_tensor(gqT[:, :, tok], gqT[:, :, tok], EGr[:, :, :], ALU.mult
                                           ).then_inc(S["gd_pool"], 1)
                        for ch in range(2):
                            if ch == 0 and b == 0:
                                pool.wait_ge(S["pool_chain"], 3)
                            else:
                                pool.wait_ge(S["gd_dve"], e_dve + 19 if ch else e_dve - N_DVE + 21)
                            last = EGr[:, :, DH * ch + DH - 1:DH * ch + DH]
                            pool.tensor_tensor(Sdec[:, :, :], Sbd[:, :, :], last.to_broadcast([P, 3, P]),
                                               ALU.mult).then_inc(S["gd_pool"], 1)

                @block.tensor
                def _(pe):
                    def three(out_ap, wt, at_, first, last):
                        (a_hi, a_lo), (b_hi, b_lo) = wt, at_
                        pe.matmul(out_ap, a_hi, b_hi, start=first, stop=False)
                        pe.matmul(out_ap, a_hi, b_lo, start=False, stop=False)
                        return pe.matmul(out_ap, a_lo, b_hi, start=False, stop=last)

                    def sum_squares(p):
                        for k in range(KD):
                            pe.wait_ge(S["sq_done"], KD * p + k + 1)
                            pe.matmul(bank[4][:, :], const("ones"), sqt[k % 2][:, :], start=(k == 0),
                                      stop=(k == KD - 1)).then_inc(S["ss_done"], 1)

                    def ffn(q):
                        p, ub = 2 * q, U_FFN[q]
                        sum_squares(p)
                        with pe.Fori(0, NF // 2) as i:
                            for j in range(2):
                                pe.wait_ge(S["w_lo"], ub + 2 * i + (j + 1))
                                for fs in range(2):
                                    pe.wait_ge(S["g_free" if j == 0 else "u_free"], NF * q + 2 * i + (fs + 1))
                                    dst = bank[2 * j + fs]
                                    cols = slice(P * fs, P * fs + P)
                                    for k in range(KD):
                                        if j == 0 and fs == 0:
                                            pe.wait_ge(S["xl_done"], KD * p + k + 1)
                                        mm = three(dst[:, :], (wh[j][:, k, cols], wl[j][:, k, cols]),
                                                   (XH[:, k, :], XL[:, k, :]), k == 0, k == KD - 1)
                                    mm.then_inc(S["gate_done" if j == 0 else "up_done"], 1)
                        pe.wait_ge(S["hl_done"], NF * (q + 1))
                        with pe.Fori(0, 2) as i:
                            for r in range(DN_UNITS // 2):
                                dp, part = divmod(r, 3)
                                slot = r % 2
                                f0, f1 = PARTS[part]
                                pe.wait_ge(S["w_lo"], ub + GU_UNITS + 6 * i + (r + 1))
                                for d in range(2):
                                    if part == 0:
                                        pe.wait_ge(S["x_up"], 2 * KD * q + 4 * i + (2 * dp + d + 1))
                                    cols = slice(P * d, P * d + P)
                                    for f in range(f0, f1):
                                        mm = three(bank[4 + 2 * dp + d][:, :],
                                                   (wh[slot][:, f - f0, cols], wl[slot][:, f - f0, cols]),
                                                   (HH[:, f, :], HL[:, f, :]), f == 0, f == NF - 1)
                                    if part == 2:
                                        mm.then_inc(S["dn_done"], 1)
                                if part < 2:
                                    mm.then_inc(S["w_used"], 1)

                    def group(gi):
                        g = GROUPS[gi]
                        slot = g["unit"] % 2
                        pe.wait_ge(S["w_lo"], g["unit"] + 1)
                        if gi >= 2:
                            pe.wait_ge(S["ev_done"], gi - 1)
                        dst, kind = bank[gi % 2], g["kind"]
                        for k in range(KD):
                            first, last = k == 0, k == KD - 1
                            act_in = (XH[:, k, :], XL[:, k, :])
                            if kind == "S":
                                continue
                            if kind == "T":
                                if gi == 0:
                                    pe.wait_ge(S["xl_done"], KD + k + 1)
                                cols = slice(g["col"], g["col"] + P)
                                mm = three(dst[:, :], (wh[slot][:, k, cols], wl[slot][:, k, cols]), act_in,
                                           first, last)
                            elif kind == "N":
                                tok = slice(g["b"] * P, g["b"] * P + P)
                                n = g["n"]
                                mm = three(dst[:, 0:n], (XH[:, k, tok], XL[:, k, tok]),
                                           (wh[slot][:, k, 0:n], wl[slot][:, k, 0:n]), first, last)
                            elif kind == "M":
                                cols = slice(g["col"], g["col"] + P)
                                mm = three(dst[:, 0:NM], (wh[slot][:, k, cols], wl[slot][:, k, cols]),
                                           (MH[:, k, :], ML[:, k, :]), first, last)
                            else:
                                tok = slice(g["b"] * P, g["b"] * P + P)
                                mm = three(dst[:, 0:WM], (MH[:, k, tok], ML[:, k, tok]),
                                           (wh[slot][:, k, :], wl[slot][:, k, :]), first, last)
                        if kind == "S":
                            for b in range(NB):
                                tok = slice(b * P, b * P + P)
                                for k in range(KD):
                                    mm = three(dst[:, b * SM:(b + 1) * SM], (XH[:, k, tok], XL[:, k, tok]),
                                               (wh[slot][:, k, P:P + SM], wl[slot][:, k, P:P + SM]),
                                               k == 0, k == KD - 1)
                        mm.then_inc(S["pj_done"], 1)

                    def head_sums(nj, n):
                        pe.wait_ge(S["nq_sq"], nj + 1)
                        if nj >= 2:
                            pe.wait_ge(S["nq_r"], nj - 1)
                        pe.matmul(bank[2 + nj % 2][:, 0:n], const("same64"), nsq[nj % 2][:, 0:n],
                                  start=True, stop=True).then_inc(S["nq_ss"], 1)

                    def index_scores():
                        pe.wait_ge(S["ev_done"], GATE_GROUP)
                        for b in range(1, NB):
                            for h in range(H_I):
                                n = (b - 1) * H_I + h
                                rows = slice(D_I * (h % 4), D_I * (h % 4) + D_I)
                                if n >= 2:
                                    pe.wait_ge(S["relu_done"], n - 1)
                                pe.matmul(bank[4 + n % 2][:, 0:P * (b + 1)], iqT[rows, h // 4, b * P:(b + 1) * P],
                                          ikT[rows, 0:P * (b + 1)], start=True, stop=True
                                          ).then_inc(S["sc_done"], 1)

                    def memory_transposes(t):
                        if t == 0:
                            pe.wait_ge(S["mem_n"], 1)
                            pe.wait_ge(S["row_ready"], 1)
                        if t >= 2:
                            pe.wait_ge(S["mem_lo"], t - 1)
                        for k in range(2 * t, 2 * t + 2):
                            for m in range(2):
                                at0 = (k - 2 * t) * NM + m * P
                                mm = pe.transpose(bank[6 + t % 2][:, at0:at0 + P], memN[:, m, k * P:(k + 1) * P],
                                                  const("ident"))
                        mm.then_inc(S["mem_t"], 1)

                    def hook(gi):
                        if gi == GATE_GROUP:
                            index_scores()
                        if gi == 8:
                            pe.wait_ge(S["g_ready"], 1)
                            g24 = gdec.rearrange("p b h -> p (b h)")
                            pe.matmul(bank[7][:, 0:24], const("prefix"), g24, start=True, stop=True)
                            pe.matmul(bank[7][:, 32:56], const("suffix"), g24, start=True, stop=True
                                      ).then_inc(S["gc_ps"], 1)
                        if gi == 10:
                            pe.wait_ge(S["gc_ready"], 1)
                            for b in range(NB):
                                tok = slice(b * P, b * P + P)
                                pe.transpose(bank[6][0:H_B, tok], beta[:, b, :], const("ident"))
                                mm = pe.transpose(bank[7][0:H_B, tok], gcum[:, b, :], const("ident"))
                            mm.then_inc(S["row_ps"], 1)
                        if gi in (13, 15):
                            for t in range(gi - 13, gi - 11):
                                memory_transposes(t)
                        if gi == 19:
                            pe.wait_ge(S["mem_lo"], 4)

                    def gdn(b, step):
                        e_act, e_dve, e_pool = b * N_ACT, b * N_DVE, b * N_POOL
                        tok0 = b * P
                        heads = [(par, pair) for par in range(2) for pair in range(3)]
                        rows = [slice(0, DH), slice(DH, P)]

                        def sig(mm):
                            mm.then_inc(S["gd_pe"], 1)

                        def col(par, pair):
                            return slice((3 * par + pair) * DH, (3 * par + pair + 1) * DH)

                        if step == S_ROWS:
                            pe.wait_ge(S["row_ready"], 1)
                            if b:
                                pe.wait_ge(S["gd_dve"], e_dve - N_DVE + 24)
                            for pair in range(3):
                                s = const("pairsel")[0:H_B, pair * P:(pair + 1) * P]
                                pe.matmul(bank[5][:, pair * P:(pair + 1) * P], s, rowb[:, tok0:tok0 + P],
                                          start=True, stop=True)
                                mm = pe.matmul(bank[6][:, pair * P:(pair + 1) * P], s, rowg[:, tok0:tok0 + P],
                                               start=True, stop=True)
                            sig(mm)
                            pe.wait_ge(S["gd_dve"], e_dve + 1)
                            sig(pe.matmul(bank[7][:, 0:WB], const("suffix"), TG.rearrange("p a b c -> p (a b c)"),
                                          start=True, stop=True))
                        elif step == S_DECAY:
                            pe.wait_ge(S["gd_dve"], e_dve + 2)
                            for pair in range(3):
                                mm = pe.transpose(bank[5][:, pair * P:(pair + 1) * P],
                                                  gkT[:, pair, tok0:tok0 + P], const("ident"))
                            sig(mm)
                        elif step in (S_KK, S_QK):
                            if step == S_KK:
                                pe.wait_ge(S["gd_act"], e_act + 2)
                            else:
                                pe.wait_ge(S["gd_dve"], e_dve + 5)
                            for pair in range(3):
                                for par in range(2):
                                    for ch in range(2):
                                        toks = slice(tok0 + DH * ch, tok0 + DH * ch + DH)
                                        rhs = (kbT[rows[par], pair, DH * ch:DH * ch + DH] if step == S_KK
                                               else gqT[rows[par], pair, toks])
                                        mm = pe.matmul(bank[6 + par][rows[ch], pair * DH:(pair + 1) * DH],
                                                       gkT[rows[par], pair, toks], rhs, start=True, stop=True)
                            sig(mm)
                        elif step == S_INV:
                            pe.wait_ge(S["gd_dve"], e_dve + 7)
                            for par, pair in heads:
                                for ch in range(2):
                                    mm = pe.matmul(bank[5][rows[ch], col(par, pair)], XT[rows[ch], par, pair, :],
                                                   const("ident64")[rows[ch], :], start=True, stop=True)
                            sig(mm)
                        elif step < S_UW:
                            j, second = divmod(step - S_LEVEL, 2)
                            j += 1
                            if not second:
                                pe.wait_ge(S["gd_dve"], e_dve + 6 + 2 * j)
                                if j == 1:
                                    pe.wait_ge(S["gd_act"], e_act + 3)
                                for par, pair in heads:
                                    for ch in range(2):
                                        mm = pe.matmul(bank[6][rows[ch], col(par, pair)],
                                                       BT[rows[ch], par, pair, :], X[rows[ch], par, pair, :],
                                                       start=True, stop=True)
                                sig(mm)
                            else:
                                pe.wait_ge(S["gd_act"], e_act + 3 + j)
                                for par, pair in heads:
                                    for ch in range(2):
                                        if j < LEVELS - 1:
                                            pe.matmul(bank[5][rows[ch], col(par, pair)],
                                                      XT[rows[ch], par, pair, :], Y[rows[ch], par, pair, :],
                                                      start=True, stop=True)
                                        mm = pe.matmul(bank[7][rows[ch], col(par, pair)],
                                                       Y[rows[ch], par, pair, :], XT[rows[ch], par, pair, :],
                                                       start=True, stop=True)
                                sig(mm)
                        elif step == S_UW:
                            pe.wait_ge(S["gd_dve"], e_dve + 17)
                            for par, pair in heads:
                                h = 2 * pair + par
                                for ch in range(2):
                                    pe.matmul(bank[5][rows[ch], h * DH:(h + 1) * DH], XT[rows[ch], par, pair, :],
                                              gvN[rows[ch], b, h * DH:(h + 1) * DH], start=True, stop=True)
                                    mm = pe.matmul(bank[6 + ch][rows[par], pair * DH:(pair + 1) * DH],
                                                   kbg[rows[ch], h, :], XT[rows[ch], par, pair, :],
                                                   start=True, stop=True)
                            sig(mm)
                        elif step < S_OUT:
                            ch, second = divmod(step - S_REC, 2)
                            if not second:
                                pe.wait_ge(S["gd_act"], e_act + 9)
                                pe.wait_ge(S["gd_pool"], e_pool + 1)
                                if b or ch:
                                    pe.wait_ge(S["gd_dve"], e_dve + 19 if ch else e_dve - N_DVE + 21)
                                else:
                                    pe.wait_ge(S["pool_chain"], 3)
                                for pair in range(3):
                                    mm = pe.matmul(bank[6][rows[ch], pair * P:(pair + 1) * P],
                                                   WT[:, ch, pair, :], Sbd[:, pair, :], start=True, stop=True)
                                sig(mm)
                                for pair in range(3):
                                    mm = pe.matmul(bank[5][rows[ch], pair * P:(pair + 1) * P],
                                                   gqT[:, pair, tok0 + DH * ch:tok0 + DH * ch + DH],
                                                   Sbd[:, pair, :], start=(pair == 0), stop=False,
                                                   skip_group_check=True)
                                sig(mm)
                            else:
                                pe.wait_ge(S["gd_dve"], e_dve + 18 + 2 * ch)
                                for pair in range(3):
                                    mm = pe.matmul(bank[7][:, pair * P:(pair + 1) * P],
                                                   kdc[rows[ch], 2 * pair:2 * pair + 2, :],
                                                   U[rows[ch], 2 * pair:2 * pair + 2, :], start=True, stop=True)
                                sig(mm)
                                for pair in range(3):
                                    for par in range(2):
                                        h = 2 * pair + par
                                        mm = pe.matmul(bank[5][rows[ch], h * DH:(h + 1) * DH],
                                                       AT[rows[ch], par, pair, :], U[rows[ch], h, :],
                                                       start=False, stop=(h == H_B - 1), skip_group_check=True)
                                sig(mm)
                        elif step == S_OUT + 1:
                            pe.wait_ge(S["gd_dve"], e_dve + 23)
                            for pair in range(3):
                                mm = pe.transpose(bank[6][:, pair * P:(pair + 1) * P],
                                                  oG[:, 2 * pair:2 * pair + 2, :], const("ident"))
                            sig(mm)

                    def attention(b, slot):
                        if slot < JOBS:
                            j, n = slot, JOBS * b + slot
                            if n >= 2:
                                pe.wait_ge(S["jt_done"], n - 1)
                            rows = slice(DH * (j % 2), DH * (j % 2) + DH)
                            tok = slice(b * P, b * P + P)
                            if j < H_A:
                                w, q, k = P * (b + 1), dqT[rows, j // 2, tok], dkT[rows, j // 2, 0:P * (b + 1)]
                            else:
                                m = j - H_A
                                w, q, k = NM, mqT[rows, m // 2, tok], mkT[rows, m // 2, :]
                            pe.matmul(bank[n % 2][:, 0:w], q, k, start=True, stop=True).then_inc(S["jl_done"], 1)
                        if 1 <= slot <= JOBS:
                            j = slot - 1
                            n = JOBS * b + j
                            pe.wait_ge(S["je_done"], n + 1)
                            if n >= 2:
                                pe.wait_ge(S["jp_done"], n - 1)
                            for i in range(b + 1 if j < H_A else 2):
                                mm = pe.transpose(bank[2 + n % 2][:, i * P:(i + 1) * P],
                                                  at[n % 2][:, i * P:(i + 1) * P], const("ident"))
                            mm.then_inc(S["jtr_done"], 1)
                        if slot >= 2:
                            j = slot - 2
                            n = JOBS * b + j
                            pe.wait_ge(S["jp_done"], n + 1)
                            if j in (0, H_A) and (b or j):
                                pe.wait_ge(S["o_lo"], 2 * b + (j == H_A))
                            nt = b + 1 if j < H_A else 2
                            at0 = DH * (j if j < H_A else j - H_A)
                            for i in range(nt):
                                v = (dvN[:, i, at0:at0 + DH] if j < H_A else mvN[:, i, at0:at0 + DH])
                                mm = pe.matmul(bank[4][:, at0:at0 + DH], pT[n % 2][:, i * P:(i + 1) * P], v,
                                               start=(i == 0), stop=(i == nt - 1))
                            mm.then_inc(S["jv_done"], 1)
                            if j in (H_A - 1, JOBS - 1):
                                ph = int(j == JOBS - 1)
                                pe.wait_ge(S["o_ev"], 2 * b + ph + 1)
                                for c in range(2 if ph else 3):
                                    mm = pe.transpose(bank[4][:, c * P:(c + 1) * P], oA[:, c * P:(c + 1) * P],
                                                      const("ident"))
                                mm.then_inc(S["o_t"], 1)

                    ffn(0)
                    sum_squares(1)
                    for gi in range(N_GROUPS):
                        group(gi)
                        if gi - 1 in NORM_OF:
                            head_sums(NORM_OF[gi - 1], NM if GROUPS[gi - 1]["name"] == "mk" else T)
                        hook(gi)
                    for b in range(NB):
                        pe.wait_ge(S["silu_done"], 1)
                        pe.wait_ge(S["ev_done"], N_GROUPS)
                        if b >= 2:
                            pe.wait_ge(S["v_done"], b - 1)
                        for pair in range(3):
                            mm = pe.transpose(bank[b % 2][:, pair * P:(pair + 1) * P],
                                              gvT[:, pair, b * P:(b + 1) * P], const("ident"))
                        mm.then_inc(S["v_t"], 1)
                    for nj in range(N_NORM_A, N_NORM_A + 6):
                        head_sums(nj, T)
                    pe.wait_ge(S["v_done"], NB)
                    pe.wait_ge(S["nq_done"], N_NORM_A + 6)
                    for b in range(NB):
                        for step in range(N_STEPS):
                            gdn(b, step)
                            if step in JOB_SLOT:
                                attention(b, JOB_SLOT[step])
                    pe.wait_ge(S["o_lo"], 2 * NB)
                    pe.wait_ge(S["gd_dve"], NB * N_DVE)
                    for c in range(KD):
                        u = U_MIX + 16 + c // 2
                        pe.wait_ge(S["w_lo"], u + 1)
                        pe.wait_ge(S["x_up"], KD + c + 1)
                        cols = slice(P * (c % 2), P * (c % 2) + P)
                        for k in range(KD):
                            mm = three(bank[4 + c % 4][:, :], (wh[u % 2][:, k, cols], wl[u % 2][:, k, cols]),
                                       (XH[:, k, :], XL[:, k, :]), k == 0, k == KD - 1)
                        mm.then_inc(S["dn_done"], 1)
                    ffn(1)

                @block.scalar
                def _(act):
                    chain = Chain(act, S["act_chain"])

                    def split_hi(v, wait_landed, slot):
                        act.wait_ge(landed[slot], wait_landed)
                        act.activation(wh[slot][:, :, :], raw[slot][:, :, :], ACT.Copy).then_inc(S["w_hi"], 1)

                    def rsqrt(dst, src, scale):
                        chain.step(act.activation(dst, src, ACT.Ln, bias=eps[0:dst.shape[0], :], scale=scale))
                        chain.join()
                        return act.activation(dst, dst, ACT.Exp, scale=-0.5)

                    def prep(p):
                        if p:
                            act.wait_ge(S["x_up"], 4 + KD * p)
                        else:
                            act.wait_ge(S["cols_in"], 16 * COL_DMAS)
                        for k in range(KD):
                            if k >= 2:
                                act.wait_ge(S["ss_done"], KD * p + k - 1)
                            act.activation(sqt[k % 2][:, :], xT[:, k, :], ACT.Square).then_inc(S["sq_done"], 1)
                        act.wait_ge(S["ss_done"], KD * (p + 1))
                        rsqrt(rB[:, :], bank[4][:, :], 1.0 / D).then_inc(S["r_done"], 1)
                        for k in range(KD):
                            act.wait_ge(S["xn_done"], KD * p + k + 1)
                            act.activation(XH[:, k, :], xn[k % 2][:, :], ACT.Copy, scale=gain[:, p, k:k + 1]
                                           ).then_inc(S["xh_done"], 1)

                    def ffn(q):
                        ub = U_FFN[q]
                        prep(2 * q)
                        with act.Fori(0, NF // 2) as i:
                            for fs in range(2):
                                act.wait_ge(S["gate_done"], NF * q + 2 * i + (fs + 1))
                                act.wait_ge(S["u_free"], NF * q + 2 * i + (fs + 1))
                                act.activation(sg[fs][:, :], bank[fs][:, :], ACT.Silu).then_inc(S["g_free"], 1)
                            split_hi(0, landed_value(ub + 2) + 16 * i, 0)
                            for fs in range(2):
                                act.wait_ge(S["u_free"], NF * q + 2 * i + (fs + 3))
                                act.activation(HH[:, 2 * i + fs, :], hf[fs][:, :], ACT.Copy
                                               ).then_inc(S["hh_done"], 1)
                            split_hi(1, landed_value(ub + 3) + 16 * i, 1)
                        with act.Fori(0, 2) as i:
                            for r in range(DN_UNITS // 2):
                                dp, part = divmod(r, 3)
                                if part < 2:
                                    act.wait_ge(S["w_used"], DN_UNITS * 2 // 3 * q + 4 * i + (2 * dp + part + 1))
                                else:
                                    act.wait_ge(S["dn_done"], 2 * KD * q + 4 * i + (2 * dp + 2))
                                split_hi(0, landed_value(ub + GU_UNITS + r + 2) + 48 * i, r % 2)

                    def evac(gi):
                        g = GROUPS[gi]
                        act.wait_ge(S["pj_done"], gi + 1)
                        name, c, b, src = g["name"], g.get("c"), g.get("b"), bank[gi % 2]
                        if name == "sm":
                            dst, src = sm.rearrange("p b n -> p (b n)"), src[:, 0:NB * SM]
                        elif name in ("iq", "dq", "dk", "mq", "gz"):
                            dst, src = {"iq": iqT, "dq": dqT, "dk": dkT, "mq": mqT, "gz": gzT}[name][:, c, :], src[:, :]
                        elif name == "ik":
                            dst, src = ikT[:, :], src[:, :]
                        elif name == "mk":
                            dst, src = mkT[:, c, :], src[:, 0:NM]
                        elif name == "mv":
                            dst, src = mvN[:, b, :], src[:, 0:WM]
                        elif name == "va":
                            dst, src = dvN[:, b, 0:256], src[:, 0:256]
                        elif name == "vb":
                            dst, src = dvN[:, b, 256:WA], src[:, 0:WA - 256]
                        else:
                            n = gi - FIRST_CONV
                            if n == 0:
                                act.wait_ge(S["mem_t"], 4)
                                act.wait_ge(S["pool_chain"], 2)
                            if n >= 2:
                                act.wait_ge(S["conv_done"], n - 1)
                            dst, src = cv[n % 2][:, CONV - 1:], src[:, :]
                        act.activation(dst, src, ACT.Copy).then_inc(S["ev_done"], 1)
                        return dst

                    def square_of(nj, ap, n):
                        if nj >= 2:
                            act.wait_ge(S["nq_ss"], nj - 1)
                        act.activation(nsq[nj % 2][:, 0:n], ap, ACT.Square).then_inc(S["nq_sq"], 1)

                    def head_rsqrt(nj, n, scale):
                        act.wait_ge(S["nq_ss"], nj + 1)
                        if nj >= 2:
                            act.wait_ge(S["nq_done"], nj - 1)
                        rsqrt(nrr[nj % 2][:, 0:n], bank[2 + nj % 2][:, 0:n], scale).then_inc(S["nq_r"], 1)

                    def index_relu():
                        for n in range(3 * H_I):
                            b = 1 + n // H_I
                            act.wait_ge(S["sc_done"], n + 1)
                            if n >= 2:
                                act.wait_ge(S["acc_done"], n - 1)
                            act.activation(rl[n % 2][:, 0:P * (b + 1)], bank[4 + n % 2][:, 0:P * (b + 1)], ACT.Relu,
                                           scale=D_I ** -0.5).then_inc(S["relu_done"], 1)

                    def hook(gi):
                        if gi == GATE_GROUP:
                            index_relu()
                        if gi == 7:
                            act.wait_ge(S["sp_e"], 1)
                            chain.step(act.activation(tmpb, tmpb, ACT.Exp))
                            chain.step(act.activation(gdnp[:, 0, :], gdnp[:, 0, :], ACT.Exp))
                            chain.step(act.activation(tmpc, tmpc, ACT.Exp))
                            chain.join()
                            act.activation(tmpb, tmpb, ACT.Ln, bias=one).then_inc(S["sp_b"], 1)
                        if gi == 9:
                            act.wait_ge(S["gc_ps"], 1)
                            ps = [bank[7][:, 32 * i:32 * i + 24] for i in range(2)]
                            flat = [t.rearrange("p b h -> p (b h)") for t in (gcum, bg, kdec)]
                            chain.step(act.activation(flat[0], ps[0], ACT.Copy))
                            chain.step(act.activation(flat[1], ps[0], ACT.Exp))
                            chain.step(act.activation(flat[2], ps[1], ACT.Exp))
                            chain.join()
                            act.sem_inc(S["gc_ready"], 1)
                        if gi == 11:
                            act.wait_ge(S["row_ps"], 1)
                            chain.step(act.activation(rowb[:, :], bank[6][0:H_B, :], ACT.Copy))
                            chain.step(act.activation(rowg[:, :], bank[7][0:H_B, :], ACT.Copy))
                            chain.join()
                            act.sem_inc(S["row_ready"], 1)
                            act.wait_ge(S["mem_in"], 16)
                            for m in range(2):
                                chain.step(act.activation(MH[:, 4 * m:4 * m + 4, :], memN[:, m, :], ACT.Square,
                                                          accum_out=memr[:, m:m + 1]))
                            chain.join()
                            rsqrt(memr[:, :], memr[:, :], 1.0 / D).then_inc(S["mem_r"], 1)
                        if gi in (14, 16):
                            for t in range(gi - 14, gi - 12):
                                act.wait_ge(S["mem_t"], t + 1)
                                for k in range(2 * t, 2 * t + 2):
                                    chain.step(act.activation(MH[:, k, :], bank[6 + t % 2][:, (k % 2) * NM:(k % 2) * NM + NM],
                                                              ACT.Copy, scale=gain[:, 3, k:k + 1]))
                                chain.join()
                                act.sem_inc(S["mem_hi"], 1)

                    def gdn(b, step):
                        e_pe, e_dve, e_pool = b * N_PE, b * N_DVE, b * N_POOL

                        def sig(ins):
                            ins.then_inc(S["gd_act"], 1)
                        flat = "p a b c -> p (a b c)"
                        if step == S_ROWS:
                            act.wait_ge(S["gd_pe"], e_pe + 1)
                            if b:
                                act.wait_ge(S["gd_pool"], e_pool)
                            sig(act.activation(EGr.rearrange("p a b -> p (a b)"), bank[6][:, 0:3 * P], ACT.Exp))
                            act.wait_ge(S["gd_pe"], e_pe + 2)
                            sig(act.activation(DT.rearrange(flat), bank[7][:, 0:WB], ACT.Exp))
                        elif step == S_INV:
                            act.wait_ge(S["gd_pe"], e_pe + 6)
                            sig(act.activation(X.rearrange(flat), bank[5][:, 0:WB], ACT.Copy))
                        elif S_LEVEL <= step < S_UW and (step - S_LEVEL) % 2 == 0:
                            j = (step - S_LEVEL) // 2 + 1
                            act.wait_ge(S["gd_pe"], e_pe + 5 + 2 * j)
                            sig(act.activation(Y.rearrange(flat), bank[6][:, 0:WB], ACT.Copy))
                        elif step == S_UW:
                            act.wait_ge(S["gd_pe"], e_pe + 17)
                            chain.step(act.activation(U.rearrange("p h d -> p (h d)"), bank[5][:, 0:WB], ACT.Copy))
                            for ch in range(2):
                                chain.step(act.activation(WT[:, ch].rearrange("p a b -> p (a b)"),
                                                          bank[6 + ch][:, 0:3 * DH], ACT.Copy))
                            chain.join()
                            act.sem_inc(S["gd_act"], 1)
                        elif step == S_OUT:
                            act.wait_ge(S["gd_pe"], e_pe + 25)
                            sig(act.activation(Y.rearrange(flat), bank[5][:, 0:WB], ACT.Square))
                            act.wait_ge(S["gd_dve"], e_dve + 22)
                            sig(rsqrt(oss[:, :], oss[:, :], 1.0 / DH))
                        elif step == S_OUT + 2:
                            act.wait_ge(S["gd_dve"], e_dve + 24)
                            sig(act.activation(XH[:, 3:6, b * P:(b + 1) * P], kbT[:, :, :], ACT.Copy))

                    def attention(b, slot):
                        if slot < JOBS:
                            j, n = slot, JOBS * b + slot
                            w = P * (b + 1) if j < H_A else NM
                            act.wait_ge(S["jl_done"], n + 1)
                            if n >= 2:
                                act.wait_ge(S["jtr_done"], n - 1)
                            bias = far[:, j:j + 1] if j < H_A else zero
                            act.activation(at[n % 2][:, 0:w], bank[n % 2][:, 0:w], ACT.Identity, bias=bias,
                                           scale=DH ** -0.5).then_inc(S["jt_done"], 1)
                            act.wait_ge(S["jm_done"], n + 1)
                            act.activation(at[n % 2][:, 0:w], at[n % 2][:, 0:w], ACT.Exp,
                                           bias=mxs[:, n % 2, 1:2], accum_out=rsum[:, j:j + 1]
                                           ).then_inc(S["je_done"], 1)
                        if slot - 2 in (H_A - 1, JOBS - 1):
                            ph = int(slot - 2 == JOBS - 1)
                            act.wait_ge(S["o_t"], 2 * b + ph + 1)
                            c0, c1 = (6, 8) if ph else (0, 3)
                            act.activation(XH[:, c0:c1, b * P:(b + 1) * P],
                                           bank[4][:, 0:P * (c1 - c0)].rearrange("p (c t) -> p c t", t=P),
                                           ACT.Copy).then_inc(S["o_hi"], 1)

                    for i, g in enumerate([ffn1_norm, mix_norm, ffn2_norm, mem_norm]):
                        act.dma_start(gain[:, i, :], g[L].rearrange("(k p) -> p k", p=P)
                                       ).then_inc(S["cols_in"], 16)
                    for i, g in enumerate([dsa_q_norm, dsa_k_norm, mem_q_norm, mem_k_norm, gdn_out_norm]):
                        for half in range(2):
                            act.dma_start(hgain[half * DH:(half + 1) * DH, i:i + 1],
                                           g[L].rearrange("(p o) -> p o", o=1)).then_inc(S["cols_in"], 16)
                    act.dma_start(convw[:, :, :], gdn_conv[L].rearrange("w (c p) -> p w c", p=P)
                                   ).then_inc(S["cols_in"], 16)
                    act.dma_start(gdnp[:, 0, :], gdn_A_log[L].partition_broadcast(P)
                                   ).then_inc(S["cols_in"], 16)
                    act.dma_start(gdnp[:, 1, :], gdn_dt_bias[L].partition_broadcast(P)
                                   ).then_inc(S["cols_in"], 16)
                    act.sem_inc(S["g_free"], 2)
                    ffn(0)
                    prep(1)
                    lag = []
                    for gi in range(N_GROUPS):
                        dst = evac(gi)
                        if gi in NORM_OF:
                            act.wait_ge(S["ev_done"], gi + 1)
                            square_of(NORM_OF[gi], dst, NM if GROUPS[gi]["name"] == "mk" else T)
                        if gi - 1 in NORM_OF:
                            head_rsqrt(NORM_OF[gi - 1], NM if GROUPS[gi - 1]["name"] == "mk" else T, 1.0 / DH)
                        hook(gi)
                        u = GROUPS[gi]["unit"]
                        if LAST_OF_UNIT[u] == gi:
                            split_hi(u + 2, landed_value(u + 2), u % 2)
                    act.wait_ge(S["conv_done"], 9)
                    act.wait_ge(S["ev_done"], N_GROUPS)
                    for t in (gvT, gqT, gkT, gzT):
                        f = t.rearrange("p c t -> p (c t)")
                        act.activation(f, f, ACT.Silu).then_inc(S["silu_done"], 1)
                    for i in range(8):
                        if i < 6:
                            act.wait_ge(S["silu_done"], 3)
                            square_of(N_NORM_A + i, (gqT if i < 3 else gkT)[:, i % 3, :], T)
                        if i >= 2:
                            head_rsqrt(N_NORM_A + i - 2, T, 1.0)
                    act.wait_ge(S["v_done"], NB)
                    act.wait_ge(S["nq_done"], N_NORM_A + 6)
                    for b in range(NB):
                        for step in range(N_STEPS):
                            gdn(b, step)
                            if step in JOB_SLOT:
                                attention(b, JOB_SLOT[step])
                    for i in range(4):
                        act.wait_ge(S["dn_done"], KD + 2 * i + 2)
                        split_hi(0, landed_value(U_MIX + 18 + i), i % 2)
                    ffn(1)

                @block.vector
                def _(dve):
                    chain = Chain(dve, S["dve_chain"])

                    def split_lo(v, slot):
                        dve.wait_ge(S["w_hi"], v - 1)
                        dve.tensor_tensor(wl[slot][:, :, :], raw[slot][:, :, :], wh[slot][:, :, :].bitcast(F32),
                                          ALU.subtract).then_inc(S["w_lo"], 1)

                    def prep(p):
                        dve.wait_ge(S["r_done"], p + 1)
                        for k in range(KD + 1):
                            if k < KD:
                                if k >= 2:
                                    dve.wait_ge(S["xl_done"], KD * p + k - 1)
                                dve.tensor_tensor(xn[k % 2][:, :], xT[:, k, :], rB[:, :], ALU.mult
                                                  ).then_inc(S["xn_done"], 1)
                            if k:
                                c = k - 1
                                dve.wait_ge(S["xh_done"], KD * p + c + 1)
                                dve.scalar_tensor_tensor(XL[:, c, :], xn[c % 2][:, :], gain[:, p, c:c + 1],
                                                         XH[:, c, :].bitcast(F32), ALU.mult, ALU.subtract
                                                         ).then_inc(S["xl_done"], 1)

                    def ffn(q):
                        ub = U_FFN[q]
                        prep(2 * q)
                        with dve.Fori(0, NF // 2) as i:
                            split_lo(ub + 2 * i + 2, 0)
                            for fs in range(2):
                                f1 = NF * q + 2 * i + (fs + 1)
                                dve.wait_ge(S["up_done"], f1)
                                dve.wait_ge(S["g_free"], NF * q + 2 * i + (fs + 3))
                                dve.tensor_tensor(hf[fs][:, :], sg[fs][:, :], bank[2 + fs][:, :], ALU.mult
                                                  ).then_inc(S["u_free"], 1)
                                dve.wait_ge(S["hh_done"], NF * q + 2 * i + (fs + 1))
                                dve.tensor_tensor(HL[:, 2 * i + fs, :], hf[fs][:, :],
                                                  HH[:, 2 * i + fs, :].bitcast(F32), ALU.subtract
                                                  ).then_inc(S["hl_done"], 1)
                            split_lo(ub + 2 * i + 3, 1)
                        with dve.Fori(0, 2) as i:
                            for r in range(DN_UNITS // 2):
                                if r % 3 == 2:
                                    for d in range(2):
                                        c = 2 * (r // 3) + d
                                        dve.wait_ge(S["dn_done"], 2 * KD * q + 4 * i + (c + 1))
                                        dve.scalar_tensor_tensor(xT[:, 4 * i + c, :], bank[4 + c][:, :], 0.5,
                                                                 xT[:, 4 * i + c, :], ALU.mult, ALU.add
                                                                 ).then_inc(S["x_up"], 1)
                                split_lo(ub + GU_UNITS + 6 * i + (r + 2), r % 2)

                    def norm_apply(nj, ap, n, factor):
                        dve.wait_ge(S["nq_r"], nj + 1)
                        dve.scalar_tensor_tensor(ap, ap, factor, nrr[nj % 2][:, 0:n], ALU.mult, ALU.mult
                                                 ).then_inc(S["nq_done"], 1)

                    def index_sum():
                        for n in range(3 * H_I):
                            b, h = 1 + n // H_I, n % H_I
                            w = P * (b + 1)
                            dve.wait_ge(S["relu_done"], n + 1)
                            if h == 0:
                                ins = dve.tensor_scalar(acc[b][:, :], rl[n % 2][:, 0:w], wI[:, b, h:h + 1], None,
                                                        ALU.mult)
                            else:
                                dve.wait_ge(S["acc_done"], n)
                                ins = dve.scalar_tensor_tensor(acc[b][:, :], rl[n % 2][:, 0:w], wI[:, b, h:h + 1],
                                                               acc[b][:, :], ALU.mult, ALU.add)
                            ins.then_inc(S["acc_done"], 1)
                        dve.wait_ge(S["acc_done"], 3 * H_I)
                        for b in range(1, NB):
                            last = acc[b][:, P * b:P * (b + 1)]
                            chain.step(dve.tensor_tensor(last, last, const("causal"), ALU.add))

                    def selection():
                        for b in range(1, NB):
                            w = P * (b + 1)
                            for r in range(TOPK // 8):
                                src = acc[b][:, :] if r == 0 else wrk[:, 0:w]
                                chain.join()
                                chain.step(dve.max(m8[:, :], src))
                                chain.join()
                                chain.step(dve.match_replace(wrk[:, 0:w], m8[:, :], src, GONE))
                                if r == TOPK // 8 - 1:
                                    chain.join()
                                    chain.step(dve.tensor_tensor(unsel[b][:, :], wrk[:, 0:w], acc[b][:, :],
                                                                 ALU.is_equal))
                                    chain.join()
                                    chain.step(dve.tensor_scalar(unsel[b][:, :], unsel[b][:, :], NEG, None,
                                                                 ALU.mult))
                                yield

                    def conv(n):
                        dst = (gqT, gkT, gvT)[n // 3][:, n % 3, :]
                        dve.wait_ge(S["ev_done"], FIRST_CONV + n + 1)
                        src = cv[n % 2]
                        chain.step(dve.tensor_scalar(dst, src[:, 0:T], convw[:, 0, n:n + 1], None, ALU.mult))
                        for i in range(1, CONV):
                            chain.join()
                            ins = dve.scalar_tensor_tensor(dst, src[:, i:i + T], convw[:, i, n:n + 1], dst,
                                                           ALU.mult, ALU.add)
                            if i < CONV - 1:
                                chain.step(ins)
                        ins.then_inc(S["conv_done"], 1)

                    def hook(gi):
                        bh = [P, NB, H_B]
                        if gi == GATE_GROUP:
                            dve.wait_ge(S["ev_done"], GATE_GROUP + 1)
                            chain.step(dve.tensor_scalar(wI[:, :, :], sm[:, :, 0:H_I], H_I ** -0.5, None, ALU.mult))
                            chain.join()
                            index_sum()
                            dtb = bcast(gdnp[:, 1, :], 1, NB)
                            chain.step(dve.tensor_tensor(tmpa, sm[:, :, H_I:H_I + H_B], dtb, ALU.add))
                            chain.step(dve.tensor_scalar(tmpc, sm[:, :, H_I + H_B:SM], -1.0, 85.0, ALU.mult, ALU.min))
                            chain.join()
                            chain.step(dve.tensor_scalar(tmpb, tmpa, -1.0, None, ALU.mult))
                            chain.join()
                            dve.tensor_tensor(tmpb, tmpb, tmpa, ALU.min).then_inc(S["sp_e"], 1)
                        if gi == 7:
                            dve.wait_ge(S["sp_b"], 1)
                            chain.step(dve.scalar_tensor_tensor(tmpa, tmpa, 0.0, tmpb, ALU.max, ALU.add))
                            chain.step(dve.tensor_scalar(tmpc, tmpc, 1.0, None, ALU.add))
                            chain.join()
                            chain.step(dve.reciprocal(beta, tmpc))
                            chain.step(dve.scalar_tensor_tensor(gdec, tmpa, -1.0, bcast(gdnp[:, 0, :], 1, NB),
                                                                ALU.mult, ALU.mult))
                            chain.join()
                            dve.sem_inc(S["g_ready"], 1)
                        if gi == 10:
                            dve.wait_ge(S["gc_ready"], 1)
                            chain.step(dve.tensor_tensor(bg, bg, beta, ALU.mult))
                        if gi == 12:
                            dve.wait_ge(S["mem_r"], 1)
                            for m in range(2):
                                chain.step(dve.tensor_scalar(memN[:, m, :], memN[:, m, :], memr[:, m:m + 1], None,
                                                             ALU.mult))
                            chain.join()
                            dve.sem_inc(S["mem_n"], 1)
                        if gi in (14, 16):
                            for t in range(gi - 14, gi - 12):
                                dve.wait_ge(S["mem_hi"], t + 1)
                                for k in range(2 * t, 2 * t + 2):
                                    ps = bank[6 + t % 2][:, (k % 2) * NM:(k % 2) * NM + NM]
                                    chain.step(dve.scalar_tensor_tensor(ML[:, k, :], ps, gain[:, 3, k:k + 1],
                                                                        MH[:, k, :].bitcast(F32), ALU.mult,
                                                                        ALU.subtract))
                                chain.join()
                                dve.sem_inc(S["mem_lo"], 1)

                    def gdn(b, step):
                        e_pe, e_act, e_dve, e_pool = b * N_PE, b * N_ACT, b * N_DVE, b * N_POOL
                        rows = [slice(0, DH), slice(DH, P)]
                        pc = "p (a c) -> p a c"

                        def sig(ins):
                            ins.then_inc(S["gd_dve"], 1)

                        def three_heads(t):
                            return t.rearrange("p a b c -> p (a b) c")
                        heads = [P, H_B, DH]
                        if step == S_ROWS:
                            g = gdec[:, b, :].rearrange("p (b a) -> p a b", a=2)
                            for par in range(2):
                                ins = dve.tensor_tensor(TG[:, par, :, :], bcast(const("upper64"), 1, 3),
                                                        g[:, par, :].unsqueeze(2).to_broadcast([P, 3, DH]), ALU.mult)
                                if par:
                                    sig(ins)
                            dve.wait_ge(S["gd_pe"], e_pe + 1)
                            if b:
                                dve.wait_ge(S["gd_dve"], e_dve)
                            sig(dve.tensor_tensor(kbT[:, :, :], gkT[:, :, b * P:(b + 1) * P],
                                                  bank[5][:, 0:3 * P].rearrange(pc, a=3), ALU.mult))
                            dve.wait_ge(S["gd_act"], e_act + 2)
                            sig(dve.tensor_tensor(three_heads(DT), three_heads(DT), bcast(const("upper64"), 1, H_B),
                                                  ALU.mult))
                        elif step == S_DECAY:
                            dve.wait_ge(S["gd_pe"], e_pe + 3)
                            k = bank[5][:, 0:WB].rearrange(pc, a=H_B)
                            dve.tensor_tensor(kbg[:, :, :], k, bg[:, b, :].unsqueeze(2).to_broadcast(heads), ALU.mult)
                            sig(dve.tensor_tensor(kdc[:, :, :], k, kdec[:, b, :].unsqueeze(2).to_broadcast(heads),
                                                  ALU.mult))
                        elif step in (S_KK, S_QK):
                            dve.wait_ge(S["gd_pe"], e_pe + (4 if step == S_KK else 5))
                            dve.wait_ge(S["gd_dve"], e_dve + 3)
                            dst = LT if step == S_KK else AT
                            for par in range(2):
                                ins = dve.tensor_tensor(dst[:, par], bank[6 + par][:, 0:3 * DH].rearrange(pc, a=3),
                                                        DT[:, par], ALU.mult)
                            sig(ins)
                        elif step == S_INV:
                            dve.wait_ge(S["gd_dve"], e_dve + 5)
                            chain.step(dve.tensor_tensor(three_heads(BT), three_heads(LT),
                                                         bcast(const("level0"), 1, H_B), ALU.mult))
                            chain.join()
                            sig(dve.tensor_tensor(three_heads(XT), bcast(const("ident64"), 1, H_B), three_heads(BT),
                                                  ALU.subtract))
                        elif step < S_UW:
                            j, second = divmod(step - S_LEVEL, 2)
                            j += 1
                            if not second:
                                if j == 1:
                                    dve.wait_ge(S["gd_dve"], e_dve + 7)
                                sig(dve.tensor_tensor(three_heads(BT), three_heads(LT),
                                                      bcast(const(f"level{j}"), 1, H_B), ALU.mult))
                            else:
                                dve.wait_ge(S["gd_pe"], e_pe + 6 + 2 * j)
                                for i, (t, bk) in enumerate([(X, 5), (XT, 7)]):
                                    if t is X and j == LEVELS - 1:
                                        continue
                                    f = t.rearrange("p a b c -> p (a b c)")
                                    ins = dve.tensor_tensor(f, f, bank[bk][:, 0:WB], ALU.subtract)
                                sig(ins)
                        elif S_REC <= step < S_OUT:
                            ch, second = divmod(step - S_REC, 2)
                            r = rows[ch]
                            if not second:
                                dve.wait_ge(S["gd_pe"], e_pe + 18 + 4 * ch)
                                dve.wait_ge(S["gd_act"], e_act + 9)
                                u = U[r, :, :].rearrange("p h d -> p (h d)")
                                sig(dve.tensor_tensor(u, u, bank[6][r, 0:WB], ALU.subtract))
                            else:
                                dve.wait_ge(S["gd_pe"], e_pe + 20 + 4 * ch)
                                dve.wait_ge(S["gd_pool"], e_pool + 2 + ch)
                                s = bank[7][:, 0:3 * P].rearrange(pc, a=3)
                                for h in range(2):
                                    q = rows[h]
                                    ins = dve.tensor_tensor(Sbd[q, :, q], Sdec[q, :, q], s[q, :, q], ALU.add)
                                sig(ins)
                        elif step == S_OUT:
                            dve.wait_ge(S["gd_act"], e_act + 10)
                            sig(dve.tensor_reduce(oss[:, :], Y.rearrange("p a b c -> p (a b) c"), AX.X, ALU.add))
                            dve.wait_ge(S["gd_act"], e_act + 11)
                            sig(dve.tensor_tensor(oG[:, :, :], bank[5][:, 0:WB].rearrange(pc, a=H_B),
                                                  oss[:, :].unsqueeze(2).to_broadcast(heads), ALU.mult))
                        elif step == S_OUT + 1:
                            dve.wait_ge(S["gd_pe"], e_pe + 26)
                            sig(dve.scalar_tensor_tensor(kbT[:, :, :], bank[6][:, 0:3 * P].rearrange(pc, a=3),
                                                         hgain[:, 4:5], gzT[:, :, b * P:(b + 1) * P],
                                                         ALU.mult, ALU.mult))
                        elif step == S_OUT + 2:
                            dve.wait_ge(S["gd_act"], e_act + 12)
                            sl = (slice(None), slice(3, 6), slice(b * P, (b + 1) * P))
                            sig(dve.tensor_tensor(XL[sl], kbT[:, :, :], XH[sl].bitcast(F32), ALU.subtract))

                    def attention(b, slot):
                        if slot < JOBS:
                            j, n = slot, JOBS * b + slot
                            w = P * (b + 1) if j < H_A else NM
                            t = at[n % 2]
                            m = mxs[:, n % 2, 0:1]
                            dve.wait_ge(S["jt_done"], n + 1)
                            if j < H_A:
                                near = min(w, 256)
                                chain.step(dve.tensor_tensor(t[:, w - near:w], t[:, w - near:w],
                                                             strips[:, j, 256 - near:256], ALU.add))
                                chain.join()
                                mask = unsel[b][:, :] if b else const("causal")
                                chain.step(dve.tensor_tensor_reduce(out=t[:, 0:w], in0=t[:, 0:w], in1=mask,
                                                                    scale=1.0, scalar=GONE, op0=ALU.add,
                                                                    op1=ALU.max, accum_out=m))
                            else:
                                chain.step(dve.tensor_reduce(m, t[:, 0:w], AX.X, ALU.max))
                            chain.join()
                            dve.tensor_scalar(mxs[:, n % 2, 1:2], m, -1.0, None, ALU.mult).then_inc(S["jm_done"], 1)
                        if 1 <= slot <= JOBS:
                            j = slot - 1
                            n = JOBS * b + j
                            w = P * (b + 1) if j < H_A else NM
                            dve.wait_ge(S["jtr_done"], n + 1)
                            if n >= 2:
                                dve.wait_ge(S["jv_done"], n - 1)
                            dve.tensor_copy(pT[n % 2][:, 0:w], bank[2 + n % 2][:, 0:w]).then_inc(S["jp_done"], 1)
                        if slot - 2 in (H_A - 1, JOBS - 1):
                            ph = int(slot - 2 == JOBS - 1)
                            c0, c1 = (6, 8) if ph else (0, 3)
                            j0, nh = (H_A, H_M) if ph else (0, H_A)
                            n = JOBS * b + slot - 2
                            dve.wait_ge(S["je_done"], n + 1)
                            chain.step(dve.reciprocal(rrec[:, j0:j0 + nh], rsum[:, j0:j0 + nh]))
                            chain.join()
                            dve.wait_ge(S["jv_done"], n + 1)
                            r = rrec[:, j0:j0 + nh].unsqueeze(2).to_broadcast([P, nh, DH])
                            dve.tensor_tensor(oA[:, 0:nh * DH].rearrange("p (h d) -> p h d", h=nh),
                                              bank[4][:, 0:nh * DH].rearrange("p (h d) -> p h d", h=nh), r,
                                              ALU.mult).then_inc(S["o_ev"], 1)
                            dve.wait_ge(S["o_hi"], 2 * b + ph + 1)
                            sl = (slice(None), slice(c0, c1), slice(b * P, (b + 1) * P))
                            dve.tensor_tensor(XL[sl], bank[4][:, 0:P * (c1 - c0)].rearrange("p (c t) -> p c t", t=P),
                                              XH[sl].bitcast(F32), ALU.subtract).then_inc(S["o_lo"], 1)

                    dve.sem_inc(S["w_lo"], 2)
                    dve.sem_inc(S["u_free"], 2)
                    dve.sem_inc(S["x_up"], 4)
                    dve.wait_ge(S["cols_in"], 16 * COL_DMAS)
                    ffn(0)
                    prep(1)
                    rounds = selection()
                    gcols = {"dq": 0, "dk": 1, "mq": 2, "mk": 3}
                    for gi in range(N_GROUPS):
                        if gi - 1 in NORM_OF:
                            g = GROUPS[gi - 1]
                            name, c = g["name"], g["c"]
                            ap = {"dq": dqT, "dk": dkT, "mq": mqT, "mk": mkT}[name][:, c, :]
                            norm_apply(NORM_OF[gi - 1], ap, NM if name == "mk" else T,
                                       hgain[:, gcols[name]:gcols[name] + 1])
                        hook(gi)
                        if GATE_GROUP < gi < FIRST_CONV:
                            for _ in range(3):
                                next(rounds, None)
                        if FIRST_CONV <= gi < FIRST_CONV + 9:
                            conv(gi - FIRST_CONV)
                        u = GROUPS[gi]["unit"]
                        if LAST_OF_UNIT[u] == gi:
                            split_lo(u + 2, u % 2)
                    for b in range(NB):
                        dve.wait_ge(S["v_t"], b + 1)
                        dve.tensor_tensor(gvN[:, b, :].rearrange("p (h d) -> p h d", h=H_B),
                                          bank[b % 2][:, 0:WB].rearrange("p (h d) -> p h d", h=H_B),
                                          beta[:, b, :].unsqueeze(2).to_broadcast([P, H_B, DH]), ALU.mult
                                          ).then_inc(S["v_done"], 1)
                    for i in range(6):
                        norm_apply(N_NORM_A + i, (gqT if i < 3 else gkT)[:, i % 3, :], T,
                                   DH ** -0.5 if i < 3 else 1.0)
                    dve.wait_ge(S["nq_done"], N_NORM_A + 6)
                    dve.wait_ge(S["strip_in"], 16)
                    for b in range(NB):
                        for step in range(N_STEPS):
                            gdn(b, step)
                            if step in JOB_SLOT:
                                attention(b, JOB_SLOT[step])
                    for c in range(KD):
                        dve.wait_ge(S["dn_done"], KD + c + 1)
                        dve.tensor_tensor(xT[:, c, :], bank[4 + c % 4][:, :], xT[:, c, :], ALU.add
                                          ).then_inc(S["x_up"], 1)
                        if c % 2:
                            split_lo(U_MIX + 18 + c // 2, (c // 2) % 2)
                    ffn(1)

            first = min(S[n].num for n in SEMAPHORES)
            nc.all_engine_barrier(sems_to_clear=range(first, first + len(SEMAPHORES)))

        fin = [ctx.enter_context(nc.semaphore(n)) for n in ("fin_t", "fin_cp", "fin_out")]
        with nc.Block() as block:
            @block.tensor
            def _(pe):
                for n in range(2 * NB):
                    b, half = divmod(n, 2)
                    if n >= 2:
                        pe.wait_ge(fin[1], n - 1)
                    for c in range(4):
                        mm = pe.transpose(bank[n % 2][:, c * P:(c + 1) * P],
                                          xT[:, 4 * half + c, b * P:(b + 1) * P], const("ident"))
                    mm.then_inc(fin[0], 1)

            @block.vector
            def _(dve):
                for n in range(2 * NB):
                    b, half = divmod(n, 2)
                    dve.wait_ge(fin[0], n + 1)
                    dve.tensor_copy(xnat[:, b, 512 * half:512 * half + 512], bank[n % 2][:, :]
                                    ).then_inc(fin[1], 1)

            @block.sync
            def _(sp):
                for b in range(NB):
                    sp.wait_ge(fin[1], 2 * b + 2)
                    sp.dma_start(out[0, b * P:(b + 1) * P, :], xnat[:, b, :]).then_inc(fin[2], 16)
                sp.wait_ge(fin[2], 16 * NB)


INPUTS = ["x", "mem", "ffn1_norm", "ffn1_w_gate", "ffn1_w_up", "ffn1_w_down", "mix_norm", "w_in",
          "dsa_q_norm", "dsa_k_norm", "rel_bias", "gdn_conv", "gdn_A_log", "gdn_dt_bias",
          "gdn_out_norm", "mem_norm", "w_mem_kv", "mem_q_norm", "mem_k_norm", "w_out",
          "ffn2_norm", "ffn2_w_gate", "ffn2_w_up", "ffn2_w_down"]


def kernel(**inputs):
    import concourse.bacc as bacc
    from concourse.bass_utils import run_bass_kernel_spmd

    nc = bacc.Bacc("TRN2", target_bir_lowering=False, num_devices=1)
    arrays = {f"in_{n}": np.ascontiguousarray(inputs[n]) for n in INPUTS}
    arrays["masks"] = np.ascontiguousarray(np.concatenate(list(CONSTS.values()), axis=1))
    arrays["hot_rows"] = bucket_rows()
    args = [nc.dram_tensor(n, a.shape, mybir.dt.from_np(a.dtype), kind="ExternalInput").ap()
            for n, a in arrays.items()]
    args.append(nc.dram_tensor("out", inputs["x"].shape, F32, kind="ExternalOutput").ap())
    hybrid_trunk(nc, *args)
    got = run_bass_kernel_spmd(nc, [arrays], core_ids=[0])
    return got.results[0]["out"]
```

```python
import math
from contextlib import ExitStack

import numpy as np

import concourse.bass as bass
from concourse import mybir

F32 = mybir.dt.float32
F32R = mybir.dt.float32r
ALU = mybir.AluOpType
ACT = mybir.ActivationFunctionType
AX = mybir.AxisListType

P = 128
EPS = 1e-6
T = 512
D = 1024
KD = D // P
NM = 256
DH = 64
FF = 2816
NF = FF // P
H_A, H_B, H_M = 6, 6, 4
H_I, D_I = 8, 32
TOPK = 128
NB = T // P
BUCKETS = 32
MAX_DIST = 128
CONV = 4
EXP_LN = "natural_log_exp_and_others"
SILU = "silu_and_others"
NEG = -1.0e30
GONE = -3.0e38
WA, WB, WM = H_A * DH, H_B * DH, H_M * DH
UNIT_COLS = 256
UNIT = KD * UNIT_COLS

O_DQ, O_DV = 0, 2 * WA
O_IQ = 3 * WA
O_IK = O_IQ + H_I * D_I
O_IW = O_IK + D_I
O_G = O_IW + H_I
O_GA = O_G + 4 * WB
O_MQ = O_GA + 2 * H_B
SM = H_I + 2 * H_B

PARTS = [(0, 8), (8, 15), (15, NF)]
GU_UNITS = 2 * (FF // UNIT_COLS)
DN_UNITS = len(PARTS) * (D // UNIT_COLS)
MIX_UNITS = 20
U_FFN = [0, GU_UNITS + DN_UNITS + MIX_UNITS]
U_MIX = GU_UNITS + DN_UNITS
LAYER_UNITS = 2 * (GU_UNITS + DN_UNITS) + MIX_UNITS

MIX_SRC = (["iq", (O_DQ, 256), "small", (O_DQ + 256, 256), (O_DQ + 512, 256), (O_DV, 256), (O_DV + 256, 128)]
           + [(O_MQ, 256)] + ["mk", "mv"] + [(O_G + 256 * i, 256) for i in range(6)]
           + [("out", i) for i in range(4)])
assert len(MIX_SRC) == MIX_UNITS
SMALL_UNIT = U_MIX + 2
SMALL_DMAS = P // D_I + 2


def unit_dmas(v):
    return SMALL_DMAS if v == SMALL_UNIT else 1


def landed_value(v):
    return 16 * sum(unit_dmas(w) for w in range(2, v + 1) if w % 2 == v % 2)


COL_DMAS = 4 + 2 * 5 + 3

GROUPS = []


def _groups():
    def g(name, u, kind, **kw):
        GROUPS.append(dict(name=name, unit=U_MIX + u, kind=kind, **kw))
    for c in range(2):
        g("iq", 0, "T", c=c, col=128 * c)
    for c in range(2):
        g("dq", 1, "T", c=c, col=128 * c, norm=True)
    g("ik", 2, "T", c=0, col=0)
    g("sm", 2, "S")
    for c in range(2, 6):
        g("dq" if c < 3 else "dk", 2 + c // 2, "T", c=c % 3, col=128 * (c % 2), norm=True)
    for b in range(NB):
        g("va", 5, "N", b=b, n=256)
    for b in range(NB):
        g("vb", 6, "N", b=b, n=128)
    for c in range(2):
        g("mq", 7, "T", c=c, col=128 * c, norm=True)
    for c in range(2):
        g("mk", 8, "M", c=c, col=128 * c, norm=True)
    for b in range(2):
        g("mv", 9, "V", b=b)
    for c in range(12):
        g(("gq", "gk", "gv", "gz")[c // 3], 10 + c // 2, "T", c=c % 3, col=128 * (c % 2))


_groups()
N_GROUPS = len(GROUPS)
GATE_GROUP = 5
FIRST_CONV = 24
NORM_OF = {i: sum(1 for x in GROUPS[:i] if x.get("norm")) for i, g in enumerate(GROUPS) if g.get("norm")}
N_NORM_A = sum(1 for g in GROUPS if g.get("norm"))
LAST_OF_UNIT = {g["unit"]: i for i, g in enumerate(GROUPS)}


def copied(gi):
    on_dve = GROUPS[gi]["kind"] in "TS"
    return ("ev_dve" if on_dve else "ev_act",
            sum(1 for g in GROUPS[:gi + 1] if (g["kind"] in "TS") == on_dve))


LO_DVE = 3
GNORM_AT = [FIRST_CONV + 7 + j for j in range(3)]
SQ_STEPS = 2 * KD - 1

LEVELS = 6
(S_ROWS, S_DECAY, S_KK, S_QK, S_INV) = range(5)
S_LEVEL = 5
S_UW = S_LEVEL + 2 * (LEVELS - 1)
S_REC = S_UW + 1
S_OUT = S_REC + 4
N_STEPS = S_OUT + 3

JOBS = H_A + H_M
SLOTS = JOBS + 2
JOB_SLOT = {1 + (n * (N_STEPS - 2)) // SLOTS: n for n in range(SLOTS)}
assert len(JOB_SLOT) == SLOTS

N_PE, N_ACT, N_DVE, N_POOL = 26, 12, 25, 3


def t5_bucket():
    n = np.arange(0, T)
    exact = BUCKETS // 2
    nf = np.maximum(n, 1).astype(np.float32)
    large = exact + (np.log(nf / np.float32(exact)) / np.float32(math.log(MAX_DIST / exact))
                     * np.float32(BUCKETS - exact)).astype(np.int32)
    return np.where(n < exact, n, np.minimum(large, BUCKETS - 1))


def constants():
    p = np.arange(P)[:, None]
    c = np.arange(P)[None, :]
    c64 = np.arange(DH)[None, :]
    f = {}
    f["ident"] = (p == c)
    f["ones"] = np.ones((P, P))
    f["same64"] = (p // 64 == c // 64)
    f["prefix"] = (p // 64 == c // 64) & (p <= c)
    f["suffix"] = (p // 64 == c // 64) & (p > c)
    f["causal"] = np.where(c > p, NEG, 0.0)
    f["upper64"] = (p % 64) <= c64
    f["ident64"] = (p % 64) == c64
    for j in range(LEVELS):
        m = 1 << j
        s = p % 64
        f[f"level{j}"] = (s // (2 * m) == c64 // (2 * m)) & (s % (2 * m) < m) & (c64 % (2 * m) >= m)
    sel = np.zeros((P, 3 * P))
    for pair in range(3):
        for m in range(P):
            sel[2 * pair + m // 64, pair * P + m] = 1.0
    f["pairsel"] = sel
    f["eps"] = np.full((P, 1), EPS)
    f["one"] = np.ones((P, 1))
    f["zero"] = np.zeros((P, 1))
    return {k: np.ascontiguousarray(v, dtype=np.float32) for k, v in f.items()}


def bucket_rows():
    hot = np.zeros((BUCKETS, 384), np.float32)
    bucket = t5_bucket()
    for i in range(384):
        hot[bucket[max(255 - i, 0)], i] += 1.0
        hot[BUCKETS - 1, i] -= 1.0
    return hot


CONSTS = constants()
CONST_AT, _at = {}, 0
for _k, _v in CONSTS.items():
    CONST_AT[_k] = (_at, _v.shape[1])
    _at += _v.shape[1]
N_CONST = _at


class Chain:

    def __init__(self, eng, sem):
        self.eng, self.sem, self.n = eng, sem, 0

    def step(self, ins):
        ins.then_inc(self.sem, 1)
        self.n += 1

    def join(self):
        self.eng.wait_ge(self.sem, self.n)


def bcast(ap, axis, n):
    shape = list(ap.shape)
    return ap.unsqueeze(axis).to_broadcast(shape[:axis] + [n] + shape[axis:])


SEMAPHORES = """
landed0 landed1 w_hi w_lo w_used
sq_done ss_done r_done xh_done xl_done x_up w_lo_pool
gate_done up_done gs_done gr_done g_free u_free hh_done hl_done dn_done
act_chain dve_chain pool_chain
cols_in mem_in strip_in
pj_done ev_act ev_dve sc_done relu_done acc_done top_done
mem_sq mem_r mem_n mem_t mem_hi mem_lo
nq_sq nq_ss nq_r nq_done conv_in conv_done silu_done
v_t v_done sm_ready sp_e sp_b g_ready gc_ps gc_ready row_ps row_ready
gd_pe gd_act gd_dve gd_pool
jl_done jt_done jm_done je_done jtr_done jp_done jv_done
o_ev o_t o_hi o_lo
""".split()


def hybrid_trunk(nc, x, mem, ffn1_norm, ffn1_w_gate, ffn1_w_up, ffn1_w_down, mix_norm, w_in,
                 dsa_q_norm, dsa_k_norm, rel_bias, gdn_conv, gdn_A_log, gdn_dt_bias,
                 gdn_out_norm, mem_norm, w_mem_kv, mem_q_norm, mem_k_norm, w_out,
                 ffn2_norm, ffn2_w_gate, ffn2_w_up, ffn2_w_down, consts, hot_rows, out):
    depth = w_in.shape[0]
    ffn_w = [(ffn1_w_gate, ffn1_w_up, ffn1_w_down), (ffn2_w_gate, ffn2_w_up, ffn2_w_down)]
    norm_w = [ffn1_norm, mix_norm, ffn2_norm]

    with ExitStack() as ctx:
        ctx.enter_context(nc.allow_non_contiguous_dma("gains and other small columns"))

        def sb(name, shape, dt=F32, stack=ctx):
            return stack.enter_context(nc.sbuf_tensor(name, shape, dt))

        xT = sb("xT", [P, KD, T])
        XH = sb("XH", [P, KD, T], F32R)
        XL = sb("XL", [P, KD, T], F32R)
        raw = [sb(f"raw{i}", [P, KD, UNIT_COLS]) for i in range(2)]
        wh = [sb(f"wh{i}", [P, KD, UNIT_COLS], F32R) for i in range(2)]
        wl = [sb(f"wl{i}", [P, KD, UNIT_COLS], F32R) for i in range(2)]
        cst = sb("cst", [P, N_CONST])

        def const(name):
            a, n = CONST_AT[name]
            return cst[:, a:a + n]

        eps, one, zero = const("eps"), const("one"), const("zero")
        far = sb("far", [P, H_A])
        gain = sb("gain", [P, 4, KD])
        hgain = sb("hgain", [P, 5])
        convw = sb("convw", [P, CONV, 9])
        gdnp = sb("gdnp", [P, 2, H_B])

        ffn_mem = ExitStack()
        HH = sb("HH", [P, NF, T], F32R, ffn_mem)
        HL = sb("HL", [P, NF, T], F32R, ffn_mem)
        sg = [sb(f"sg{i}", [P, T], F32, ffn_mem) for i in range(2)]
        hf = [sb(f"hf{i}", [P, T], F32, ffn_mem) for i in range(2)]
        rF = sb("rF", [P, T], F32, ffn_mem)
        ffn_mem.close()
        sqt, ssum = sg
        io_mem = ExitStack()
        xnat = sb("xnat", [P, NB, D], F32, io_mem)
        hot = sb("hot", [BUCKETS, 384], F32, io_mem)
        relb = sb("relb", [BUCKETS, H_A], F32, io_mem)
        rowsb = sb("rowsb", [H_A, 384], F32, io_mem)
        io_mem.close()
        dqT = sb("dqT", [P, 3, T])
        dkT = sb("dkT", [P, 3, T])
        dvN = sb("dvN", [P, NB, WA])
        mqT = sb("mqT", [P, 2, T])
        mkT = sb("mkT", [P, 2, NM])
        mvN = sb("mvN", [P, 2, WM])
        gqT = sb("gqT", [P, 3, T])
        gkT = sb("gkT", [P, 3, T])
        gzT = sb("gzT", [P, 3, T])
        gvN = sb("gvN", [P, NB, WB])
        unsel = [None] + [sb(f"unsel{b}", [P, P * (b + 1)]) for b in range(1, NB)]
        sm = sb("sm", [P, NB, SM])
        wI = sb("wI", [P, NB, H_I])
        gcol = sb("gcol", [P, 8, NB, H_B])
        beta, gdec, gcum, bg, kdec, tmpa, tmpb, tmpc = (gcol[:, i] for i in range(8))
        rowb = sb("rowb", [H_B, T])
        rowg = sb("rowg", [H_B, T])
        m8 = sb("m8", [P, 8])
        mxs = sb("mxs", [P, 2, 2])
        rsum = sb("rsum", [P, JOBS])
        rrec = sb("rrec", [P, JOBS])
        memr = sb("memr", [P, 2])
        oss = sb("oss", [P, H_B])
        rcol = sb("rcol", [P, NB])

        t_mem = ExitStack()
        rM = sb("rM", [P, T], F32, t_mem)
        acc = [None] + [sb(f"acc{b}", [P, P * (b + 1)], F32, t_mem) for b in range(1, NB)]
        wrk = sb("wrk", [P, T], F32, t_mem)
        MH = sb("MH", [P, KD, NM], F32R, t_mem)
        ML = sb("ML", [P, KD, NM], F32R, t_mem)
        nsq = [sb(f"nsq{i}", [P, T], F32, t_mem) for i in range(2)]
        nrr = nsq
        idx_mem = ExitStack()
        iqT = sb("iqT", [P, 2, T], F32, idx_mem)
        ikT = sb("ikT", [P, T], F32, idx_mem)
        rl = [sb(f"rl{i}", [P, T], F32, idx_mem) for i in range(2)]
        idx_mem.close()
        tok_mem = ExitStack()
        memN = sb("memN", [P, 2, D], F32, tok_mem)
        tok_mem.close()
        cv = [sb(f"cv{i}", [P, CONV - 1 + T], F32, t_mem) for i in range(2)]
        gvT = sb("gvT", [P, 3, T], F32, t_mem)
        t_mem.close()

        a_mem = ExitStack()

        def ab(name, shape):
            return sb(name, shape, F32, a_mem)
        at = [ab(f"at{i}", [P, T]) for i in range(2)]
        pT = [ab(f"pT{i}", [P, T]) for i in range(2)]
        oA = ab("oA", [P, WA])
        kbT = ab("kbT", [P, 3, P])
        EGr = ab("EGr", [P, 3, P])
        TG = ab("TG", [P, 2, 3, DH])
        DT = ab("DT", [P, 2, 3, DH])
        LT = ab("LT", [P, 2, 3, DH])
        AT = ab("AT", [P, 2, 3, DH])
        X = ab("X", [P, 2, 3, DH])
        XT = ab("XT", [P, 2, 3, DH])
        Y = ab("Y", [P, 2, 3, DH])
        BT = ab("BT", [P, 2, 3, DH])
        kbg = ab("kbg", [P, H_B, DH])
        kdc = ab("kdc", [P, H_B, DH])
        U = ab("U", [P, H_B, DH])
        WT = ab("WT", [P, 2, 3, DH])
        Sbd = ab("Sbd", [P, 3, P])
        Sdec = ab("Sdec", [P, 3, P])
        oG = ab("oG", [P, H_B, DH])
        strips = ab("strips", [P, H_A, 256])
        a_mem.close()

        bank = [ctx.enter_context(nc.psum_tensor(f"bank{i}", [P, T], F32)) for i in range(8)]
        strip_dram = nc.dram_tensor("bias_rows", [H_A, P, 384], F32).ap()

        S = {n: ctx.enter_context(nc.semaphore(n)) for n in SEMAPHORES}
        setup = [ctx.enter_context(nc.semaphore(f"setup_{n}"))
                 for n in ("cst", "x", "w", "pe", "cp", "rows", "hi", "lo", "out", "cols", "xh", "sq")]
        landed = [S["landed0"], S["landed1"]]

        def unit_src(v, L):
            if v in (0, 1):
                return [(ffn_w[0][v][L].rearrange("(k p) f -> p k f", p=P)[:, :, 0:UNIT_COLS], raw[v][:, :, :])]
            m = v - U_MIX
            dst = raw[v % 2]
            w = w_in[L].rearrange("(k p) n -> p k n", p=P)
            src = MIX_SRC[m]
            if src == "iq":
                return [(w[:, :, O_IQ:O_IQ + 256], dst[:, :, :])]
            if src == "small":
                reps = [(w[:, :, O_IK:O_IK + D_I], dst[:, :, D_I * r:D_I * (r + 1)]) for r in range(P // D_I)]
                return reps + [(w[:, :, O_IW:O_IW + H_I], dst[:, :, P:P + H_I]),
                               (w[:, :, O_GA:O_GA + 2 * H_B], dst[:, :, P + H_I:P + SM])]
            if src in ("mk", "mv"):
                kv = w_mem_kv[L].rearrange("(k p) n -> p k n", p=P)
                return [(kv[:, :, WM * (src == "mv"):WM * (1 + (src == "mv"))], dst[:, :, :])]
            if src[0] == "out":
                wo = w_out[L].rearrange("(k p) n -> p k n", p=P)
                return [(wo[:, :, 256 * src[1]:256 * src[1] + 256], dst[:, :, :])]
            return [(w[:, :, src[0]:src[0] + src[1]], dst[:, :, 0:src[1]])]

        def load_columns(queue, layer, done):
            for i, g in enumerate([ffn1_norm, mix_norm, ffn2_norm, mem_norm]):
                queue.dma_start(gain[:, i, :], g[layer].rearrange("(k p) -> p k", p=P)).then_inc(done, 16)
            for i, g in enumerate([dsa_q_norm, dsa_k_norm, mem_q_norm, mem_k_norm, gdn_out_norm]):
                for half in range(2):
                    queue.dma_start(hgain[half * DH:(half + 1) * DH, i:i + 1],
                                    g[layer].rearrange("(p o) -> p o", o=1)).then_inc(done, 16)
            queue.dma_start(convw[:, :, :], gdn_conv[layer].rearrange("w (c p) -> p w c", p=P)
                            ).then_inc(done, 16)
            queue.dma_start(gdnp[:, 0, :], gdn_A_log[layer].partition_broadcast(P)).then_inc(done, 16)
            queue.dma_start(gdnp[:, 1, :], gdn_dt_bias[layer].partition_broadcast(P)).then_inc(done, 16)

        def add_squares(pool, updated, updated_from, done, done_from):
            for k in range(KD):
                pool.wait_ge(updated, updated_from + k + 1)
                if k >= 2:
                    pool.wait_ge(done, done_from + 2 * k - 1)
                pool.tensor_tensor((sqt if k else ssum)[:, :], xT[:, k, :], xT[:, k, :], ALU.mult
                                   ).then_inc(done, 1)
                if k:
                    pool.wait_ge(done, done_from + 2 * k)
                    pool.tensor_tensor(ssum[:, :], ssum[:, :], sqt[:, :], ALU.add).then_inc(done, 1)
        (s_cst, s_x, s_w, s_pe, s_cp, s_rows, s_hi, s_lo, s_out, s_cols, s_xh, s_sq) = setup
        with nc.Block() as block:
            @block.sync
            def _(sp):
                for v in range(2):
                    for src, dst in unit_src(v, 0):
                        sp.dma_start(dst, src).then_inc(s_w, 16)
                sp.dma_start(xnat[:, :, :], x[0].rearrange("(b p) d -> p b d", p=P)).then_inc(s_x, 16)
                sp.wait_ge(s_rows, 1)
                sp.dma_start(strip_dram, rowsb[:, None, :].to_broadcast([H_A, P, 384])).then_inc(s_out, 16)
                sp.wait_ge(s_out, 16)

            @block.gpsimd
            def _(pool):
                pool.dma_start(cst[:, :], consts).then_inc(s_cst, 16)
                pool.dma_start(hot[:, :], hot_rows).then_inc(s_cst, 16)
                pool.dma_start(relb[:, :], rel_bias).then_inc(s_cst, 16)
                pool.dma_start(far[:, :], rel_bias[BUCKETS - 1, :].partition_broadcast(P)).then_inc(s_cst, 16)
                add_squares(pool, s_cp, 0, s_sq, 0)

            @block.tensor
            def _(pe):
                pe.wait_ge(s_cst, 64)
                pe.wait_ge(s_x, 16)
                for k in range(KD):
                    if k >= 2:
                        pe.wait_ge(s_cp, k - 1)
                    for b in range(NB):
                        mm = pe.transpose(bank[k % 2][:, b * P:(b + 1) * P], xnat[:, b, k * P:(k + 1) * P],
                                          const("ident"))
                    mm.then_inc(s_pe, 1)
                pe.matmul(bank[2][0:H_A, 0:384], relb[:, :], hot[:, :], start=True, stop=True).then_inc(s_pe, 1)

            @block.scalar
            def _(act):
                load_columns(act, 0, s_cols)
                act.wait_ge(s_cols, 16 * COL_DMAS)
                for k in range(KD):
                    act.wait_ge(s_cp, k + 1)
                    act.activation(XH[:, k, :], xT[:, k, :], ACT.Copy, scale=gain[:, 0, k:k + 1]).then_inc(s_xh, 1)
                act.wait_ge(s_w, 32)
                for v in range(2):
                    act.activation(wh[v][:, :, :], raw[v][:, :, :], ACT.Copy).then_inc(s_hi, 1)

            @block.vector
            def _(dve):
                for k in range(KD):
                    dve.wait_ge(s_pe, k + 1)
                    dve.tensor_copy(xT[:, k, :], bank[k % 2][:, :]).then_inc(s_cp, 1)
                dve.wait_ge(s_pe, KD + 1)
                dve.tensor_copy(rowsb[:, :], bank[2][0:H_A, 0:384]).then_inc(s_rows, 1)
                for k in range(KD):
                    dve.wait_ge(s_xh, k + 1)
                    dve.scalar_tensor_tensor(XL[:, k, :], xT[:, k, :], gain[:, 0, k:k + 1],
                                             XH[:, k, :].bitcast(F32), ALU.mult, ALU.subtract)
                for v in range(2):
                    dve.wait_ge(s_hi, v + 1)
                    dve.tensor_tensor(wl[v][:, :, :], raw[v][:, :, :], wh[v][:, :, :].bitcast(F32),
                                      ALU.subtract).then_inc(s_lo, 1)

        with nc.Fori(0, depth) as L:
            with nc.Block() as block:

                @block.sync
                def _(sp):
                    def load(v, pairs, slot):
                        for src, dst in pairs:
                            sp.dma_start(dst, src).then_inc(landed[slot], 16)

                    def ffn_units(q):
                        w_gate, w_up, w_down = ffn_w[q]
                        ub = U_FFN[q]
                        gu = [w[L].rearrange("(k p) (c n) -> p k c n", p=P, n=UNIT_COLS) for w in (w_gate, w_up)]
                        dn = w_down[L].rearrange("(f p) (c n) -> p f c n", p=P, n=UNIT_COLS)
                        with sp.Fori(1 - q, NF // 2) as i:
                            for j in range(2):
                                sp.wait_ge(S["w_lo"], ub + 2 * i + j - 1)
                                sp.dma_start(raw[j][:, :, :], gu[j][:, :, i, :]).then_inc(landed[j], 16)
                        with sp.Fori(0, 2) as i:
                            for r in range(DN_UNITS // 2):
                                f0, f1 = PARTS[r % 3]
                                sp.wait_ge(S["w_lo"], ub + GU_UNITS + 6 * i + (r - 1))
                                sp.dma_start(raw[r % 2][:, 0:f1 - f0, :],
                                             dn[:, f0:f1, 2 * i + r // 3, :]).then_inc(landed[r % 2], 16)

                    ffn_units(0)
                    for v in range(U_MIX, U_MIX + MIX_UNITS):
                        sp.wait_ge(S["w_lo"], v - 1)
                        if U_MIX + 2 <= v - 2 < U_MIX + 18:
                            sp.wait_ge(S["w_lo_pool"], v - 2 - U_MIX - 1)
                        load(v, unit_src(v, L), v % 2)
                        if v == U_MIX + 17:
                            sp.wait_ge(S["v_done"], NB)
                            sp.wait_ge(S["nq_done"], N_NORM_A + 6)
                            sp.dma_start(strips[:, :, :], bass.AP(
                                tensor=strip_dram.tensor, offset=strip_dram.offset + P - 1,
                                ap=[[384 - 1, P], [P * 384, H_A], [1, 256]])).then_inc(S["strip_in"], 16)
                        if v == U_MIX + 4:
                            sp.wait_ge(S["sc_done"], 24)
                            sp.wait_ge(S["acc_done"], 24)
                            sp.dma_start(memN[:, :, :], mem[0].rearrange("(m p) d -> p m d", p=P)
                                         ).then_inc(S["mem_in"], 16)
                    ffn_units(1)
                    nxt = (L + 1) % depth
                    for v in range(2):
                        sp.wait_ge(S["w_lo"], LAYER_UNITS + v - 1)
                        load(v, unit_src(v, nxt), v)

                @block.gpsimd
                def _(pool):
                    def gate_norm(q):
                        pool.wait_ge(S["r_done"], 2 * q + 1)
                        with pool.Fori(0, NF // 2) as i:
                            for fs in range(2):
                                pool.wait_ge(S["gs_done"], NF * q + 2 * i + (fs + 1))
                                pool.tensor_tensor(sg[fs][:, :], sg[fs][:, :], rF[:, :], ALU.mult
                                                   ).then_inc(S["gr_done"], 1)

                    gate_norm(0)
                    add_squares(pool, S["x_up"], 4, S["sq_done"], 0)
                    for gi in range(N_GROUPS):
                        if gi == FIRST_CONV - 4:
                            pool.wait_ge(S["acc_done"], 24)
                            pool.wait_ge(S["mem_lo"], 4)
                            for i in range(2):
                                pool.memset(cv[i][:, 0:CONV - 1], 0.0).then_inc(S["pool_chain"], 1)
                        u = GROUPS[gi]["unit"]
                        if LAST_OF_UNIT[u] == gi:
                            slot = u % 2
                            pool.wait_ge(S["w_hi"], u + 2 - 1)
                            pool.tensor_tensor(wl[slot][:, LO_DVE:, :], raw[slot][:, LO_DVE:, :],
                                               wh[slot][:, LO_DVE:, :].bitcast(F32), ALU.subtract
                                               ).then_inc(S["w_lo_pool"], 1)
                    pool.wait_ge(S["v_done"], NB)
                    pool.wait_ge(S["nq_done"], N_NORM_A + 6)
                    pool.memset(Sbd[:, :, :], 0.0).then_inc(S["pool_chain"], 1)
                    for b in range(NB):
                        tok = slice(b * P, (b + 1) * P)
                        e_pe, e_act, e_dve = b * N_PE, b * N_ACT, b * N_DVE
                        pool.wait_ge(S["gd_pe"], e_pe + 5)
                        pool.wait_ge(S["gd_act"], e_act + 1)
                        pool.tensor_tensor(gqT[:, :, tok], gqT[:, :, tok], EGr[:, :, :], ALU.mult
                                           ).then_inc(S["gd_pool"], 1)
                        for ch in range(2):
                            if ch == 0 and b == 0:
                                pool.wait_ge(S["pool_chain"], 3)
                            else:
                                pool.wait_ge(S["gd_dve"], e_dve + 19 if ch else e_dve - N_DVE + 21)
                            last = EGr[:, :, DH * ch + DH - 1:DH * ch + DH]
                            pool.tensor_tensor(Sdec[:, :, :], Sbd[:, :, :], last.to_broadcast([P, 3, P]),
                                               ALU.mult).then_inc(S["gd_pool"], 1)
                    add_squares(pool, S["x_up"], 4 + KD, S["sq_done"], SQ_STEPS)
                    gate_norm(1)
                    add_squares(pool, S["x_up"], 4 + 2 * KD, S["sq_done"], 2 * SQ_STEPS)

                @block.tensor
                def _(pe):
                    def three(out_ap, wt, at_, first, last):
                        (a_hi, a_lo), (b_hi, b_lo) = wt, at_
                        pe.matmul(out_ap, a_hi, b_hi, start=first, stop=False)
                        pe.matmul(out_ap, a_hi, b_lo, start=False, stop=False)
                        return pe.matmul(out_ap, a_lo, b_hi, start=False, stop=last)

                    def sum_squares(p):
                        if p:
                            pe.wait_ge(S["sq_done"], SQ_STEPS * p)
                        mm = pe.matmul(bank[3][:, :], const("ones"), ssum[:, :], start=True, stop=True)
                        if p == 1:
                            for b in range(NB):
                                mm = pe.matmul(bank[7][:, b:b + 1], ssum[:, b * P:(b + 1) * P], one,
                                               start=True, stop=True)
                        mm.then_inc(S["ss_done"], 1)

                    def wait_copied(gi):
                        sem, n = copied(gi)
                        pe.wait_ge(S[sem], n)

                    def wait_split(u):
                        pe.wait_ge(S["w_lo"], u + 1)
                        if U_MIX + 2 <= u < U_MIX + 18:
                            pe.wait_ge(S["w_lo_pool"], u - U_MIX - 1)

                    def ffn(q):
                        p, ub = 2 * q, U_FFN[q]
                        sum_squares(p)
                        with pe.Fori(0, NF // 2) as i:
                            for j in range(2):
                                pe.wait_ge(S["w_lo"], ub + 2 * i + (j + 1))
                                for fs in range(2):
                                    pe.wait_ge(S["g_free" if j == 0 else "u_free"], NF * q + 2 * i + (fs + 1))
                                    if j and fs:
                                        pe.wait_ge(S["r_done"], p + 1)
                                    dst = bank[2 * j + fs]
                                    cols = slice(P * fs, P * fs + P)
                                    for k in range(KD):
                                        if j == 0 and fs == 0 and q:
                                            pe.wait_ge(S["xl_done"], KD * q + k + 1)
                                        mm = three(dst[:, :], (wh[j][:, k, cols], wl[j][:, k, cols]),
                                                   (XH[:, k, :], XL[:, k, :]), k == 0, k == KD - 1)
                                    mm.then_inc(S["gate_done" if j == 0 else "up_done"], 1)
                        pe.wait_ge(S["hl_done"], NF * (q + 1))
                        with pe.Fori(0, 2) as i:
                            for r in range(DN_UNITS // 2):
                                dp, part = divmod(r, 3)
                                slot = r % 2
                                f0, f1 = PARTS[part]
                                pe.wait_ge(S["w_lo"], ub + GU_UNITS + 6 * i + (r + 1))
                                for d in range(2):
                                    if part == 0:
                                        pe.wait_ge(S["x_up"], 2 * KD * q + 4 * i + (2 * dp + d + 1))
                                    cols = slice(P * d, P * d + P)
                                    for f in range(f0, f1):
                                        mm = three(bank[4 + 2 * dp + d][:, :],
                                                   (wh[slot][:, f - f0, cols], wl[slot][:, f - f0, cols]),
                                                   (HH[:, f, :], HL[:, f, :]), f == 0, f == NF - 1)
                                    if part == 2:
                                        mm.then_inc(S["dn_done"], 1)
                                if part < 2:
                                    mm.then_inc(S["w_used"], 1)

                    def group(gi):
                        g = GROUPS[gi]
                        slot = g["unit"] % 2
                        wait_split(g["unit"])
                        if gi >= 2:
                            wait_copied(gi - 2)
                        dst, kind = bank[gi % 2], g["kind"]
                        for k in range(KD):
                            first, last = k == 0, k == KD - 1
                            act_in = (XH[:, k, :], XL[:, k, :])
                            if kind == "S":
                                continue
                            if kind == "T":
                                if gi == 0:
                                    pe.wait_ge(S["xl_done"], k + 1)
                                cols = slice(g["col"], g["col"] + P)
                                mm = three(dst[:, :], (wh[slot][:, k, cols], wl[slot][:, k, cols]), act_in,
                                           first, last)
                            elif kind == "N":
                                tok = slice(g["b"] * P, g["b"] * P + P)
                                n = g["n"]
                                mm = three(dst[:, 0:n], (XH[:, k, tok], XL[:, k, tok]),
                                           (wh[slot][:, k, 0:n], wl[slot][:, k, 0:n]), first, last)
                            elif kind == "M":
                                cols = slice(g["col"], g["col"] + P)
                                mm = three(dst[:, 0:NM], (wh[slot][:, k, cols], wl[slot][:, k, cols]),
                                           (MH[:, k, :], ML[:, k, :]), first, last)
                            else:
                                tok = slice(g["b"] * P, g["b"] * P + P)
                                mm = three(dst[:, 0:WM], (MH[:, k, tok], ML[:, k, tok]),
                                           (wh[slot][:, k, :], wl[slot][:, k, :]), first, last)
                        if kind == "S":
                            for b in range(NB):
                                tok = slice(b * P, b * P + P)
                                for k in range(KD):
                                    mm = three(dst[:, b * SM:(b + 1) * SM], (XH[:, k, tok], XL[:, k, tok]),
                                               (wh[slot][:, k, P:P + SM], wl[slot][:, k, P:P + SM]),
                                               k == 0, k == KD - 1)
                        mm.then_inc(S["pj_done"], 1)

                    def head_sums(nj, n):
                        pe.wait_ge(S["nq_sq"], nj + 1)
                        if nj >= 2:
                            pe.wait_ge(S["nq_r"], nj - 1)
                        pe.matmul(bank[2 + nj % 2][:, 0:n], const("same64"), nsq[nj % 2][:, 0:n],
                                  start=True, stop=True).then_inc(S["nq_ss"], 1)

                    def index_scores():
                        wait_copied(GATE_GROUP - 1)
                        for b in range(1, NB):
                            for h in range(H_I):
                                n = (b - 1) * H_I + h
                                rows = slice(D_I * (h % 4), D_I * (h % 4) + D_I)
                                if n >= 2:
                                    pe.wait_ge(S["relu_done"], n - 1)
                                pe.matmul(bank[4 + n % 2][:, 0:P * (b + 1)], iqT[rows, h // 4, b * P:(b + 1) * P],
                                          ikT[rows, 0:P * (b + 1)], start=True, stop=True
                                          ).then_inc(S["sc_done"], 1)

                    def memory_transposes(t):
                        if t == 0:
                            pe.wait_ge(S["mem_n"], 1)
                            pe.wait_ge(S["row_ready"], 1)
                        if t >= 2:
                            pe.wait_ge(S["mem_lo"], t - 1)
                        for k in range(2 * t, 2 * t + 2):
                            for m in range(2):
                                at0 = (k - 2 * t) * NM + m * P
                                mm = pe.transpose(bank[6 + t % 2][:, at0:at0 + P], memN[:, m, k * P:(k + 1) * P],
                                                  const("ident"))
                        mm.then_inc(S["mem_t"], 1)

                    def hook(gi):
                        if gi == GATE_GROUP:
                            index_scores()
                        if gi == 8:
                            pe.wait_ge(S["g_ready"], 1)
                            g24 = gdec.rearrange("p b h -> p (b h)")
                            pe.matmul(bank[7][:, 0:24], const("prefix"), g24, start=True, stop=True)
                            pe.matmul(bank[7][:, 32:56], const("suffix"), g24, start=True, stop=True
                                      ).then_inc(S["gc_ps"], 1)
                        if gi == 10:
                            pe.wait_ge(S["gc_ready"], 1)
                            for b in range(NB):
                                tok = slice(b * P, b * P + P)
                                pe.transpose(bank[6][0:H_B, tok], beta[:, b, :], const("ident"))
                                mm = pe.transpose(bank[7][0:H_B, tok], gcum[:, b, :], const("ident"))
                            mm.then_inc(S["row_ps"], 1)
                        if gi in (13, 15):
                            for t in range(gi - 13, gi - 11):
                                memory_transposes(t)
                        if gi == 19:
                            pe.wait_ge(S["mem_lo"], 4)

                    def gdn(b, step):
                        e_act, e_dve, e_pool = b * N_ACT, b * N_DVE, b * N_POOL
                        tok0 = b * P
                        heads = [(par, pair) for par in range(2) for pair in range(3)]
                        rows = [slice(0, DH), slice(DH, P)]

                        def sig(mm):
                            mm.then_inc(S["gd_pe"], 1)

                        def col(par, pair):
                            return slice((3 * par + pair) * DH, (3 * par + pair + 1) * DH)

                        if step == S_ROWS:
                            pe.wait_ge(S["row_ready"], 1)
                            if b:
                                pe.wait_ge(S["gd_dve"], e_dve - N_DVE + 24)
                            for pair in range(3):
                                s = const("pairsel")[0:H_B, pair * P:(pair + 1) * P]
                                pe.matmul(bank[5][:, pair * P:(pair + 1) * P], s, rowb[:, tok0:tok0 + P],
                                          start=True, stop=True)
                                mm = pe.matmul(bank[6][:, pair * P:(pair + 1) * P], s, rowg[:, tok0:tok0 + P],
                                               start=True, stop=True)
                            sig(mm)
                            pe.wait_ge(S["gd_dve"], e_dve + 1)
                            sig(pe.matmul(bank[7][:, 0:WB], const("suffix"), TG.rearrange("p a b c -> p (a b c)"),
                                          start=True, stop=True))
                        elif step == S_DECAY:
                            pe.wait_ge(S["gd_dve"], e_dve + 2)
                            for pair in range(3):
                                mm = pe.transpose(bank[5][:, pair * P:(pair + 1) * P],
                                                  gkT[:, pair, tok0:tok0 + P], const("ident"))
                            sig(mm)
                        elif step in (S_KK, S_QK):
                            if step == S_KK:
                                pe.wait_ge(S["gd_act"], e_act + 2)
                            else:
                                pe.wait_ge(S["gd_dve"], e_dve + 5)
                            for pair in range(3):
                                for par in range(2):
                                    for ch in range(2):
                                        toks = slice(tok0 + DH * ch, tok0 + DH * ch + DH)
                                        rhs = (kbT[rows[par], pair, DH * ch:DH * ch + DH] if step == S_KK
                                               else gqT[rows[par], pair, toks])
                                        mm = pe.matmul(bank[6 + par][rows[ch], pair * DH:(pair + 1) * DH],
                                                       gkT[rows[par], pair, toks], rhs, start=True, stop=True)
                            sig(mm)
                        elif step == S_INV:
                            pe.wait_ge(S["gd_dve"], e_dve + 7)
                            for par, pair in heads:
                                for ch in range(2):
                                    mm = pe.matmul(bank[5][rows[ch], col(par, pair)], XT[rows[ch], par, pair, :],
                                                   const("ident64")[rows[ch], :], start=True, stop=True)
                            sig(mm)
                        elif step < S_UW:
                            j, second = divmod(step - S_LEVEL, 2)
                            j += 1
                            if not second:
                                pe.wait_ge(S["gd_dve"], e_dve + 6 + 2 * j)
                                if j == 1:
                                    pe.wait_ge(S["gd_act"], e_act + 3)
                                for par, pair in heads:
                                    for ch in range(2):
                                        mm = pe.matmul(bank[6][rows[ch], col(par, pair)],
                                                       BT[rows[ch], par, pair, :], X[rows[ch], par, pair, :],
                                                       start=True, stop=True)
                                sig(mm)
                            else:
                                pe.wait_ge(S["gd_act"], e_act + 3 + j)
                                for par, pair in heads:
                                    for ch in range(2):
                                        if j < LEVELS - 1:
                                            pe.matmul(bank[5][rows[ch], col(par, pair)],
                                                      XT[rows[ch], par, pair, :], Y[rows[ch], par, pair, :],
                                                      start=True, stop=True)
                                        mm = pe.matmul(bank[7][rows[ch], col(par, pair)],
                                                       Y[rows[ch], par, pair, :], XT[rows[ch], par, pair, :],
                                                       start=True, stop=True)
                                sig(mm)
                        elif step == S_UW:
                            pe.wait_ge(S["gd_dve"], e_dve + 17)
                            for par, pair in heads:
                                h = 2 * pair + par
                                for ch in range(2):
                                    pe.matmul(bank[5][rows[ch], h * DH:(h + 1) * DH], XT[rows[ch], par, pair, :],
                                              gvN[rows[ch], b, h * DH:(h + 1) * DH], start=True, stop=True)
                                    mm = pe.matmul(bank[6 + ch][rows[par], pair * DH:(pair + 1) * DH],
                                                   kbg[rows[ch], h, :], XT[rows[ch], par, pair, :],
                                                   start=True, stop=True)
                            sig(mm)
                        elif step < S_OUT:
                            ch, second = divmod(step - S_REC, 2)
                            if not second:
                                pe.wait_ge(S["gd_act"], e_act + 9)
                                pe.wait_ge(S["gd_pool"], e_pool + 1)
                                if b or ch:
                                    pe.wait_ge(S["gd_dve"], e_dve + 19 if ch else e_dve - N_DVE + 21)
                                else:
                                    pe.wait_ge(S["pool_chain"], 3)
                                for pair in range(3):
                                    mm = pe.matmul(bank[6][rows[ch], pair * P:(pair + 1) * P],
                                                   WT[:, ch, pair, :], Sbd[:, pair, :], start=True, stop=True)
                                sig(mm)
                                for pair in range(3):
                                    mm = pe.matmul(bank[5][rows[ch], pair * P:(pair + 1) * P],
                                                   gqT[:, pair, tok0 + DH * ch:tok0 + DH * ch + DH],
                                                   Sbd[:, pair, :], start=(pair == 0), stop=False,
                                                   skip_group_check=True)
                                sig(mm)
                            else:
                                pe.wait_ge(S["gd_dve"], e_dve + 18 + 2 * ch)
                                for pair in range(3):
                                    mm = pe.matmul(bank[7][:, pair * P:(pair + 1) * P],
                                                   kdc[rows[ch], 2 * pair:2 * pair + 2, :],
                                                   U[rows[ch], 2 * pair:2 * pair + 2, :], start=True, stop=True)
                                sig(mm)
                                for pair in range(3):
                                    for par in range(2):
                                        h = 2 * pair + par
                                        mm = pe.matmul(bank[5][rows[ch], h * DH:(h + 1) * DH],
                                                       AT[rows[ch], par, pair, :], U[rows[ch], h, :],
                                                       start=False, stop=(h == H_B - 1), skip_group_check=True)
                                sig(mm)
                        elif step == S_OUT + 1:
                            pe.wait_ge(S["gd_dve"], e_dve + 23)
                            for pair in range(3):
                                mm = pe.transpose(bank[6][:, pair * P:(pair + 1) * P],
                                                  oG[:, 2 * pair:2 * pair + 2, :], const("ident"))
                            sig(mm)

                    def attention(b, slot):
                        if slot < JOBS:
                            j, n = slot, JOBS * b + slot
                            if n >= 2:
                                pe.wait_ge(S["jt_done"], n - 1)
                            rows = slice(DH * (j % 2), DH * (j % 2) + DH)
                            tok = slice(b * P, b * P + P)
                            if j < H_A:
                                w, q, k = P * (b + 1), dqT[rows, j // 2, tok], dkT[rows, j // 2, 0:P * (b + 1)]
                            else:
                                m = j - H_A
                                w, q, k = NM, mqT[rows, m // 2, tok], mkT[rows, m // 2, :]
                            pe.matmul(bank[n % 2][:, 0:w], q, k, start=True, stop=True).then_inc(S["jl_done"], 1)
                        if 1 <= slot <= JOBS:
                            j = slot - 1
                            n = JOBS * b + j
                            pe.wait_ge(S["je_done"], n + 1)
                            if n >= 2:
                                pe.wait_ge(S["jp_done"], n - 1)
                            for i in range(b + 1 if j < H_A else 2):
                                mm = pe.transpose(bank[2 + n % 2][:, i * P:(i + 1) * P],
                                                  at[n % 2][:, i * P:(i + 1) * P], const("ident"))
                            mm.then_inc(S["jtr_done"], 1)
                        if slot >= 2:
                            j = slot - 2
                            n = JOBS * b + j
                            pe.wait_ge(S["jp_done"], n + 1)
                            if j in (0, H_A) and (b or j):
                                pe.wait_ge(S["o_lo"], 2 * b + (j == H_A))
                            nt = b + 1 if j < H_A else 2
                            at0 = DH * (j if j < H_A else j - H_A)
                            for i in range(nt):
                                v = (dvN[:, i, at0:at0 + DH] if j < H_A else mvN[:, i, at0:at0 + DH])
                                mm = pe.matmul(bank[4][:, at0:at0 + DH], pT[n % 2][:, i * P:(i + 1) * P], v,
                                               start=(i == 0), stop=(i == nt - 1))
                            mm.then_inc(S["jv_done"], 1)
                            if j in (H_A - 1, JOBS - 1):
                                ph = int(j == JOBS - 1)
                                pe.wait_ge(S["o_ev"], 2 * b + ph + 1)
                                for c in range(2 if ph else 3):
                                    mm = pe.transpose(bank[4][:, c * P:(c + 1) * P], oA[:, c * P:(c + 1) * P],
                                                      const("ident"))
                                mm.then_inc(S["o_t"], 1)

                    ffn(0)
                    for gi in range(N_GROUPS):
                        group(gi)
                        if gi == 0:
                            sum_squares(1)
                        if gi - 1 in NORM_OF:
                            head_sums(NORM_OF[gi - 1], NM if GROUPS[gi - 1]["name"] == "mk" else T)
                        hook(gi)
                        if gi in GNORM_AT:
                            for i in range(2):
                                head_sums(N_NORM_A + 2 * GNORM_AT.index(gi) + i, T)
                    for b in range(NB):
                        pe.wait_ge(S["silu_done"], 3)
                        wait_copied(N_GROUPS - 1)
                        if b >= 2:
                            pe.wait_ge(S["v_done"], b - 1)
                        for pair in range(3):
                            mm = pe.transpose(bank[b % 2][:, pair * P:(pair + 1) * P],
                                              gvT[:, pair, b * P:(b + 1) * P], const("ident"))
                        mm.then_inc(S["v_t"], 1)
                    pe.wait_ge(S["v_done"], NB)
                    pe.wait_ge(S["nq_done"], N_NORM_A + 6)
                    for b in range(NB):
                        for step in range(N_STEPS):
                            gdn(b, step)
                            if step in JOB_SLOT:
                                attention(b, JOB_SLOT[step])
                    pe.wait_ge(S["o_lo"], 2 * NB)
                    pe.wait_ge(S["gd_dve"], NB * N_DVE)
                    for c in range(KD):
                        u = U_MIX + 16 + c // 2
                        wait_split(u)
                        pe.wait_ge(S["x_up"], KD + c + 1)
                        cols = slice(P * (c % 2), P * (c % 2) + P)
                        for k in range(KD):
                            mm = three(bank[4 + c % 4][:, :], (wh[u % 2][:, k, cols], wl[u % 2][:, k, cols]),
                                       (XH[:, k, :], XL[:, k, :]), k == 0, k == KD - 1)
                        mm.then_inc(S["dn_done"], 1)
                    ffn(1)

                @block.scalar
                def _(act):
                    chain = Chain(act, S["act_chain"])

                    def split_hi(v, wait_landed, slot):
                        act.wait_ge(landed[slot], wait_landed)
                        act.activation(wh[slot][:, :, :], raw[slot][:, :, :], ACT.Copy).then_inc(S["w_hi"], 1)

                    def rsqrt(dst, src, scale):
                        chain.step(act.activation(dst, src, ACT.Ln, bias=eps[0:dst.shape[0], :], scale=scale))
                        chain.join()
                        return act.activation(dst, dst, ACT.Exp, scale=-0.5)

                    def hi_of_x(p, k, scale_at):
                        act.activation(XH[:, k, :], xT[:, k, :], ACT.Copy, scale=gain[:, p, scale_at]
                                       ).then_inc(S["xh_done"], 1)

                    def ffn(q):
                        ub = U_FFN[q]
                        act.preload_act_table_set(EXP_LN)
                        act.wait_ge(S["ss_done"], 2 * q + 1)
                        rsqrt(rF[:, :], bank[3][:, :], 1.0 / D).then_inc(S["r_done"], 1)
                        act.preload_act_table_set(SILU)
                        with act.Fori(0, NF // 2) as i:
                            for fs in range(2):
                                act.wait_ge(S["g_free"], NF * q + 2 * i + (fs + 3))
                                act.activation(sg[fs][:, :], sg[fs][:, :], ACT.Silu).then_inc(S["gs_done"], 1)
                            split_hi(0, landed_value(ub + 2) + 16 * i, 0)
                            for fs in range(2):
                                act.wait_ge(S["u_free"], NF * q + 2 * i + (fs + 3))
                                act.activation(HH[:, 2 * i + fs, :], hf[fs][:, :], ACT.Copy
                                               ).then_inc(S["hh_done"], 1)
                            split_hi(1, landed_value(ub + 3) + 16 * i, 1)
                        if q:
                            act.wait_ge(S["xl_done"], 2 * KD)
                            load_columns(act, (L + 1) % depth, S["cols_in"])
                            act.wait_ge(S["cols_in"], 16 * COL_DMAS)
                        with act.Fori(0, 2) as i:
                            for r in range(DN_UNITS // 2):
                                dp, part = divmod(r, 3)
                                if part < 2:
                                    act.wait_ge(S["w_used"], DN_UNITS * 2 // 3 * q + 4 * i + (2 * dp + part + 1))
                                else:
                                    act.wait_ge(S["dn_done"], 2 * KD * q + 4 * i + (2 * dp + 2))
                                split_hi(0, landed_value(ub + GU_UNITS + r + 2) + 48 * i, r % 2)
                                if part == 2:
                                    for d in range(2):
                                        c = 2 * dp + d
                                        act.wait_ge(S["x_up"], 2 * KD * q + 4 * i + (4 + c + 1))
                                        hi_of_x(1 - q, 4 * i + c, bass.ds(4 * i + c, 1))

                    def evac(gi):
                        g = GROUPS[gi]
                        act.wait_ge(S["pj_done"], gi + 1)
                        name, c, b, src = g["name"], g.get("c"), g.get("b"), bank[gi % 2]
                        if name == "mk":
                            act.activation(mkT[:, c, :], src[:, 0:NM], ACT.Copy).then_inc(S["ev_act"], 1)
                        elif name == "mv":
                            act.activation(mvN[:, b, :], src[:, 0:WM], ACT.Copy).then_inc(S["ev_act"], 1)
                        else:
                            dst = dvN[:, b, 0:256] if name == "va" else dvN[:, b, 256:WA]
                            act.activation(dst, src[:, 0:g["n"]], ACT.Copy, scale=rcol[:, b:b + 1]
                                           ).then_inc(S["ev_act"], 1)

                    def wait_copied(gi):
                        sem, n = copied(gi)
                        act.wait_ge(S[sem], n)

                    def square_of(nj, ap, n):
                        if nj >= 2:
                            act.wait_ge(S["nq_done"], nj - 1)
                        act.activation(nsq[nj % 2][:, 0:n], ap, ACT.Square).then_inc(S["nq_sq"], 1)

                    def head_rsqrt(nj, n, scale):
                        act.wait_ge(S["nq_ss"], nj + 1)
                        rsqrt(nrr[nj % 2][:, 0:n], bank[2 + nj % 2][:, 0:n], scale).then_inc(S["nq_r"], 1)

                    def index_relu():
                        for n in range(3 * H_I):
                            b = 1 + n // H_I
                            act.wait_ge(S["sc_done"], n + 1)
                            if n >= 2:
                                act.wait_ge(S["acc_done"], n - 1)
                            act.activation(rl[n % 2][:, 0:P * (b + 1)], bank[4 + n % 2][:, 0:P * (b + 1)], ACT.Relu,
                                           scale=D_I ** -0.5).then_inc(S["relu_done"], 1)

                    def hook(gi):
                        if gi == GATE_GROUP:
                            index_relu()
                        if gi == 7:
                            act.wait_ge(S["sp_e"], 1)
                            chain.step(act.activation(tmpb, tmpb, ACT.Exp))
                            chain.step(act.activation(gdnp[:, 0, :], gdnp[:, 0, :], ACT.Exp))
                            chain.step(act.activation(tmpc, tmpc, ACT.Exp))
                            chain.join()
                            act.activation(tmpb, tmpb, ACT.Ln, bias=one).then_inc(S["sp_b"], 1)
                        if gi == 9:
                            act.wait_ge(S["gc_ps"], 1)
                            ps = [bank[7][:, 32 * i:32 * i + 24] for i in range(2)]
                            flat = [t.rearrange("p b h -> p (b h)") for t in (gcum, bg, kdec)]
                            chain.step(act.activation(flat[0], ps[0], ACT.Copy))
                            chain.step(act.activation(flat[1], ps[0], ACT.Exp))
                            chain.step(act.activation(flat[2], ps[1], ACT.Exp))
                            chain.join()
                            act.sem_inc(S["gc_ready"], 1)
                        if gi == 11:
                            act.wait_ge(S["row_ps"], 1)
                            chain.step(act.activation(rowb[:, :], bank[6][0:H_B, :], ACT.Copy))
                            chain.step(act.activation(rowg[:, :], bank[7][0:H_B, :], ACT.Copy))
                            chain.join()
                            act.sem_inc(S["row_ready"], 1)
                            act.wait_ge(S["mem_in"], 16)
                            for m in range(2):
                                chain.step(act.activation(MH[:, 4 * m:4 * m + 4, :], memN[:, m, :], ACT.Square,
                                                          accum_out=memr[:, m:m + 1]))
                            chain.join()
                            rsqrt(memr[:, :], memr[:, :], 1.0 / D).then_inc(S["mem_r"], 1)
                        if gi in (14, 16):
                            for t in range(gi - 14, gi - 12):
                                act.wait_ge(S["mem_t"], t + 1)
                                for k in range(2 * t, 2 * t + 2):
                                    chain.step(act.activation(MH[:, k, :], bank[6 + t % 2][:, (k % 2) * NM:(k % 2) * NM + NM],
                                                              ACT.Copy, scale=gain[:, 3, k:k + 1]))
                                chain.join()
                                act.sem_inc(S["mem_hi"], 1)

                    def gdn(b, step):
                        e_pe, e_dve, e_pool = b * N_PE, b * N_DVE, b * N_POOL

                        def sig(ins):
                            ins.then_inc(S["gd_act"], 1)
                        flat = "p a b c -> p (a b c)"
                        if step == S_ROWS:
                            act.wait_ge(S["gd_pe"], e_pe + 1)
                            if b:
                                act.wait_ge(S["gd_pool"], e_pool)
                            sig(act.activation(EGr.rearrange("p a b -> p (a b)"), bank[6][:, 0:3 * P], ACT.Exp))
                            act.wait_ge(S["gd_pe"], e_pe + 2)
                            sig(act.activation(DT.rearrange(flat), bank[7][:, 0:WB], ACT.Exp))
                        elif step == S_INV:
                            act.wait_ge(S["gd_pe"], e_pe + 6)
                            sig(act.activation(X.rearrange(flat), bank[5][:, 0:WB], ACT.Copy))
                        elif S_LEVEL <= step < S_UW and (step - S_LEVEL) % 2 == 0:
                            j = (step - S_LEVEL) // 2 + 1
                            act.wait_ge(S["gd_pe"], e_pe + 5 + 2 * j)
                            sig(act.activation(Y.rearrange(flat), bank[6][:, 0:WB], ACT.Copy))
                        elif step == S_UW:
                            act.wait_ge(S["gd_pe"], e_pe + 17)
                            chain.step(act.activation(U.rearrange("p h d -> p (h d)"), bank[5][:, 0:WB], ACT.Copy))
                            for ch in range(2):
                                chain.step(act.activation(WT[:, ch].rearrange("p a b -> p (a b)"),
                                                          bank[6 + ch][:, 0:3 * DH], ACT.Copy))
                            chain.join()
                            act.sem_inc(S["gd_act"], 1)
                        elif step == S_OUT:
                            act.wait_ge(S["gd_pe"], e_pe + 25)
                            sig(act.activation(Y.rearrange(flat), bank[5][:, 0:WB], ACT.Square))
                            act.wait_ge(S["gd_dve"], e_dve + 22)
                            sig(rsqrt(oss[:, :], oss[:, :], 1.0 / DH))
                        elif step == S_OUT + 2:
                            act.wait_ge(S["gd_dve"], e_dve + 24)
                            sig(act.activation(XH[:, 3:6, b * P:(b + 1) * P], kbT[:, :, :], ACT.Copy))

                    def attention(b, slot):
                        if slot < JOBS:
                            j, n = slot, JOBS * b + slot
                            w = P * (b + 1) if j < H_A else NM
                            act.wait_ge(S["jl_done"], n + 1)
                            if n >= 2:
                                act.wait_ge(S["jtr_done"], n - 1)
                            bias = far[:, j:j + 1] if j < H_A else zero
                            act.activation(at[n % 2][:, 0:w], bank[n % 2][:, 0:w], ACT.Identity, bias=bias,
                                           scale=DH ** -0.5).then_inc(S["jt_done"], 1)
                            act.wait_ge(S["jm_done"], n + 1)
                            act.activation(at[n % 2][:, 0:w], at[n % 2][:, 0:w], ACT.Exp,
                                           bias=mxs[:, n % 2, 1:2], accum_out=rsum[:, j:j + 1]
                                           ).then_inc(S["je_done"], 1)
                        if slot - 2 in (H_A - 1, JOBS - 1):
                            ph = int(slot - 2 == JOBS - 1)
                            act.wait_ge(S["o_t"], 2 * b + ph + 1)
                            c0, c1 = (6, 8) if ph else (0, 3)
                            act.activation(XH[:, c0:c1, b * P:(b + 1) * P],
                                           bank[4][:, 0:P * (c1 - c0)].rearrange("p (c t) -> p c t", t=P),
                                           ACT.Copy).then_inc(S["o_hi"], 1)

                    ffn(0)
                    act.preload_act_table_set(EXP_LN)
                    act.wait_ge(S["ss_done"], 2)
                    rsqrt(rM[:, :], bank[3][:, :], 1.0 / D).then_inc(S["act_chain"], 1)
                    chain.n += 1
                    rsqrt(rcol[:, :], bank[7][:, 0:NB], 1.0 / D).then_inc(S["act_chain"], 1)
                    chain.n += 1
                    chain.join()
                    act.sem_inc(S["r_done"], 1)
                    for gi in range(N_GROUPS):
                        g = GROUPS[gi]
                        if copied(gi)[0] == "ev_act":
                            evac(gi)
                        if gi - 1 in NORM_OF:
                            head_rsqrt(NORM_OF[gi - 1], NM if GROUPS[gi - 1]["name"] == "mk" else T, 1.0 / DH)
                        if gi in NORM_OF:
                            wait_copied(gi)
                            c = g["c"]
                            square_of(NORM_OF[gi], mkT[:, c, :] if g["name"] == "mk" else
                                      {"dq": dqT, "dk": dkT, "mq": mqT}[g["name"]][:, c, :],
                                      NM if g["name"] == "mk" else T)
                        if gi - 1 in GNORM_AT:
                            for i in range(2):
                                head_rsqrt(N_NORM_A + 2 * GNORM_AT.index(gi - 1) + i, T, 1.0)
                        if gi == GNORM_AT[0]:
                            act.wait_ge(S["conv_done"], 6)
                            for t in (gqT, gkT):
                                f = t.rearrange("p c t -> p (c t)")
                                act.activation(f, f, ACT.Silu).then_inc(S["silu_done"], 1)
                            act.preload_act_table_set(EXP_LN)
                            act.wait_ge(S["silu_done"], 2)
                        if gi in GNORM_AT:
                            for i in range(2):
                                n = 2 * GNORM_AT.index(gi) + i
                                square_of(N_NORM_A + n, (gqT if n < 3 else gkT)[:, n % 3, :], T)
                        hook(gi)
                        u = g["unit"]
                        if LAST_OF_UNIT[u] == gi:
                            act.wait_ge(S["pj_done"], gi + 1)
                            split_hi(u + 2, landed_value(u + 2), u % 2)
                    act.wait_ge(S["conv_done"], 9)
                    wait_copied(N_GROUPS - 1)
                    for t in (gvT, gzT):
                        f = t.rearrange("p c t -> p (c t)")
                        act.activation(f, f, ACT.Silu).then_inc(S["silu_done"], 1)
                    act.preload_act_table_set(EXP_LN)
                    act.wait_ge(S["v_done"], NB)
                    act.wait_ge(S["nq_done"], N_NORM_A + 6)
                    for b in range(NB):
                        for step in range(N_STEPS):
                            gdn(b, step)
                            if step in JOB_SLOT:
                                attention(b, JOB_SLOT[step])
                    for i in range(4):
                        act.wait_ge(S["dn_done"], KD + 2 * i + 2)
                        split_hi(0, landed_value(U_MIX + 18 + i), i % 2)
                    act.wait_ge(S["dn_done"], 2 * KD)
                    for k in range(KD):
                        act.wait_ge(S["x_up"], 4 + KD + k + 1)
                        hi_of_x(2, k, slice(k, k + 1))
                    ffn(1)

                @block.vector
                def _(dve):
                    chain = Chain(dve, S["dve_chain"])

                    def split_lo(v, slot, upto=KD):
                        dve.wait_ge(S["w_hi"], v - 1)
                        dve.tensor_tensor(wl[slot][:, 0:upto, :], raw[slot][:, 0:upto, :],
                                          wh[slot][:, 0:upto, :].bitcast(F32), ALU.subtract
                                          ).then_inc(S["w_lo"], 1)

                    def lo_of_x(p, k, scale_at, done):
                        dve.wait_ge(S["xh_done"], done)
                        dve.scalar_tensor_tensor(XL[:, k, :], xT[:, k, :], gain[:, p, scale_at],
                                                 XH[:, k, :].bitcast(F32), ALU.mult, ALU.subtract
                                                 ).then_inc(S["xl_done"], 1)

                    def ffn(q):
                        ub = U_FFN[q]
                        dve.wait_ge(S["r_done"], 2 * q + 1)
                        with dve.Fori(0, NF // 2) as i:
                            for fs in range(2):
                                f1 = NF * q + 2 * i + (fs + 1)
                                dve.wait_ge(S["gate_done"], f1)
                                dve.wait_ge(S["u_free"], f1)
                                dve.tensor_tensor(sg[fs][:, :], bank[fs][:, :], rF[:, :], ALU.mult
                                                  ).then_inc(S["g_free"], 1)
                            split_lo(ub + 2 * i + 2, 0)
                            for fs in range(2):
                                f1 = NF * q + 2 * i + (fs + 1)
                                dve.wait_ge(S["up_done"], f1)
                                dve.wait_ge(S["gr_done"], f1)
                                dve.tensor_tensor(hf[fs][:, :], sg[fs][:, :], bank[2 + fs][:, :], ALU.mult
                                                  ).then_inc(S["u_free"], 1)
                                dve.wait_ge(S["hh_done"], NF * q + 2 * i + (fs + 1))
                                dve.tensor_tensor(HL[:, 2 * i + fs, :], hf[fs][:, :],
                                                  HH[:, 2 * i + fs, :].bitcast(F32), ALU.subtract
                                                  ).then_inc(S["hl_done"], 1)
                            split_lo(ub + 2 * i + 3, 1)
                        with dve.Fori(0, 2) as i:
                            for r in range(DN_UNITS // 2):
                                if r % 3 == 2:
                                    for d in range(2):
                                        c = 2 * (r // 3) + d
                                        dve.wait_ge(S["dn_done"], 2 * KD * q + 4 * i + (c + 1))
                                        dve.scalar_tensor_tensor(xT[:, 4 * i + c, :], bank[4 + c][:, :], 0.5,
                                                                 xT[:, 4 * i + c, :], ALU.mult, ALU.add
                                                                 ).then_inc(S["x_up"], 1)
                                split_lo(ub + GU_UNITS + 6 * i + (r + 2), r % 2)
                                if r % 3 == 2:
                                    for d in range(2):
                                        c = 2 * (r // 3) + d
                                        lo_of_x(1 - q, 4 * i + c, bass.ds(4 * i + c, 1),
                                                2 * KD * q + 4 * i + (c + 1))

                    def norm_apply(nj, ap, n, factor):
                        dve.wait_ge(S["nq_r"], nj + 1)
                        dve.scalar_tensor_tensor(ap, ap, factor, nrr[nj % 2][:, 0:n], ALU.mult, ALU.mult
                                                 ).then_inc(S["nq_done"], 1)

                    def index_sum():
                        for n in range(3 * H_I):
                            b, h = 1 + n // H_I, n % H_I
                            w = P * (b + 1)
                            dve.wait_ge(S["relu_done"], n + 1)
                            if h == 0:
                                ins = dve.tensor_scalar(acc[b][:, :], rl[n % 2][:, 0:w], wI[:, b, h:h + 1], None,
                                                        ALU.mult)
                            else:
                                dve.wait_ge(S["acc_done"], n)
                                ins = dve.scalar_tensor_tensor(acc[b][:, :], rl[n % 2][:, 0:w], wI[:, b, h:h + 1],
                                                               acc[b][:, :], ALU.mult, ALU.add)
                            ins.then_inc(S["acc_done"], 1)
                        dve.wait_ge(S["acc_done"], 3 * H_I)
                        for b in range(1, NB):
                            last = acc[b][:, P * b:P * (b + 1)]
                            chain.step(dve.tensor_tensor(last, last, const("causal"), ALU.add))

                    def selection():
                        for b in range(1, NB):
                            w = P * (b + 1)
                            for r in range(TOPK // 8):
                                src = acc[b][:, :] if r == 0 else wrk[:, 0:w]
                                chain.join()
                                chain.step(dve.max(m8[:, :], src))
                                chain.join()
                                chain.step(dve.match_replace(wrk[:, 0:w], m8[:, :], src, GONE))
                                if r == TOPK // 8 - 1:
                                    chain.join()
                                    chain.step(dve.tensor_tensor(unsel[b][:, :], wrk[:, 0:w], acc[b][:, :],
                                                                 ALU.is_equal))
                                    chain.join()
                                    chain.step(dve.tensor_scalar(unsel[b][:, :], unsel[b][:, :], NEG, None,
                                                                 ALU.mult))
                                yield

                    def conv(n):
                        dst = (gqT, gkT, gvT)[n // 3][:, n % 3, :]
                        wait_copied(FIRST_CONV + n)
                        src = cv[n % 2]
                        chain.step(dve.tensor_scalar(dst, src[:, 0:T], convw[:, 0, n:n + 1], None, ALU.mult))
                        for i in range(1, CONV):
                            chain.join()
                            ins = dve.scalar_tensor_tensor(dst, src[:, i:i + T], convw[:, i, n:n + 1], dst,
                                                           ALU.mult, ALU.add)
                            if i < CONV - 1:
                                chain.step(ins)
                        ins.then_inc(S["conv_done"], 1)

                    def wait_copied(gi):
                        sem, n = copied(gi)
                        dve.wait_ge(S[sem], n)

                    def evac(gi):
                        g = GROUPS[gi]
                        dve.wait_ge(S["pj_done"], gi + 1)
                        name, c, src = g["name"], g.get("c"), bank[gi % 2]
                        if name == "sm":
                            dve.tensor_tensor(sm[:, :, :], src[:, 0:NB * SM].rearrange("p (b n) -> p b n", b=NB),
                                              rcol[:, :].unsqueeze(2).to_broadcast([P, NB, SM]), ALU.mult
                                              ).then_inc(S["ev_dve"], 1)
                            return
                        if name == "ik":
                            dst = ikT[:, :]
                        elif name in ("gq", "gk", "gv"):
                            n = gi - FIRST_CONV
                            if n == 0:
                                dve.wait_ge(S["mem_t"], 4)
                                dve.wait_ge(S["pool_chain"], 2)
                            if n >= 2:
                                dve.wait_ge(S["conv_done"], n - 1)
                            dst = cv[n % 2][:, CONV - 1:]
                        else:
                            dst = {"iq": iqT, "dq": dqT, "dk": dkT, "mq": mqT, "gz": gzT}[name][:, c, :]
                        dve.tensor_tensor(dst, src[:, :], rM[:, :], ALU.mult).then_inc(S["ev_dve"], 1)

                    def hook(gi):
                        if gi == GATE_GROUP:
                            wait_copied(GATE_GROUP)
                            chain.step(dve.tensor_scalar(wI[:, :, :], sm[:, :, 0:H_I], H_I ** -0.5, None, ALU.mult))
                            chain.join()
                            index_sum()
                            dtb = bcast(gdnp[:, 1, :], 1, NB)
                            chain.step(dve.tensor_tensor(tmpa, sm[:, :, H_I:H_I + H_B], dtb, ALU.add))
                            chain.step(dve.tensor_scalar(tmpc, sm[:, :, H_I + H_B:SM], -1.0, 85.0, ALU.mult, ALU.min))
                            chain.join()
                            chain.step(dve.tensor_scalar(tmpb, tmpa, -1.0, None, ALU.mult))
                            chain.join()
                            dve.tensor_tensor(tmpb, tmpb, tmpa, ALU.min).then_inc(S["sp_e"], 1)
                        if gi == 7:
                            dve.wait_ge(S["sp_b"], 1)
                            chain.step(dve.scalar_tensor_tensor(tmpa, tmpa, 0.0, tmpb, ALU.max, ALU.add))
                            chain.step(dve.tensor_scalar(tmpc, tmpc, 1.0, None, ALU.add))
                            chain.join()
                            chain.step(dve.reciprocal(beta, tmpc))
                            chain.step(dve.scalar_tensor_tensor(gdec, tmpa, -1.0, bcast(gdnp[:, 0, :], 1, NB),
                                                                ALU.mult, ALU.mult))
                            chain.join()
                            dve.sem_inc(S["g_ready"], 1)
                        if gi == 10:
                            dve.wait_ge(S["gc_ready"], 1)
                            chain.step(dve.tensor_tensor(bg, bg, beta, ALU.mult))
                        if gi == 12:
                            dve.wait_ge(S["mem_r"], 1)
                            for m in range(2):
                                chain.step(dve.tensor_scalar(memN[:, m, :], memN[:, m, :], memr[:, m:m + 1], None,
                                                             ALU.mult))
                            chain.join()
                            dve.sem_inc(S["mem_n"], 1)
                        if gi in (14, 16):
                            for t in range(gi - 14, gi - 12):
                                dve.wait_ge(S["mem_hi"], t + 1)
                                for k in range(2 * t, 2 * t + 2):
                                    ps = bank[6 + t % 2][:, (k % 2) * NM:(k % 2) * NM + NM]
                                    chain.step(dve.scalar_tensor_tensor(ML[:, k, :], ps, gain[:, 3, k:k + 1],
                                                                        MH[:, k, :].bitcast(F32), ALU.mult,
                                                                        ALU.subtract))
                                chain.join()
                                dve.sem_inc(S["mem_lo"], 1)

                    def gdn(b, step):
                        e_pe, e_act, e_dve, e_pool = b * N_PE, b * N_ACT, b * N_DVE, b * N_POOL
                        rows = [slice(0, DH), slice(DH, P)]
                        pc = "p (a c) -> p a c"

                        def sig(ins):
                            ins.then_inc(S["gd_dve"], 1)

                        def three_heads(t):
                            return t.rearrange("p a b c -> p (a b) c")
                        heads = [P, H_B, DH]
                        if step == S_ROWS:
                            g = gdec[:, b, :].rearrange("p (b a) -> p a b", a=2)
                            for par in range(2):
                                ins = dve.tensor_tensor(TG[:, par, :, :], bcast(const("upper64"), 1, 3),
                                                        g[:, par, :].unsqueeze(2).to_broadcast([P, 3, DH]), ALU.mult)
                                if par:
                                    sig(ins)
                            dve.wait_ge(S["gd_pe"], e_pe + 1)
                            if b:
                                dve.wait_ge(S["gd_dve"], e_dve)
                            sig(dve.tensor_tensor(kbT[:, :, :], gkT[:, :, b * P:(b + 1) * P],
                                                  bank[5][:, 0:3 * P].rearrange(pc, a=3), ALU.mult))
                            dve.wait_ge(S["gd_act"], e_act + 2)
                            sig(dve.tensor_tensor(three_heads(DT), three_heads(DT), bcast(const("upper64"), 1, H_B),
                                                  ALU.mult))
                        elif step == S_DECAY:
                            dve.wait_ge(S["gd_pe"], e_pe + 3)
                            k = bank[5][:, 0:WB].rearrange(pc, a=H_B)
                            dve.tensor_tensor(kbg[:, :, :], k, bg[:, b, :].unsqueeze(2).to_broadcast(heads), ALU.mult)
                            sig(dve.tensor_tensor(kdc[:, :, :], k, kdec[:, b, :].unsqueeze(2).to_broadcast(heads),
                                                  ALU.mult))
                        elif step in (S_KK, S_QK):
                            dve.wait_ge(S["gd_pe"], e_pe + (4 if step == S_KK else 5))
                            dve.wait_ge(S["gd_dve"], e_dve + 3)
                            dst = LT if step == S_KK else AT
                            for par in range(2):
                                ins = dve.tensor_tensor(dst[:, par], bank[6 + par][:, 0:3 * DH].rearrange(pc, a=3),
                                                        DT[:, par], ALU.mult)
                            sig(ins)
                        elif step == S_INV:
                            dve.wait_ge(S["gd_dve"], e_dve + 5)
                            chain.step(dve.tensor_tensor(three_heads(BT), three_heads(LT),
                                                         bcast(const("level0"), 1, H_B), ALU.mult))
                            chain.join()
                            sig(dve.tensor_tensor(three_heads(XT), bcast(const("ident64"), 1, H_B), three_heads(BT),
                                                  ALU.subtract))
                        elif step < S_UW:
                            j, second = divmod(step - S_LEVEL, 2)
                            j += 1
                            if not second:
                                if j == 1:
                                    dve.wait_ge(S["gd_dve"], e_dve + 7)
                                sig(dve.tensor_tensor(three_heads(BT), three_heads(LT),
                                                      bcast(const(f"level{j}"), 1, H_B), ALU.mult))
                            else:
                                dve.wait_ge(S["gd_pe"], e_pe + 6 + 2 * j)
                                for i, (t, bk) in enumerate([(X, 5), (XT, 7)]):
                                    if t is X and j == LEVELS - 1:
                                        continue
                                    f = t.rearrange("p a b c -> p (a b c)")
                                    ins = dve.tensor_tensor(f, f, bank[bk][:, 0:WB], ALU.subtract)
                                sig(ins)
                        elif S_REC <= step < S_OUT:
                            ch, second = divmod(step - S_REC, 2)
                            r = rows[ch]
                            if not second:
                                dve.wait_ge(S["gd_pe"], e_pe + 18 + 4 * ch)
                                dve.wait_ge(S["gd_act"], e_act + 9)
                                u = U[r, :, :].rearrange("p h d -> p (h d)")
                                sig(dve.tensor_tensor(u, u, bank[6][r, 0:WB], ALU.subtract))
                            else:
                                dve.wait_ge(S["gd_pe"], e_pe + 20 + 4 * ch)
                                dve.wait_ge(S["gd_pool"], e_pool + 2 + ch)
                                s = bank[7][:, 0:3 * P].rearrange(pc, a=3)
                                for h in range(2):
                                    q = rows[h]
                                    ins = dve.tensor_tensor(Sbd[q, :, q], Sdec[q, :, q], s[q, :, q], ALU.add)
                                sig(ins)
                        elif step == S_OUT:
                            dve.wait_ge(S["gd_act"], e_act + 10)
                            sig(dve.tensor_reduce(oss[:, :], Y.rearrange("p a b c -> p (a b) c"), AX.X, ALU.add))
                            dve.wait_ge(S["gd_act"], e_act + 11)
                            sig(dve.tensor_tensor(oG[:, :, :], bank[5][:, 0:WB].rearrange(pc, a=H_B),
                                                  oss[:, :].unsqueeze(2).to_broadcast(heads), ALU.mult))
                        elif step == S_OUT + 1:
                            dve.wait_ge(S["gd_pe"], e_pe + 26)
                            sig(dve.scalar_tensor_tensor(kbT[:, :, :], bank[6][:, 0:3 * P].rearrange(pc, a=3),
                                                         hgain[:, 4:5], gzT[:, :, b * P:(b + 1) * P],
                                                         ALU.mult, ALU.mult))
                        elif step == S_OUT + 2:
                            dve.wait_ge(S["gd_act"], e_act + 12)
                            sl = (slice(None), slice(3, 6), slice(b * P, (b + 1) * P))
                            sig(dve.tensor_tensor(XL[sl], kbT[:, :, :], XH[sl].bitcast(F32), ALU.subtract))

                    def attention(b, slot):
                        if slot < JOBS:
                            j, n = slot, JOBS * b + slot
                            w = P * (b + 1) if j < H_A else NM
                            t = at[n % 2]
                            m = mxs[:, n % 2, 0:1]
                            dve.wait_ge(S["jt_done"], n + 1)
                            if j < H_A:
                                near = min(w, 256)
                                chain.step(dve.tensor_tensor(t[:, w - near:w], t[:, w - near:w],
                                                             strips[:, j, 256 - near:256], ALU.add))
                                chain.join()
                                mask = unsel[b][:, :] if b else const("causal")
                                chain.step(dve.tensor_tensor_reduce(out=t[:, 0:w], in0=t[:, 0:w], in1=mask,
                                                                    scale=1.0, scalar=GONE, op0=ALU.add,
                                                                    op1=ALU.max, accum_out=m))
                            else:
                                chain.step(dve.tensor_reduce(m, t[:, 0:w], AX.X, ALU.max))
                            chain.join()
                            dve.tensor_scalar(mxs[:, n % 2, 1:2], m, -1.0, None, ALU.mult).then_inc(S["jm_done"], 1)
                        if 1 <= slot <= JOBS:
                            j = slot - 1
                            n = JOBS * b + j
                            w = P * (b + 1) if j < H_A else NM
                            dve.wait_ge(S["jtr_done"], n + 1)
                            if n >= 2:
                                dve.wait_ge(S["jv_done"], n - 1)
                            dve.tensor_copy(pT[n % 2][:, 0:w], bank[2 + n % 2][:, 0:w]).then_inc(S["jp_done"], 1)
                        if slot - 2 in (H_A - 1, JOBS - 1):
                            ph = int(slot - 2 == JOBS - 1)
                            c0, c1 = (6, 8) if ph else (0, 3)
                            j0, nh = (H_A, H_M) if ph else (0, H_A)
                            n = JOBS * b + slot - 2
                            dve.wait_ge(S["je_done"], n + 1)
                            chain.step(dve.reciprocal(rrec[:, j0:j0 + nh], rsum[:, j0:j0 + nh]))
                            chain.join()
                            dve.wait_ge(S["jv_done"], n + 1)
                            r = rrec[:, j0:j0 + nh].unsqueeze(2).to_broadcast([P, nh, DH])
                            dve.tensor_tensor(oA[:, 0:nh * DH].rearrange("p (h d) -> p h d", h=nh),
                                              bank[4][:, 0:nh * DH].rearrange("p (h d) -> p h d", h=nh), r,
                                              ALU.mult).then_inc(S["o_ev"], 1)
                            dve.wait_ge(S["o_hi"], 2 * b + ph + 1)
                            sl = (slice(None), slice(c0, c1), slice(b * P, (b + 1) * P))
                            dve.tensor_tensor(XL[sl], bank[4][:, 0:P * (c1 - c0)].rearrange("p (c t) -> p c t", t=P),
                                              XH[sl].bitcast(F32), ALU.subtract).then_inc(S["o_lo"], 1)

                    dve.sem_inc(S["w_lo"], 2)
                    dve.sem_inc(S["u_free"], 2)
                    dve.sem_inc(S["g_free"], 2)
                    dve.sem_inc(S["x_up"], 4)
                    ffn(0)
                    dve.wait_ge(S["r_done"], 2)
                    rounds = selection()
                    gcols = {"dq": 0, "dk": 1, "mq": 2, "mk": 3}
                    for gi in range(N_GROUPS):
                        if copied(gi)[0] == "ev_dve":
                            evac(gi)
                        if gi - 1 in GNORM_AT:
                            for i in range(2):
                                n = 2 * GNORM_AT.index(gi - 1) + i
                                norm_apply(N_NORM_A + n, (gqT if n < 3 else gkT)[:, n % 3, :], T,
                                           DH ** -0.5 if n < 3 else 1.0)
                        if gi - 1 in NORM_OF:
                            g = GROUPS[gi - 1]
                            name, c = g["name"], g["c"]
                            ap = {"dq": dqT, "dk": dkT, "mq": mqT, "mk": mkT}[name][:, c, :]
                            norm_apply(NORM_OF[gi - 1], ap, NM if name == "mk" else T,
                                       hgain[:, gcols[name]:gcols[name] + 1])
                        hook(gi)
                        if GATE_GROUP < gi < FIRST_CONV:
                            for _ in range(3):
                                next(rounds, None)
                        if FIRST_CONV <= gi < FIRST_CONV + 9:
                            conv(gi - FIRST_CONV)
                        u = GROUPS[gi]["unit"]
                        if LAST_OF_UNIT[u] == gi:
                            split_lo(u + 2, u % 2, LO_DVE)
                    for b in range(NB):
                        dve.wait_ge(S["v_t"], b + 1)
                        dve.tensor_tensor(gvN[:, b, :].rearrange("p (h d) -> p h d", h=H_B),
                                          bank[b % 2][:, 0:WB].rearrange("p (h d) -> p h d", h=H_B),
                                          beta[:, b, :].unsqueeze(2).to_broadcast([P, H_B, DH]), ALU.mult
                                          ).then_inc(S["v_done"], 1)
                    dve.wait_ge(S["nq_done"], N_NORM_A + 6)
                    dve.wait_ge(S["strip_in"], 16)
                    for b in range(NB):
                        for step in range(N_STEPS):
                            gdn(b, step)
                            if step in JOB_SLOT:
                                attention(b, JOB_SLOT[step])
                    for c in range(KD):
                        dve.wait_ge(S["dn_done"], KD + c + 1)
                        dve.tensor_tensor(xT[:, c, :], bank[4 + c % 4][:, :], xT[:, c, :], ALU.add
                                          ).then_inc(S["x_up"], 1)
                        if c % 2:
                            split_lo(U_MIX + 18 + c // 2, (c // 2) % 2)
                    for k in range(KD):
                        lo_of_x(2, k, slice(k, k + 1), KD + k + 1)
                    ffn(1)

            first = min(S[n].num for n in SEMAPHORES)
            nc.all_engine_barrier(sems_to_clear=range(first, first + len(SEMAPHORES)))

        fin = [ctx.enter_context(nc.semaphore(n)) for n in ("fin_t", "fin_cp", "fin_out")]
        with nc.Block() as block:
            @block.tensor
            def _(pe):
                for n in range(2 * NB):
                    b, half = divmod(n, 2)
                    if n >= 2:
                        pe.wait_ge(fin[1], n - 1)
                    for c in range(4):
                        mm = pe.transpose(bank[n % 2][:, c * P:(c + 1) * P],
                                          xT[:, 4 * half + c, b * P:(b + 1) * P], const("ident"))
                    mm.then_inc(fin[0], 1)

            @block.vector
            def _(dve):
                for n in range(2 * NB):
                    b, half = divmod(n, 2)
                    dve.wait_ge(fin[0], n + 1)
                    dve.tensor_copy(xnat[:, b, 512 * half:512 * half + 512], bank[n % 2][:, :]
                                    ).then_inc(fin[1], 1)

            @block.sync
            def _(sp):
                for b in range(NB):
                    sp.wait_ge(fin[1], 2 * b + 2)
                    sp.dma_start(out[0, b * P:(b + 1) * P, :], xnat[:, b, :]).then_inc(fin[2], 16)
                sp.wait_ge(fin[2], 16 * NB)


INPUTS = ["x", "mem", "ffn1_norm", "ffn1_w_gate", "ffn1_w_up", "ffn1_w_down", "mix_norm", "w_in",
          "dsa_q_norm", "dsa_k_norm", "rel_bias", "gdn_conv", "gdn_A_log", "gdn_dt_bias",
          "gdn_out_norm", "mem_norm", "w_mem_kv", "mem_q_norm", "mem_k_norm", "w_out",
          "ffn2_norm", "ffn2_w_gate", "ffn2_w_up", "ffn2_w_down"]


def kernel(**inputs):
    import concourse.bacc as bacc
    from concourse.bass_utils import run_bass_kernel_spmd

    nc = bacc.Bacc("TRN2", target_bir_lowering=False, num_devices=1)
    arrays = {f"in_{n}": np.ascontiguousarray(inputs[n]) for n in INPUTS}
    arrays["masks"] = np.ascontiguousarray(np.concatenate(list(CONSTS.values()), axis=1))
    arrays["hot_rows"] = bucket_rows()
    args = [nc.dram_tensor(n, a.shape, mybir.dt.from_np(a.dtype), kind="ExternalInput").ap()
            for n, a in arrays.items()]
    args.append(nc.dram_tensor("out", inputs["x"].shape, F32, kind="ExternalOutput").ap())
    hybrid_trunk(nc, *args)
    got = run_bass_kernel_spmd(nc, [arrays], core_ids=[0])
    return got.results[0]["out"]
```

```python
import math
from contextlib import ExitStack

import numpy as np

import concourse.bass as bass
from concourse import mybir

F32 = mybir.dt.float32
F32R = mybir.dt.float32r
ALU = mybir.AluOpType
ACT = mybir.ActivationFunctionType
AX = mybir.AxisListType

P = 128
EPS = 1e-6
T = 512
D = 1024
KD = D // P
NM = 256
DH = 64
FF = 2816
NF = FF // P
H_A, H_B, H_M = 6, 6, 4
H_I, D_I = 8, 32
TOPK = 128
NB = T // P
BUCKETS = 32
MAX_DIST = 128
CONV = 4
EXP_LN = "natural_log_exp_and_others"
SILU = "silu_and_others"
NEG = -1.0e30
GONE = -3.0e38
WA, WB, WM = H_A * DH, H_B * DH, H_M * DH
UNIT_COLS = 256
UNIT = KD * UNIT_COLS

O_DQ, O_DV = 0, 2 * WA
O_IQ = 3 * WA
O_IK = O_IQ + H_I * D_I
O_IW = O_IK + D_I
O_G = O_IW + H_I
O_GA = O_G + 4 * WB
O_MQ = O_GA + 2 * H_B
SM = H_I + 2 * H_B

PARTS = [(0, 8), (8, 15), (15, NF)]
GU_UNITS = 2 * (FF // UNIT_COLS)
DN_UNITS = len(PARTS) * (D // UNIT_COLS)
MIX_UNITS = 20
U_FFN = [0, GU_UNITS + DN_UNITS + MIX_UNITS]
U_MIX = GU_UNITS + DN_UNITS
LAYER_UNITS = 2 * (GU_UNITS + DN_UNITS) + MIX_UNITS

MIX_SRC = (["iq", (O_DQ, 256), "small", (O_DQ + 256, 256), (O_DQ + 512, 256), (O_DV, 256), (O_DV + 256, 128)]
           + [(O_MQ, 256)] + ["mk", "mv"] + [(O_G + 256 * i, 256) for i in range(6)]
           + [("out", i) for i in range(4)])
assert len(MIX_SRC) == MIX_UNITS
SMALL_UNIT = U_MIX + 2
SMALL_DMAS = P // D_I + 2


def unit_dmas(v):
    return SMALL_DMAS if v == SMALL_UNIT else 1


def landed_value(v):
    return 16 * sum(unit_dmas(w) for w in range(2, v + 1) if w % 2 == v % 2)


COL_DMAS = 4 + 2 * 5 + 3

GROUPS = []


def _groups():
    def g(name, u, kind, **kw):
        GROUPS.append(dict(name=name, unit=U_MIX + u, kind=kind, **kw))
    for c in range(2):
        g("iq", 0, "T", c=c, col=128 * c)
    for c in range(2):
        g("dq", 1, "T", c=c, col=128 * c, norm=True)
    g("ik", 2, "T", c=0, col=0)
    g("sm", 2, "S")
    for c in range(2, 6):
        g("dq" if c < 3 else "dk", 2 + c // 2, "T", c=c % 3, col=128 * (c % 2), norm=True)
    for b in range(NB):
        g("va", 5, "N", b=b, n=256)
    for b in range(NB):
        g("vb", 6, "N", b=b, n=128)
    for c in range(2):
        g("mq", 7, "T", c=c, col=128 * c, norm=True)
    for c in range(2):
        g("mk", 8, "M", c=c, col=128 * c, norm=True)
    for b in range(2):
        g("mv", 9, "V", b=b)
    for c in range(12):
        g(("gq", "gk", "gv", "gz")[c // 3], 10 + c // 2, "T", c=c % 3, col=128 * (c % 2))


_groups()
N_GROUPS = len(GROUPS)
GATE_GROUP = 5
FIRST_CONV = 24
NORM_OF = {i: sum(1 for x in GROUPS[:i] if x.get("norm")) for i, g in enumerate(GROUPS) if g.get("norm")}
N_NORM_A = sum(1 for g in GROUPS if g.get("norm"))
LAST_OF_UNIT = {g["unit"]: i for i, g in enumerate(GROUPS)}


def copied(gi):
    on_dve = GROUPS[gi]["kind"] in ("T", "S")
    return ("ev_dve" if on_dve else "ev_act",
            sum(1 for g in GROUPS[:gi + 1] if (g["kind"] in ("T", "S")) == on_dve))


LO_DVE = 3
GNORM_AT = [FIRST_CONV + 7 + j for j in range(3)]
SQ_STEPS = 2 * KD - 1

LEVELS = 6
(S_ROWS, S_DECAY, S_KK, S_QK, S_INV) = range(5)
S_LEVEL = 5
S_UW = S_LEVEL + 4 * (LEVELS - 1)
S_REC = S_UW + 1
S_OUT = S_REC + 4
N_STEPS = S_OUT + 3

JOBS = H_A + H_M
N_JOBS = JOBS * NB
SLOT_STEPS = [S_ROWS, S_DECAY, S_KK, S_QK, S_LEVEL + 5, S_LEVEL + 9, S_UW, S_REC, S_REC + 1, S_REC + 2, S_OUT]
JOB_SLOT = {step: n for n, step in enumerate(SLOT_STEPS)}
assert len(SLOT_STEPS) * NB >= N_JOBS + 4

N_PE, N_ACT, N_DVE, N_POOL = 15, 6, 14, 3


def level_count(b, j, par, first=1, levels=LEVELS - 1):
    return 2 * (levels * b + j - first) + par + 1


def t5_bucket():
    n = np.arange(0, T)
    exact = BUCKETS // 2
    nf = np.maximum(n, 1).astype(np.float32)
    large = exact + (np.log(nf / np.float32(exact)) / np.float32(math.log(MAX_DIST / exact))
                     * np.float32(BUCKETS - exact)).astype(np.int32)
    return np.where(n < exact, n, np.minimum(large, BUCKETS - 1))


def constants():
    p = np.arange(P)[:, None]
    c = np.arange(P)[None, :]
    c64 = np.arange(DH)[None, :]
    f = {}
    f["ident"] = (p == c)
    f["ones"] = np.ones((P, P))
    f["same64"] = (p // 64 == c // 64)
    f["prefix"] = (p // 64 == c // 64) & (p <= c)
    f["suffix"] = (p // 64 == c // 64) & (p > c)
    f["causal"] = np.where(c > p, NEG, 0.0)
    f["upper64"] = (p % 64) <= c64
    for j in range(LEVELS):
        m = 1 << j
        f[f"level{j}"] = (p // (2 * m) == c // (2 * m)) & (p % (2 * m) < m) & (c % (2 * m) >= m)
    sel = np.zeros((P, 3 * P))
    for pair in range(3):
        for m in range(P):
            sel[2 * pair + m // 64, pair * P + m] = 1.0
    f["pairsel"] = sel
    f["eps"] = np.full((P, 1), EPS)
    f["one"] = np.ones((P, 1))
    f["quarter"] = (p // D_I == np.arange(4)[None, :])
    f["half"] = (p // DH == np.arange(2)[None, :])
    f["zero"] = np.zeros((P, 1))
    return {k: np.ascontiguousarray(v, dtype=np.float32) for k, v in f.items()}


def bucket_rows():
    hot = np.zeros((BUCKETS, 384), np.float32)
    bucket = t5_bucket()
    for i in range(384):
        hot[bucket[max(255 - i, 0)], i] += 1.0
        hot[BUCKETS - 1, i] -= 1.0
    return hot


CONSTS = constants()
CONST_AT, _at = {}, 0
for _k, _v in CONSTS.items():
    CONST_AT[_k] = (_at, _v.shape[1])
    _at += _v.shape[1]
N_CONST = _at


class Chain:

    def __init__(self, eng, sem):
        self.eng, self.sem, self.n = eng, sem, 0

    def step(self, ins):
        ins.then_inc(self.sem, 1)
        self.n += 1

    def join(self):
        self.eng.wait_ge(self.sem, self.n)


def bcast(ap, axis, n):
    shape = list(ap.shape)
    return ap.unsqueeze(axis).to_broadcast(shape[:axis] + [n] + shape[axis:])


SEMAPHORES = """
landed0 landed1 w_hi w_lo w_used
sq_done ss_done r_done xh_done xl_done x_up w_lo_pool
gate_done up_done gs_done gr_done g_free u_free hh_done hl_done dn_done
act_chain dve_chain pool_chain
cols_in mem_in strip_in
pj_done ev_act ev_dve sc_done relu_done acc_done
mem_r mem_n mem_t mem_hi mem_lo
nq_sq nq_ss nq_r nq_done conv_done silu_done
v_t v_done sp_e sp_b g_ready gc_ps gc_ready row_ps row_ready
gd_pe gd_act gd_dve gd_pool
iv_xt0 iv_t iv_x0 iv_bt iv_yp iv_y iv_xp iv_xtp iv_xu iv_xtu
sm_t jq_done jl_done jt_done jm_done je_done jtr_done jp_done jv_done
o_ev o_t o_hi o_lo
""".split()


def hybrid_trunk(nc, x, mem, ffn1_norm, ffn1_w_gate, ffn1_w_up, ffn1_w_down, mix_norm, w_in,
                 dsa_q_norm, dsa_k_norm, rel_bias, gdn_conv, gdn_A_log, gdn_dt_bias,
                 gdn_out_norm, mem_norm, w_mem_kv, mem_q_norm, mem_k_norm, w_out,
                 ffn2_norm, ffn2_w_gate, ffn2_w_up, ffn2_w_down, consts, hot_rows, out):
    depth = w_in.shape[0]
    ffn_w = [(ffn1_w_gate, ffn1_w_up, ffn1_w_down), (ffn2_w_gate, ffn2_w_up, ffn2_w_down)]
    norm_w = [ffn1_norm, mix_norm, ffn2_norm]

    with ExitStack() as ctx:
        ctx.enter_context(nc.allow_non_contiguous_dma("gains and other small columns"))

        def sb(name, shape, dt=F32, stack=ctx):
            return stack.enter_context(nc.sbuf_tensor(name, shape, dt))

        xT = sb("xT", [P, KD, T])
        XH = sb("XH", [P, KD, T], F32R)
        XL = sb("XL", [P, KD, T], F32R)
        raw = [sb(f"raw{i}", [P, KD, UNIT_COLS]) for i in range(2)]
        wh = [sb(f"wh{i}", [P, KD, UNIT_COLS], F32R) for i in range(2)]
        wl = [sb(f"wl{i}", [P, KD, UNIT_COLS], F32R) for i in range(2)]
        cst = sb("cst", [P, N_CONST])

        def const(name):
            a, n = CONST_AT[name]
            return cst[:, a:a + n]

        eps, one, zero = const("eps"), const("one"), const("zero")
        far = sb("far", [P, H_A])
        gain = sb("gain", [P, 4, KD])
        hgain = sb("hgain", [P, 5])
        convw = sb("convw", [P, CONV, 9])
        gdnp = sb("gdnp", [P, 2, H_B])

        ffn_mem = ExitStack()
        HH = sb("HH", [P, NF, T], F32R, ffn_mem)
        HL = sb("HL", [P, NF, T], F32R, ffn_mem)
        sg = [sb(f"sg{i}", [P, T], F32, ffn_mem) for i in range(2)]
        hf = [sb(f"hf{i}", [P, T], F32, ffn_mem) for i in range(2)]
        rF = sb("rF", [P, T], F32, ffn_mem)
        ffn_mem.close()
        sqt, ssum = sg
        io_mem = ExitStack()
        xnat = sb("xnat", [P, NB, D], F32, io_mem)
        hot = sb("hot", [BUCKETS, 384], F32, io_mem)
        relb = sb("relb", [BUCKETS, H_A], F32, io_mem)
        rowsb = sb("rowsb", [H_A, 384], F32, io_mem)
        io_mem.close()
        dqT = sb("dqT", [P, 3, T])
        dkT = sb("dkT", [P, 3, T])
        dvN = sb("dvN", [P, NB, WA])
        mqT = sb("mqT", [P, 2, T])
        mkT = sb("mkT", [P, 2, NM])
        mvN = sb("mvN", [P, 2, WM])
        gqT = sb("gqT", [P, 3, T])
        gkT = sb("gkT", [P, 3, T])
        gzT = sb("gzT", [P, 3, T])
        gvN = sb("gvN", [P, NB, WB])
        unsel = [None] + [sb(f"unsel{b}", [P, P * (b + 1)]) for b in range(1, NB)]
        sm = sb("sm", [P, NB, SM])
        wI = sb("wI", [P, NB, H_I])
        gcol = sb("gcol", [P, 8, NB, H_B])
        beta, gdec, gcum, bg, kdec, tmpa, tmpb, tmpc = (gcol[:, i] for i in range(8))
        rowb = sb("rowb", [H_B, T])
        rowg = sb("rowg", [H_B, T])
        m8 = sb("m8", [P, 8])
        mxs = sb("mxs", [P, 2, 2])
        rsum = sb("rsum", [P, JOBS])
        rrec = sb("rrec", [P, JOBS])
        memr = sb("memr", [P, 2])
        oss = sb("oss", [P, H_B])
        rcol = sb("rcol", [P, NB])

        t_mem = ExitStack()
        rM = sb("rM", [P, T], F32, t_mem)
        acc = [None] + [sb(f"acc{b}", [P, P * (b + 1)], F32, t_mem) for b in range(1, NB)]
        wrk = sb("wrk", [P, T], F32, t_mem)
        with ExitStack() as early:
            smT = sb("smT", [SM, T], F32, early)
        MH = sb("MH", [P, KD, NM], F32R, t_mem)
        with ExitStack() as early:
            ikz = sb("ikz", [P, 4, T], F32, early)
        ML = sb("ML", [P, KD, NM], F32R, t_mem)
        nsq = [sb(f"nsq{i}", [P, T], F32, t_mem) for i in range(2)]
        nrr = nsq
        idx_mem = ExitStack()
        iqT = sb("iqT", [P, 2, T], F32, idx_mem)
        rl = [sb(f"rl{i}", [P, T], F32, idx_mem) for i in range(2)]
        idx_mem.close()
        tok_mem = ExitStack()
        memN = sb("memN", [P, 2, D], F32, tok_mem)
        tok_mem.close()
        cv = [sb(f"cv{i}", [P, CONV - 1 + T], F32, t_mem) for i in range(2)]
        gvT = sb("gvT", [P, 3, T], F32, t_mem)
        t_mem.close()

        a_mem = ExitStack()

        def ab(name, shape):
            return sb(name, shape, F32, a_mem)
        at = [ab(f"at{i}", [P, T]) for i in range(2)]
        pT = [ab(f"pT{i}", [P, T]) for i in range(2)]
        oA = ab("oA", [P, WA])
        qz = [ab(f"qz{i}", [P, P]) for i in range(2)]
        EGr = ab("EGr", [P, 3, P])
        with ExitStack() as early:
            TG = sb("TG", [P, 2, 3, DH], F32, early)
            DT = sb("DT", [P, 2, 3, DH], F32, early)
        BT = ab("BT", [P, 2, 3, P])
        with ExitStack() as early:
            kbT = sb("kbT", [P, 3, P], F32, early)
            oG = sb("oG", [P, H_B, DH], F32, early)
        Y = ab("Y", [P, 2, 3, P])
        LT = ab("LT", [P, 2, 3, DH])
        AT = ab("AT", [P, 2, 3, DH])
        X = ab("X", [P, 2, 3, P])
        XT = ab("XT", [P, 2, 3, P])
        with ExitStack() as early:
            kbg = sb("kbg", [P, H_B, DH], F32, early)
        WT = ab("WT", [P, 3, P])
        kdc = ab("kdc", [P, H_B, DH])
        U = ab("U", [P, H_B, DH])
        Sbd = ab("Sbd", [P, 3, P])
        Sdec = ab("Sdec", [P, 3, P])
        strips = ab("strips", [P, H_A, 256])
        a_mem.close()

        bank = [ctx.enter_context(nc.psum_tensor(f"bank{i}", [P, T], F32)) for i in range(8)]
        strip_dram = nc.dram_tensor("bias_rows", [H_A, P, 384], F32).ap()

        S = {n: ctx.enter_context(nc.semaphore(n)) for n in SEMAPHORES}
        setup = [ctx.enter_context(nc.semaphore(f"setup_{n}"))
                 for n in ("cst", "x", "w", "pe", "cp", "rows", "hi", "lo", "out", "cols", "xh", "sq")]
        landed = [S["landed0"], S["landed1"]]

        def unit_src(v, L):
            if v in (0, 1):
                return [(ffn_w[0][v][L].rearrange("(k p) f -> p k f", p=P)[:, :, 0:UNIT_COLS], raw[v][:, :, :])]
            m = v - U_MIX
            dst = raw[v % 2]
            w = w_in[L].rearrange("(k p) n -> p k n", p=P)
            src = MIX_SRC[m]
            if src == "iq":
                return [(w[:, :, O_IQ:O_IQ + 256], dst[:, :, :])]
            if src == "small":
                reps = [(w[:, :, O_IK:O_IK + D_I], dst[:, :, D_I * r:D_I * (r + 1)]) for r in range(P // D_I)]
                return reps + [(w[:, :, O_IW:O_IW + H_I], dst[:, :, P:P + H_I]),
                               (w[:, :, O_GA:O_GA + 2 * H_B], dst[:, :, P + H_I:P + SM])]
            if src in ("mk", "mv"):
                kv = w_mem_kv[L].rearrange("(k p) n -> p k n", p=P)
                return [(kv[:, :, WM * (src == "mv"):WM * (1 + (src == "mv"))], dst[:, :, :])]
            if src[0] == "out":
                wo = w_out[L].rearrange("(k p) n -> p k n", p=P)
                return [(wo[:, :, 256 * src[1]:256 * src[1] + 256], dst[:, :, :])]
            return [(w[:, :, src[0]:src[0] + src[1]], dst[:, :, 0:src[1]])]

        def load_columns(queue, layer, done):
            for i, g in enumerate([ffn1_norm, mix_norm, ffn2_norm, mem_norm]):
                queue.dma_start(gain[:, i, :], g[layer].rearrange("(k p) -> p k", p=P)).then_inc(done, 16)
            for i, g in enumerate([dsa_q_norm, dsa_k_norm, mem_q_norm, mem_k_norm, gdn_out_norm]):
                for half in range(2):
                    queue.dma_start(hgain[half * DH:(half + 1) * DH, i:i + 1],
                                    g[layer].rearrange("(p o) -> p o", o=1)).then_inc(done, 16)
            queue.dma_start(convw[:, :, :], gdn_conv[layer].rearrange("w (c p) -> p w c", p=P)
                            ).then_inc(done, 16)
            queue.dma_start(gdnp[:, 0, :], gdn_A_log[layer].partition_broadcast(P)).then_inc(done, 16)
            queue.dma_start(gdnp[:, 1, :], gdn_dt_bias[layer].partition_broadcast(P)).then_inc(done, 16)

        def add_squares(pool, updated, updated_from, done, done_from):
            for k in range(KD):
                pool.wait_ge(updated, updated_from + k + 1)
                if k >= 2:
                    pool.wait_ge(done, done_from + 2 * k - 1)
                pool.tensor_tensor((sqt if k else ssum)[:, :], xT[:, k, :], xT[:, k, :], ALU.mult
                                   ).then_inc(done, 1)
                if k:
                    pool.wait_ge(done, done_from + 2 * k)
                    pool.tensor_tensor(ssum[:, :], ssum[:, :], sqt[:, :], ALU.add).then_inc(done, 1)
        (s_cst, s_x, s_w, s_pe, s_cp, s_rows, s_hi, s_lo, s_out, s_cols, s_xh, s_sq) = setup
        with nc.Block() as block:
            @block.sync
            def _(sp):
                for b in range(NB):
                    sp.dma_start(xnat[:, b, :], x[0, b * P:(b + 1) * P, :]).then_inc(s_x, 16)
                for v in range(2):
                    for src, dst in unit_src(v, 0):
                        sp.dma_start(dst, src).then_inc(s_w, 16)
                sp.wait_ge(s_rows, 1)
                sp.dma_start(strip_dram, rowsb[:, None, :].to_broadcast([H_A, P, 384])).then_inc(s_out, 16)

            @block.gpsimd
            def _(pool):
                pool.dma_start(cst[:, :], consts).then_inc(s_cst, 16)
                pool.dma_start(hot[:, :], hot_rows).then_inc(s_cst, 16)
                pool.dma_start(relb[:, :], rel_bias).then_inc(s_cst, 16)
                pool.dma_start(far[:, :], rel_bias[BUCKETS - 1, :].partition_broadcast(P)).then_inc(s_cst, 16)
                add_squares(pool, s_cp, 0, s_sq, 0)

            @block.tensor
            def _(pe):
                pe.wait_ge(s_cst, 64)
                pe.wait_ge(s_x, 16 * NB)
                for k in range(KD):
                    if k >= 2:
                        pe.wait_ge(s_cp, k - 1)
                    for b in range(NB):
                        mm = pe.transpose(bank[k % 2][:, b * P:(b + 1) * P], xnat[:, b, k * P:(k + 1) * P],
                                          const("ident"))
                    mm.then_inc(s_pe, 1)
                pe.matmul(bank[2][0:H_A, 0:384], relb[:, :], hot[:, :], start=True, stop=True).then_inc(s_pe, 1)

            @block.scalar
            def _(act):
                load_columns(act, 0, s_cols)
                act.wait_ge(s_cols, 16 * COL_DMAS)
                for k in range(KD):
                    act.wait_ge(s_cp, k + 1)
                    act.activation(XH[:, k, :], xT[:, k, :], ACT.Copy, scale=gain[:, 0, k:k + 1]).then_inc(s_xh, 1)
                act.wait_ge(s_w, 32)
                for v in range(2):
                    act.activation(wh[v][:, :, :], raw[v][:, :, :], ACT.Copy).then_inc(s_hi, 1)

            @block.vector
            def _(dve):
                for k in range(KD):
                    dve.wait_ge(s_pe, k + 1)
                    dve.tensor_copy(xT[:, k, :], bank[k % 2][:, :]).then_inc(s_cp, 1)
                dve.wait_ge(s_pe, KD + 1)
                dve.tensor_copy(rowsb[:, :], bank[2][0:H_A, 0:384]).then_inc(s_rows, 1)
                for k in range(KD):
                    dve.wait_ge(s_xh, k + 1)
                    dve.scalar_tensor_tensor(XL[:, k, :], xT[:, k, :], gain[:, 0, k:k + 1],
                                             XH[:, k, :].bitcast(F32), ALU.mult, ALU.subtract)
                for v in range(2):
                    dve.wait_ge(s_hi, v + 1)
                    dve.tensor_tensor(wl[v][:, :, :], raw[v][:, :, :], wh[v][:, :, :].bitcast(F32),
                                      ALU.subtract).then_inc(s_lo, 1)

        with nc.Fori(0, depth) as L:
            with nc.Block() as block:

                @block.sync
                def _(sp):
                    def load(v, pairs, slot):
                        for src, dst in pairs:
                            sp.dma_start(dst, src).then_inc(landed[slot], 16)

                    def ffn_units(q):
                        w_gate, w_up, w_down = ffn_w[q]
                        ub = U_FFN[q]
                        gu = [w[L].rearrange("(k p) (c n) -> p k c n", p=P, n=UNIT_COLS) for w in (w_gate, w_up)]
                        dn = w_down[L].rearrange("(f p) (c n) -> p f c n", p=P, n=UNIT_COLS)
                        with sp.Fori(1 - q, NF // 2) as i:
                            for j in range(2):
                                sp.wait_ge(S["w_lo"], ub + 2 * i + j - 1)
                                sp.dma_start(raw[j][:, :, :], gu[j][:, :, i, :]).then_inc(landed[j], 16)
                        with sp.Fori(0, 2) as i:
                            for r in range(DN_UNITS // 2):
                                f0, f1 = PARTS[r % 3]
                                sp.wait_ge(S["w_lo"], ub + GU_UNITS + 6 * i + (r - 1))
                                sp.dma_start(raw[r % 2][:, 0:f1 - f0, :],
                                             dn[:, f0:f1, 2 * i + r // 3, :]).then_inc(landed[r % 2], 16)

                    ffn_units(0)
                    for v in range(U_MIX, U_MIX + MIX_UNITS):
                        sp.wait_ge(S["w_lo"], v - 1)
                        if U_MIX + 2 <= v - 2 < U_MIX + 18:
                            sp.wait_ge(S["w_lo_pool"], v - 2 - U_MIX - 1)
                        load(v, unit_src(v, L), v % 2)
                        if v == U_MIX + 17:
                            sp.wait_ge(S["v_done"], NB)
                            sp.wait_ge(S["nq_done"], N_NORM_A + 6)
                            sp.wait_ge(s_out, 16)
                            sp.dma_start(strips[:, :, :], bass.AP(
                                tensor=strip_dram.tensor, offset=strip_dram.offset + P - 1,
                                ap=[[384 - 1, P], [P * 384, H_A], [1, 256]])).then_inc(S["strip_in"], 16)
                        if v == U_MIX + 4:
                            sp.wait_ge(S["sc_done"], 24)
                            sp.wait_ge(S["acc_done"], 24)
                            sp.dma_start(memN[:, :, :], mem[0].rearrange("(m p) d -> p m d", p=P)
                                         ).then_inc(S["mem_in"], 16)
                    ffn_units(1)
                    nxt = (L + 1) % depth
                    for v in range(2):
                        sp.wait_ge(S["w_lo"], LAYER_UNITS + v - 1)
                        load(v, unit_src(v, nxt), v)

                @block.gpsimd
                def _(pool):
                    def gate_norm(q):
                        pool.wait_ge(S["r_done"], 2 * q + 1)
                        with pool.Fori(0, NF // 2) as i:
                            for fs in range(2):
                                pool.wait_ge(S["gs_done"], NF * q + 2 * i + (fs + 1))
                                pool.tensor_tensor(sg[fs][:, :], sg[fs][:, :], rF[:, :], ALU.mult
                                                   ).then_inc(S["gr_done"], 1)

                    gate_norm(0)
                    add_squares(pool, S["x_up"], 4, S["sq_done"], 0)
                    for gi in range(N_GROUPS):
                        if gi == FIRST_CONV - 4:
                            pool.wait_ge(S["acc_done"], 24)
                            pool.wait_ge(S["mem_lo"], 4)
                            for i in range(2):
                                pool.memset(cv[i][:, 0:CONV - 1], 0.0).then_inc(S["pool_chain"], 1)
                        u = GROUPS[gi]["unit"]
                        if LAST_OF_UNIT[u] == gi:
                            slot = u % 2
                            pool.wait_ge(S["w_hi"], u + 2 - 1)
                            pool.tensor_tensor(wl[slot][:, LO_DVE:, :], raw[slot][:, LO_DVE:, :],
                                               wh[slot][:, LO_DVE:, :].bitcast(F32), ALU.subtract
                                               ).then_inc(S["w_lo_pool"], 1)
                    pool.wait_ge(S["v_done"], NB)
                    pool.wait_ge(S["nq_done"], N_NORM_A + 6)
                    pool.memset(Sbd[:, :, :], 0.0).then_inc(S["pool_chain"], 1)

                    def mask_q(n):
                        if n < N_JOBS:
                            b, j = divmod(n, JOBS)
                            tok = slice(b * P, b * P + P)
                            q = dqT[:, j // 2, tok] if j < H_A else mqT[:, (j - H_A) // 2, tok]
                            if n >= 2:
                                pool.wait_ge(S["jl_done"], n - 1)
                            pool.tensor_tensor(qz[n % 2][:, :], q,
                                               const("half")[:, j % 2:j % 2 + 1].to_broadcast([P, P]), ALU.mult
                                               ).then_inc(S["jq_done"], 1)

                    def gdn(b, step):
                        e_pe, e_act, e_dve = b * N_PE, b * N_ACT, b * N_DVE
                        if step == S_QK:
                            tok = slice(b * P, (b + 1) * P)
                            pool.wait_ge(S["gd_pe"], e_pe + 5)
                            pool.wait_ge(S["gd_act"], e_act + 1)
                            pool.tensor_tensor(gqT[:, :, tok], gqT[:, :, tok], EGr[:, :, :], ALU.mult
                                               ).then_inc(S["gd_pool"], 1)
                        elif S_LEVEL <= step < S_UW and (step - S_LEVEL) % 4 < 2:
                            j, par = (step - S_LEVEL) // 4 + 1, (step - S_LEVEL) % 4
                            n = level_count(b, j, par)
                            if step == S_LEVEL:
                                pool.wait_ge(S["gd_dve"], e_dve + 6)
                            if n > 2:
                                pool.wait_ge(S["iv_yp"], n - 2)
                            pool.tensor_tensor(BT[:, par].rearrange("p a (h c) -> p a h c", h=2),
                                               bcast(LT[:, par], 2, 2),
                                               bcast(const(f"level{j}").rearrange("p (h c) -> p h c", h=2), 1, 3),
                                               ALU.mult).then_inc(S["iv_bt"], 1)
                        elif step == S_UW or step == S_REC + 1:
                            ch = int(step > S_UW)
                            if ch == 0 and b == 0:
                                pool.wait_ge(S["pool_chain"], 3)
                            else:
                                pool.wait_ge(S["gd_dve"], e_dve + 8 if ch else e_dve - N_DVE + 10)
                            last = EGr[:, :, DH * ch + DH - 1:DH * ch + DH]
                            pool.tensor_tensor(Sdec[:, :, :], Sbd[:, :, :], last.to_broadcast([P, 3, P]),
                                               ALU.mult).then_inc(S["gd_pool"], 1)

                    for n in range(2):
                        mask_q(n)
                    for b in range(NB):
                        for step in range(N_STEPS):
                            gdn(b, step)
                            if step in JOB_SLOT:
                                mask_q(len(SLOT_STEPS) * b + JOB_SLOT[step] + 2)
                    add_squares(pool, S["x_up"], 4 + KD, S["sq_done"], SQ_STEPS)
                    gate_norm(1)
                    add_squares(pool, S["x_up"], 4 + 2 * KD, S["sq_done"], 2 * SQ_STEPS)

                @block.tensor
                def _(pe):
                    def three(out_ap, wt, at_, first, last):
                        (a_hi, a_lo), (b_hi, b_lo) = wt, at_
                        pe.matmul(out_ap, a_hi, b_hi, start=first, stop=False)
                        pe.matmul(out_ap, a_hi, b_lo, start=False, stop=False)
                        return pe.matmul(out_ap, a_lo, b_hi, start=False, stop=last)

                    def sum_squares(p):
                        if p:
                            pe.wait_ge(S["sq_done"], SQ_STEPS * p)
                        mm = pe.matmul(bank[3][:, :], const("ones"), ssum[:, :], start=True, stop=True)
                        if p == 1:
                            for b in range(NB):
                                mm = pe.matmul(bank[7][:, b:b + 1], ssum[:, b * P:(b + 1) * P], one,
                                               start=True, stop=True)
                        mm.then_inc(S["ss_done"], 1)

                    def wait_copied(gi):
                        sem, n = copied(gi)
                        pe.wait_ge(S[sem], n)

                    def wait_split(u):
                        pe.wait_ge(S["w_lo"], u + 1)
                        if U_MIX + 2 <= u < U_MIX + 18:
                            pe.wait_ge(S["w_lo_pool"], u - U_MIX - 1)

                    def ffn(q):
                        p, ub = 2 * q, U_FFN[q]
                        sum_squares(p)
                        with pe.Fori(0, NF // 2) as i:
                            for j in range(2):
                                pe.wait_ge(S["w_lo"], ub + 2 * i + (j + 1))
                                for fs in range(2):
                                    pe.wait_ge(S["g_free" if j == 0 else "u_free"], NF * q + 2 * i + (fs + 1))
                                    if j and fs:
                                        pe.wait_ge(S["r_done"], p + 1)
                                    dst = bank[2 * j + fs]
                                    cols = slice(P * fs, P * fs + P)
                                    for k in range(KD):
                                        if j == 0 and fs == 0 and q:
                                            pe.wait_ge(S["xl_done"], KD * q + k + 1)
                                        mm = three(dst[:, :], (wh[j][:, k, cols], wl[j][:, k, cols]),
                                                   (XH[:, k, :], XL[:, k, :]), k == 0, k == KD - 1)
                                    mm.then_inc(S["gate_done" if j == 0 else "up_done"], 1)
                        with pe.Fori(0, 2) as i:
                            for r in range(DN_UNITS // 2):
                                dp, part = divmod(r, 3)
                                slot = r % 2
                                f0, f1 = PARTS[part]
                                pe.wait_ge(S["w_lo"], ub + GU_UNITS + 6 * i + (r + 1))
                                if dp == 0:
                                    pe.wait_ge(S["hl_done"], NF * q + f1)
                                for d in range(2):
                                    if part == 0:
                                        pe.wait_ge(S["x_up"], 2 * KD * q + 4 * i + (2 * dp + d + 1))
                                    cols = slice(P * d, P * d + P)
                                    for f in range(f0, f1):
                                        mm = three(bank[4 + 2 * dp + d][:, :],
                                                   (wh[slot][:, f - f0, cols], wl[slot][:, f - f0, cols]),
                                                   (HH[:, f, :], HL[:, f, :]), f == 0, f == NF - 1)
                                    if part == 2:
                                        mm.then_inc(S["dn_done"], 1)
                                if part < 2:
                                    mm.then_inc(S["w_used"], 1)

                    def group(gi):
                        g = GROUPS[gi]
                        slot = g["unit"] % 2
                        wait_split(g["unit"])
                        if gi >= 2:
                            wait_copied(gi - 2)
                        dst, kind = bank[gi % 2], g["kind"]
                        for k in range(KD):
                            first, last = k == 0, k == KD - 1
                            act_in = (XH[:, k, :], XL[:, k, :])
                            if kind == "S":
                                mm = three(dst[0:SM, :], (wh[slot][:, k, P:P + SM], wl[slot][:, k, P:P + SM]),
                                           act_in, first, last)
                                continue
                            if kind == "T":
                                if gi == 0:
                                    pe.wait_ge(S["xl_done"], k + 1)
                                cols = slice(g["col"], g["col"] + P)
                                mm = three(dst[:, :], (wh[slot][:, k, cols], wl[slot][:, k, cols]), act_in,
                                           first, last)
                            elif kind == "N":
                                tok = slice(g["b"] * P, g["b"] * P + P)
                                n = g["n"]
                                mm = three(dst[:, 0:n], (XH[:, k, tok], XL[:, k, tok]),
                                           (wh[slot][:, k, 0:n], wl[slot][:, k, 0:n]), first, last)
                            elif kind == "M":
                                cols = slice(g["col"], g["col"] + P)
                                mm = three(dst[:, 0:NM], (wh[slot][:, k, cols], wl[slot][:, k, cols]),
                                           (MH[:, k, :], ML[:, k, :]), first, last)
                            else:
                                tok = slice(g["b"] * P, g["b"] * P + P)
                                mm = three(dst[:, 0:WM], (MH[:, k, tok], ML[:, k, tok]),
                                           (wh[slot][:, k, :], wl[slot][:, k, :]), first, last)
                        mm.then_inc(S["pj_done"], 1)

                    def head_sums(nj, n):
                        pe.wait_ge(S["nq_sq"], nj + 1)
                        if nj >= 2:
                            pe.wait_ge(S["nq_r"], nj - 1)
                        pe.matmul(bank[2 + nj % 2][:, 0:n], const("same64"), nsq[nj % 2][:, 0:n],
                                  start=True, stop=True).then_inc(S["nq_ss"], 1)

                    def index_scores():
                        wait_copied(GATE_GROUP - 1)
                        for b in range(1, NB):
                            for h in range(H_I):
                                n = (b - 1) * H_I + h
                                if n == 2:
                                    wait_copied(GATE_GROUP)
                                    for c in range(NB):
                                        mm = pe.transpose(bank[6][:, c * SM:(c + 1) * SM],
                                                          smT[:, c * P:(c + 1) * P], const("ident")[0:SM, 0:SM])
                                    mm.then_inc(S["sm_t"], 1)
                                if n >= 2:
                                    pe.wait_ge(S["relu_done"], n - 1)
                                pe.matmul(bank[4 + n % 2][:, 0:P * (b + 1)], iqT[:, h // 4, b * P:(b + 1) * P],
                                          ikz[:, h % 4, 0:P * (b + 1)], start=True, stop=True
                                          ).then_inc(S["sc_done"], 1)

                    def memory_transposes(t):
                        if t == 0:
                            pe.wait_ge(S["mem_n"], 1)
                            pe.wait_ge(S["row_ready"], 1)
                        if t >= 2:
                            pe.wait_ge(S["mem_lo"], t - 1)
                        for k in range(2 * t, 2 * t + 2):
                            for m in range(2):
                                at0 = (k - 2 * t) * NM + m * P
                                mm = pe.transpose(bank[6 + t % 2][:, at0:at0 + P], memN[:, m, k * P:(k + 1) * P],
                                                  const("ident"))
                        mm.then_inc(S["mem_t"], 1)

                    def hook(gi):
                        if gi == GATE_GROUP:
                            index_scores()
                        if gi == 8:
                            pe.wait_ge(S["g_ready"], 1)
                            g24 = gdec.rearrange("p b h -> p (b h)")
                            pe.matmul(bank[7][:, 0:24], const("prefix"), g24, start=True, stop=True)
                            pe.matmul(bank[7][:, 32:56], const("suffix"), g24, start=True, stop=True
                                      ).then_inc(S["gc_ps"], 1)
                        if gi == 10:
                            pe.wait_ge(S["gc_ready"], 1)
                            for b in range(NB):
                                tok = slice(b * P, b * P + P)
                                pe.transpose(bank[6][0:H_B, tok], beta[:, b, :], const("ident"))
                                mm = pe.transpose(bank[7][0:H_B, tok], gcum[:, b, :], const("ident"))
                            mm.then_inc(S["row_ps"], 1)
                        if gi in (13, 15):
                            for t in range(gi - 13, gi - 11):
                                memory_transposes(t)
                        if gi == 19:
                            pe.wait_ge(S["mem_lo"], 4)

                    def gdn(b, step):
                        e_act, e_dve, e_pool = b * N_ACT, b * N_DVE, b * N_POOL
                        tok0 = b * P
                        heads = [(par, pair) for par in range(2) for pair in range(3)]
                        rows = [slice(0, DH), slice(DH, P)]

                        def sig(mm):
                            mm.then_inc(S["gd_pe"], 1)

                        if step == S_ROWS:
                            pe.wait_ge(S["row_ready"], 1)
                            if b:
                                pe.wait_ge(S["gd_dve"], e_dve - N_DVE + 13)
                            for pair in range(3):
                                s = const("pairsel")[0:H_B, pair * P:(pair + 1) * P]
                                pe.matmul(bank[5][:, pair * P:(pair + 1) * P], s, rowb[:, tok0:tok0 + P],
                                          start=True, stop=True)
                                mm = pe.matmul(bank[6][:, pair * P:(pair + 1) * P], s, rowg[:, tok0:tok0 + P],
                                               start=True, stop=True)
                            sig(mm)
                            pe.wait_ge(S["gd_dve"], e_dve + 1)
                            sig(pe.matmul(bank[7][:, 0:WB], const("suffix"), TG.rearrange("p a b c -> p (a b c)"),
                                          start=True, stop=True))
                        elif step == S_DECAY:
                            pe.wait_ge(S["gd_dve"], e_dve + 2)
                            for pair in range(3):
                                mm = pe.transpose(bank[5][:, pair * P:(pair + 1) * P],
                                                  gkT[:, pair, tok0:tok0 + P], const("ident"))
                            sig(mm)
                        elif step in (S_KK, S_QK):
                            if step == S_KK:
                                pe.wait_ge(S["gd_act"], e_act + 2)
                            else:
                                pe.wait_ge(S["gd_dve"], e_dve + 5)
                            for pair in range(3):
                                for par in range(2):
                                    for ch in range(2):
                                        toks = slice(tok0 + DH * ch, tok0 + DH * ch + DH)
                                        rhs = (kbT[rows[par], pair, DH * ch:DH * ch + DH] if step == S_KK
                                               else gqT[rows[par], pair, toks])
                                        mm = pe.matmul(bank[6 + par][rows[ch], pair * DH:(pair + 1) * DH],
                                                       gkT[rows[par], pair, toks], rhs, start=True, stop=True)
                            sig(mm)
                        elif step == S_INV:
                            for par in range(2):
                                pe.wait_ge(S["iv_xt0"], 2 * b + par + 1)
                                for pair in range(3):
                                    mm = pe.transpose(bank[6 + par][:, pair * P:(pair + 1) * P],
                                                      XT[:, par, pair, :], const("ident"))
                                mm.then_inc(S["iv_t"], 1)
                        elif step < S_UW:
                            j, part = divmod(step - S_LEVEL, 4)
                            j, second, par = j + 1, part // 2, part % 2
                            n = level_count(b, j, par)
                            if not second:
                                pe.wait_ge(S["iv_bt"], n)
                                if j == 1:
                                    pe.wait_ge(S["iv_x0"], 2 * b + par + 1)
                                else:
                                    pe.wait_ge(S["iv_xu"], level_count(b, j - 1, par, levels=LEVELS - 2))
                                if n > 1:
                                    pe.wait_ge(S["iv_y"], n - 1)
                                for pair in range(3):
                                    mm = pe.matmul(bank[5][:, pair * P:(pair + 1) * P], BT[:, par, pair, :],
                                                   X[:, par, pair, :], start=True, stop=True)
                                mm.then_inc(S["iv_yp"], 1)
                            else:
                                pe.wait_ge(S["iv_y"], n)
                                if j > 1:
                                    pe.wait_ge(S["iv_xtu"], n - 2)
                                if j < LEVELS - 1:
                                    nx = level_count(b, j, par, levels=LEVELS - 2)
                                    if nx > 1:
                                        pe.wait_ge(S["iv_xu"], nx - 1)
                                    for pair in range(3):
                                        mm = pe.matmul(bank[6][:, pair * P:(pair + 1) * P], XT[:, par, pair, :],
                                                       Y[:, par, pair, :], start=True, stop=True)
                                    mm.then_inc(S["iv_xp"], 1)
                                if n > 1:
                                    pe.wait_ge(S["iv_xtu"], n - 1)
                                if j == 1:
                                    pe.wait_ge(S["iv_x0"], 2 * b + 2)
                                for pair in range(3):
                                    mm = pe.matmul(bank[7][:, pair * P:(pair + 1) * P], Y[:, par, pair, :],
                                                   XT[:, par, pair, :], start=True, stop=True)
                                mm.then_inc(S["iv_xtp"], 1)
                        elif step == S_UW:
                            pe.wait_ge(S["iv_xtu"], level_count(b, LEVELS - 1, 1))
                            for par, pair in heads:
                                h = 2 * pair + par
                                pe.matmul(bank[5][:, h * DH:(h + 1) * DH], XT[:, par, pair, :],
                                          gvN[:, b, h * DH:(h + 1) * DH], start=True, stop=True)
                                mm = pe.matmul(bank[6][rows[par], pair * P:(pair + 1) * P], kbg[:, h, :],
                                               XT[:, par, pair, :], start=True, stop=True)
                            sig(mm)
                        elif step < S_OUT:
                            ch, second = divmod(step - S_REC, 2)
                            if not second:
                                pe.wait_ge(S["gd_act"], e_act + 3)
                                pe.wait_ge(S["gd_pool"], e_pool + 1)
                                if b or ch:
                                    pe.wait_ge(S["gd_dve"], e_dve + 8 if ch else e_dve - N_DVE + 10)
                                else:
                                    pe.wait_ge(S["pool_chain"], 3)
                                for pair in range(3):
                                    mm = pe.matmul(bank[6][rows[ch], pair * P:(pair + 1) * P],
                                                   WT[:, pair, rows[ch]], Sbd[:, pair, :], start=True, stop=True)
                                sig(mm)
                                for pair in range(3):
                                    mm = pe.matmul(bank[5][rows[ch], pair * P:(pair + 1) * P],
                                                   gqT[:, pair, tok0 + DH * ch:tok0 + DH * ch + DH],
                                                   Sbd[:, pair, :], start=(pair == 0), stop=False,
                                                   skip_group_check=True)
                                sig(mm)
                            else:
                                pe.wait_ge(S["gd_dve"], e_dve + 7 + 2 * ch)
                                for pair in range(3):
                                    mm = pe.matmul(bank[7][:, pair * P:(pair + 1) * P],
                                                   kdc[rows[ch], 2 * pair:2 * pair + 2, :],
                                                   U[rows[ch], 2 * pair:2 * pair + 2, :], start=True, stop=True)
                                sig(mm)
                                for pair in range(3):
                                    for par in range(2):
                                        h = 2 * pair + par
                                        mm = pe.matmul(bank[5][rows[ch], h * DH:(h + 1) * DH],
                                                       AT[rows[ch], par, pair, :], U[rows[ch], h, :],
                                                       start=False, stop=(h == H_B - 1), skip_group_check=True)
                                sig(mm)
                        elif step == S_OUT + 1:
                            pe.wait_ge(S["gd_dve"], e_dve + 12)
                            for pair in range(3):
                                mm = pe.transpose(bank[6][:, pair * P:(pair + 1) * P],
                                                  oG[:, 2 * pair:2 * pair + 2, :], const("ident"))
                            sig(mm)

                    def attention(slot):
                        n = slot - 4
                        if 0 <= n < N_JOBS and n % JOBS in (H_A - 1, JOBS - 1):
                            b, ph = n // JOBS, int(n % JOBS == JOBS - 1)
                            pe.wait_ge(S["o_ev"], 2 * b + ph + 1)
                            for c in range(2 if ph else 3):
                                mm = pe.transpose(bank[4][:, c * P:(c + 1) * P], oA[:, c * P:(c + 1) * P],
                                                  const("ident"))
                            mm.then_inc(S["o_t"], 1)
                        n = slot - 2
                        if 0 <= n < N_JOBS:
                            b, j = divmod(n, JOBS)
                            pe.wait_ge(S["je_done"], n + 1)
                            if n >= 2:
                                pe.wait_ge(S["jp_done"], n - 1)
                            for i in range(b + 1 if j < H_A else 2):
                                mm = pe.transpose(bank[2 + n % 2][:, i * P:(i + 1) * P],
                                                  at[n % 2][:, i * P:(i + 1) * P], const("ident"))
                            mm.then_inc(S["jtr_done"], 1)
                        n = slot
                        if n < N_JOBS:
                            b, j = divmod(n, JOBS)
                            if n >= 2:
                                pe.wait_ge(S["jt_done"], n - 1)
                            pe.wait_ge(S["jq_done"], n + 1)
                            w = P * (b + 1) if j < H_A else NM
                            k = dkT[:, j // 2, 0:w] if j < H_A else mkT[:, (j - H_A) // 2, :]
                            pe.matmul(bank[n % 2][:, 0:w], qz[n % 2][:, :], k, start=True, stop=True
                                      ).then_inc(S["jl_done"], 1)
                        n = slot - 3
                        if 0 <= n < N_JOBS:
                            b, j = divmod(n, JOBS)
                            pe.wait_ge(S["jp_done"], n + 1)
                            if j in (0, H_A) and n:
                                pe.wait_ge(S["o_lo"], 2 * b + (j == H_A))
                            nt = b + 1 if j < H_A else 2
                            at0 = DH * (j if j < H_A else j - H_A)
                            for i in range(nt):
                                v = (dvN[:, i, at0:at0 + DH] if j < H_A else mvN[:, i, at0:at0 + DH])
                                mm = pe.matmul(bank[4][:, at0:at0 + DH], pT[n % 2][:, i * P:(i + 1) * P], v,
                                               start=(i == 0), stop=(i == nt - 1))
                            mm.then_inc(S["jv_done"], 1)

                    ffn(0)
                    for gi in range(N_GROUPS):
                        group(gi)
                        if gi == 0:
                            sum_squares(1)
                        if gi - 1 in NORM_OF:
                            head_sums(NORM_OF[gi - 1], NM if GROUPS[gi - 1]["name"] == "mk" else T)
                        hook(gi)
                        if gi in GNORM_AT:
                            for i in range(2):
                                head_sums(N_NORM_A + 2 * GNORM_AT.index(gi) + i, T)
                    for b in range(NB):
                        pe.wait_ge(S["silu_done"], 3)
                        wait_copied(N_GROUPS - 1)
                        if b >= 2:
                            pe.wait_ge(S["v_done"], b - 1)
                        for pair in range(3):
                            mm = pe.transpose(bank[b % 2][:, pair * P:(pair + 1) * P],
                                              gvT[:, pair, b * P:(b + 1) * P], const("ident"))
                        mm.then_inc(S["v_t"], 1)
                    pe.wait_ge(S["v_done"], NB)
                    pe.wait_ge(S["nq_done"], N_NORM_A + 6)
                    for b in range(NB):
                        for step in range(N_STEPS):
                            gdn(b, step)
                            if step in JOB_SLOT:
                                attention(len(SLOT_STEPS) * b + JOB_SLOT[step])
                    pe.wait_ge(S["o_lo"], 2 * NB)
                    pe.wait_ge(S["gd_dve"], NB * N_DVE)
                    for c in range(KD):
                        u = U_MIX + 16 + c // 2
                        wait_split(u)
                        pe.wait_ge(S["x_up"], KD + c + 1)
                        cols = slice(P * (c % 2), P * (c % 2) + P)
                        for k in range(KD):
                            mm = three(bank[4 + c % 4][:, :], (wh[u % 2][:, k, cols], wl[u % 2][:, k, cols]),
                                       (XH[:, k, :], XL[:, k, :]), k == 0, k == KD - 1)
                        mm.then_inc(S["dn_done"], 1)
                    ffn(1)

                @block.scalar
                def _(act):
                    chain = Chain(act, S["act_chain"])

                    def split_hi(v, wait_landed, slot):
                        act.wait_ge(landed[slot], wait_landed)
                        act.activation(wh[slot][:, :, :], raw[slot][:, :, :], ACT.Copy).then_inc(S["w_hi"], 1)

                    def rsqrt(dst, src, scale):
                        chain.step(act.activation(dst, src, ACT.Ln, bias=eps[0:dst.shape[0], :], scale=scale))
                        chain.join()
                        return act.activation(dst, dst, ACT.Exp, scale=-0.5)

                    def hi_of_x(p, k, scale_at):
                        act.activation(XH[:, k, :], xT[:, k, :], ACT.Copy, scale=gain[:, p, scale_at]
                                       ).then_inc(S["xh_done"], 1)

                    def ffn(q):
                        ub = U_FFN[q]
                        act.preload_act_table_set(EXP_LN)
                        act.wait_ge(S["ss_done"], 2 * q + 1)
                        rsqrt(rF[:, :], bank[3][:, :], 1.0 / D).then_inc(S["r_done"], 1)
                        act.preload_act_table_set(SILU)
                        with act.Fori(0, NF // 2) as i:
                            for fs in range(2):
                                act.wait_ge(S["g_free"], NF * q + 2 * i + (fs + 3))
                                act.activation(sg[fs][:, :], sg[fs][:, :], ACT.Silu).then_inc(S["gs_done"], 1)
                            split_hi(0, landed_value(ub + 2) + 16 * i, 0)
                            for fs in range(2):
                                act.wait_ge(S["u_free"], NF * q + 2 * i + (fs + 3))
                                act.activation(HH[:, 2 * i + fs, :], hf[fs][:, :], ACT.Copy
                                               ).then_inc(S["hh_done"], 1)
                            split_hi(1, landed_value(ub + 3) + 16 * i, 1)
                        if q:
                            act.wait_ge(S["xl_done"], 2 * KD)
                            load_columns(act, (L + 1) % depth, S["cols_in"])
                            act.wait_ge(S["cols_in"], 16 * COL_DMAS)
                        with act.Fori(0, 2) as i:
                            for r in range(DN_UNITS // 2):
                                dp, part = divmod(r, 3)
                                if part < 2:
                                    act.wait_ge(S["w_used"], DN_UNITS * 2 // 3 * q + 4 * i + (2 * dp + part + 1))
                                else:
                                    act.wait_ge(S["dn_done"], 2 * KD * q + 4 * i + (2 * dp + 2))
                                split_hi(0, landed_value(ub + GU_UNITS + r + 2) + 48 * i, r % 2)
                                if part == 2:
                                    for d in range(2):
                                        c = 2 * dp + d
                                        act.wait_ge(S["x_up"], 2 * KD * q + 4 * i + (4 + c + 1))
                                        hi_of_x(1 - q, 4 * i + c, bass.ds(4 * i + c, 1))

                    def evac(gi):
                        g = GROUPS[gi]
                        act.wait_ge(S["pj_done"], gi + 1)
                        name, c, b, src = g["name"], g.get("c"), g.get("b"), bank[gi % 2]
                        if name == "mk":
                            act.activation(mkT[:, c, :], src[:, 0:NM], ACT.Copy).then_inc(S["ev_act"], 1)
                        elif name == "mv":
                            act.activation(mvN[:, b, :], src[:, 0:WM], ACT.Copy).then_inc(S["ev_act"], 1)
                        else:
                            dst = dvN[:, b, 0:256] if name == "va" else dvN[:, b, 256:WA]
                            act.activation(dst, src[:, 0:g["n"]], ACT.Copy, scale=rcol[:, b:b + 1]
                                           ).then_inc(S["ev_act"], 1)

                    def wait_copied(gi):
                        sem, n = copied(gi)
                        act.wait_ge(S[sem], n)

                    def square_of(nj, ap, n):
                        if nj >= 2:
                            act.wait_ge(S["nq_done"], nj - 1)
                        act.activation(nsq[nj % 2][:, 0:n], ap, ACT.Square).then_inc(S["nq_sq"], 1)

                    def head_rsqrt(nj, n, scale):
                        act.wait_ge(S["nq_ss"], nj + 1)
                        rsqrt(nrr[nj % 2][:, 0:n], bank[2 + nj % 2][:, 0:n], scale).then_inc(S["nq_r"], 1)

                    def index_relu():
                        for n in range(3 * H_I):
                            b = 1 + n // H_I
                            act.wait_ge(S["sc_done"], n + 1)
                            if n >= 2:
                                act.wait_ge(S["acc_done"], n - 1)
                            act.activation(rl[n % 2][:, 0:P * (b + 1)], bank[4 + n % 2][:, 0:P * (b + 1)], ACT.Relu,
                                           scale=D_I ** -0.5).then_inc(S["relu_done"], 1)

                    def hook(gi):
                        if gi == GATE_GROUP:
                            index_relu()
                        if gi == 7:
                            act.wait_ge(S["sp_e"], 1)
                            chain.step(act.activation(tmpb, tmpb, ACT.Exp))
                            chain.step(act.activation(gdnp[:, 0, :], gdnp[:, 0, :], ACT.Exp))
                            chain.step(act.activation(tmpc, tmpc, ACT.Exp))
                            chain.join()
                            act.activation(tmpb, tmpb, ACT.Ln, bias=one).then_inc(S["sp_b"], 1)
                        if gi == 9:
                            act.wait_ge(S["gc_ps"], 1)
                            ps = [bank[7][:, 32 * i:32 * i + 24] for i in range(2)]
                            flat = [t.rearrange("p b h -> p (b h)") for t in (gcum, bg, kdec)]
                            chain.step(act.activation(flat[0], ps[0], ACT.Copy))
                            chain.step(act.activation(flat[1], ps[0], ACT.Exp))
                            chain.step(act.activation(flat[2], ps[1], ACT.Exp))
                            chain.join()
                            act.sem_inc(S["gc_ready"], 1)
                        if gi == 11:
                            act.wait_ge(S["row_ps"], 1)
                            chain.step(act.activation(rowb[:, :], bank[6][0:H_B, :], ACT.Copy))
                            chain.step(act.activation(rowg[:, :], bank[7][0:H_B, :], ACT.Copy))
                            chain.join()
                            act.sem_inc(S["row_ready"], 1)
                            act.wait_ge(S["mem_in"], 16)
                            for m in range(2):
                                chain.step(act.activation(MH[:, 4 * m:4 * m + 4, :], memN[:, m, :], ACT.Square,
                                                          accum_out=memr[:, m:m + 1]))
                            chain.join()
                            rsqrt(memr[:, :], memr[:, :], 1.0 / D).then_inc(S["mem_r"], 1)
                        if gi in (14, 16):
                            for t in range(gi - 14, gi - 12):
                                act.wait_ge(S["mem_t"], t + 1)
                                for k in range(2 * t, 2 * t + 2):
                                    chain.step(act.activation(MH[:, k, :], bank[6 + t % 2][:, (k % 2) * NM:(k % 2) * NM + NM],
                                                              ACT.Copy, scale=gain[:, 3, k:k + 1]))
                                chain.join()
                                act.sem_inc(S["mem_hi"], 1)

                    def gdn(b, step):
                        e_pe, e_dve, e_pool = b * N_PE, b * N_DVE, b * N_POOL

                        def sig(ins):
                            ins.then_inc(S["gd_act"], 1)
                        flat = "p a b c -> p (a b c)"
                        if step == S_ROWS:
                            act.wait_ge(S["gd_pe"], e_pe + 1)
                            if b:
                                act.wait_ge(S["gd_pool"], e_pool)
                            sig(act.activation(EGr.rearrange("p a b -> p (a b)"), bank[6][:, 0:3 * P], ACT.Exp))
                            act.wait_ge(S["gd_pe"], e_pe + 2)
                            sig(act.activation(DT.rearrange(flat), bank[7][:, 0:WB], ACT.Exp))
                        elif step == S_INV:
                            for par in range(2):
                                act.wait_ge(S["iv_t"], 2 * b + par + 1)
                                act.activation(X[:, par].rearrange("p a c -> p (a c)"), bank[6 + par][:, 0:3 * P],
                                               ACT.Copy).then_inc(S["iv_x0"], 1)
                        elif S_LEVEL <= step < S_UW and (step - S_LEVEL) % 4 < 2:
                            j, par = (step - S_LEVEL) // 4 + 1, (step - S_LEVEL) % 4
                            act.wait_ge(S["iv_yp"], level_count(b, j, par))
                            act.activation(Y[:, par].rearrange("p a c -> p (a c)"), bank[5][:, 0:3 * P], ACT.Copy
                                           ).then_inc(S["iv_y"], 1)
                        elif step == S_UW:
                            act.wait_ge(S["gd_pe"], e_pe + 6)
                            chain.step(act.activation(WT.rearrange("p a c -> p (a c)"), bank[6][:, 0:3 * P],
                                                      ACT.Copy))
                            chain.step(act.activation(U.rearrange("p h d -> p (h d)"), bank[5][:, 0:WB], ACT.Copy))
                            chain.join()
                            act.sem_inc(S["gd_act"], 1)
                        elif step == S_OUT:
                            act.wait_ge(S["gd_pe"], e_pe + 14)
                            sig(act.activation(Y[:, 0].rearrange("p a c -> p (a c)"), bank[5][:, 0:WB], ACT.Square))
                            act.wait_ge(S["gd_dve"], e_dve + 11)
                            sig(rsqrt(oss[:, :], oss[:, :], 1.0 / DH))
                        elif step == S_OUT + 2:
                            act.wait_ge(S["gd_dve"], e_dve + 13)
                            sig(act.activation(XH[:, 3:6, b * P:(b + 1) * P], kbT[:, :, :], ACT.Copy))

                    def attention(slot):
                        n = slot - 4
                        if 0 <= n < N_JOBS and n % JOBS in (H_A - 1, JOBS - 1):
                            b, ph = n // JOBS, int(n % JOBS == JOBS - 1)
                            act.wait_ge(S["o_t"], 2 * b + ph + 1)
                            c0, c1 = (6, 8) if ph else (0, 3)
                            act.activation(XH[:, c0:c1, b * P:(b + 1) * P],
                                           bank[4][:, 0:P * (c1 - c0)].rearrange("p (c t) -> p c t", t=P),
                                           ACT.Copy).then_inc(S["o_hi"], 1)
                        n = slot - 1
                        if 0 <= n < N_JOBS:
                            b, j = divmod(n, JOBS)
                            w = P * (b + 1) if j < H_A else NM
                            act.wait_ge(S["jm_done"], n + 1)
                            act.activation(at[n % 2][:, 0:w], at[n % 2][:, 0:w], ACT.Exp,
                                           bias=mxs[:, n % 2, 1:2], accum_out=rsum[:, j:j + 1]
                                           ).then_inc(S["je_done"], 1)
                        n = slot
                        if n < N_JOBS:
                            b, j = divmod(n, JOBS)
                            w = P * (b + 1) if j < H_A else NM
                            act.wait_ge(S["jl_done"], n + 1)
                            if n >= 2:
                                act.wait_ge(S["jtr_done"], n - 1)
                            bias = far[:, j:j + 1] if j < H_A else zero
                            act.activation(at[n % 2][:, 0:w], bank[n % 2][:, 0:w], ACT.Identity, bias=bias,
                                           scale=DH ** -0.5).then_inc(S["jt_done"], 1)

                    ffn(0)
                    act.preload_act_table_set(EXP_LN)
                    act.wait_ge(S["ss_done"], 2)
                    rsqrt(rM[:, :], bank[3][:, :], 1.0 / D).then_inc(S["act_chain"], 1)
                    chain.n += 1
                    rsqrt(rcol[:, :], bank[7][:, 0:NB], 1.0 / D).then_inc(S["act_chain"], 1)
                    chain.n += 1
                    chain.join()
                    act.sem_inc(S["r_done"], 1)
                    for gi in range(N_GROUPS):
                        g = GROUPS[gi]
                        if copied(gi)[0] == "ev_act":
                            evac(gi)
                        if gi - 1 in NORM_OF:
                            head_rsqrt(NORM_OF[gi - 1], NM if GROUPS[gi - 1]["name"] == "mk" else T, 1.0 / DH)
                        if gi in NORM_OF:
                            wait_copied(gi)
                            c = g["c"]
                            square_of(NORM_OF[gi], mkT[:, c, :] if g["name"] == "mk" else
                                      {"dq": dqT, "dk": dkT, "mq": mqT}[g["name"]][:, c, :],
                                      NM if g["name"] == "mk" else T)
                        if gi - 1 in GNORM_AT:
                            for i in range(2):
                                head_rsqrt(N_NORM_A + 2 * GNORM_AT.index(gi - 1) + i, T, 1.0)
                        if gi == GNORM_AT[0]:
                            act.wait_ge(S["conv_done"], 6)
                            for t in (gqT, gkT):
                                f = t.rearrange("p c t -> p (c t)")
                                act.activation(f, f, ACT.Silu).then_inc(S["silu_done"], 1)
                            act.preload_act_table_set(EXP_LN)
                            act.wait_ge(S["silu_done"], 2)
                        if gi in GNORM_AT:
                            for i in range(2):
                                n = 2 * GNORM_AT.index(gi) + i
                                square_of(N_NORM_A + n, (gqT if n < 3 else gkT)[:, n % 3, :], T)
                        hook(gi)
                        u = g["unit"]
                        if LAST_OF_UNIT[u] == gi:
                            act.wait_ge(S["pj_done"], gi + 1)
                            split_hi(u + 2, landed_value(u + 2), u % 2)
                    act.wait_ge(S["conv_done"], 9)
                    wait_copied(N_GROUPS - 1)
                    for t in (gvT, gzT):
                        f = t.rearrange("p c t -> p (c t)")
                        act.activation(f, f, ACT.Silu).then_inc(S["silu_done"], 1)
                    act.preload_act_table_set(EXP_LN)
                    act.wait_ge(S["v_done"], NB)
                    act.wait_ge(S["nq_done"], N_NORM_A + 6)
                    for b in range(NB):
                        for step in range(N_STEPS):
                            gdn(b, step)
                            if step in JOB_SLOT:
                                attention(len(SLOT_STEPS) * b + JOB_SLOT[step])
                    for i in range(4):
                        act.wait_ge(S["dn_done"], KD + 2 * i + 2)
                        split_hi(0, landed_value(U_MIX + 18 + i), i % 2)
                    act.wait_ge(S["dn_done"], 2 * KD)
                    for k in range(KD):
                        act.wait_ge(S["x_up"], 4 + KD + k + 1)
                        hi_of_x(2, k, slice(k, k + 1))
                    ffn(1)

                @block.vector
                def _(dve):
                    chain = Chain(dve, S["dve_chain"])

                    def split_lo(v, slot, upto=KD):
                        dve.wait_ge(S["w_hi"], v - 1)
                        dve.tensor_tensor(wl[slot][:, 0:upto, :], raw[slot][:, 0:upto, :],
                                          wh[slot][:, 0:upto, :].bitcast(F32), ALU.subtract
                                          ).then_inc(S["w_lo"], 1)

                    def lo_of_x(p, k, scale_at, done):
                        dve.wait_ge(S["xh_done"], done)
                        dve.scalar_tensor_tensor(XL[:, k, :], xT[:, k, :], gain[:, p, scale_at],
                                                 XH[:, k, :].bitcast(F32), ALU.mult, ALU.subtract
                                                 ).then_inc(S["xl_done"], 1)

                    def ffn(q):
                        ub = U_FFN[q]
                        dve.wait_ge(S["r_done"], 2 * q + 1)
                        with dve.Fori(0, NF // 2) as i:
                            for fs in range(2):
                                f1 = NF * q + 2 * i + (fs + 1)
                                dve.wait_ge(S["gate_done"], f1)
                                dve.wait_ge(S["u_free"], f1)
                                dve.tensor_tensor(sg[fs][:, :], bank[fs][:, :], rF[:, :], ALU.mult
                                                  ).then_inc(S["g_free"], 1)
                            split_lo(ub + 2 * i + 2, 0)
                            for fs in range(2):
                                f1 = NF * q + 2 * i + (fs + 1)
                                dve.wait_ge(S["up_done"], f1)
                                dve.wait_ge(S["gr_done"], f1)
                                dve.tensor_tensor(hf[fs][:, :], sg[fs][:, :], bank[2 + fs][:, :], ALU.mult
                                                  ).then_inc(S["u_free"], 1)
                                dve.wait_ge(S["hh_done"], NF * q + 2 * i + (fs + 1))
                                dve.tensor_tensor(HL[:, 2 * i + fs, :], hf[fs][:, :],
                                                  HH[:, 2 * i + fs, :].bitcast(F32), ALU.subtract
                                                  ).then_inc(S["hl_done"], 1)
                            split_lo(ub + 2 * i + 3, 1)
                        with dve.Fori(0, 2) as i:
                            for r in range(DN_UNITS // 2):
                                if r % 3 == 2:
                                    for d in range(2):
                                        c = 2 * (r // 3) + d
                                        dve.wait_ge(S["dn_done"], 2 * KD * q + 4 * i + (c + 1))
                                        dve.scalar_tensor_tensor(xT[:, 4 * i + c, :], bank[4 + c][:, :], 0.5,
                                                                 xT[:, 4 * i + c, :], ALU.mult, ALU.add
                                                                 ).then_inc(S["x_up"], 1)
                                split_lo(ub + GU_UNITS + 6 * i + (r + 2), r % 2)
                                if r % 3 == 2:
                                    for d in range(2):
                                        c = 2 * (r // 3) + d
                                        lo_of_x(1 - q, 4 * i + c, bass.ds(4 * i + c, 1),
                                                2 * KD * q + 4 * i + (c + 1))

                    def norm_apply(nj, ap, n, factor):
                        dve.wait_ge(S["nq_r"], nj + 1)
                        dve.scalar_tensor_tensor(ap, ap, factor, nrr[nj % 2][:, 0:n], ALU.mult, ALU.mult
                                                 ).then_inc(S["nq_done"], 1)

                    def index_sum():
                        for n in range(3 * H_I):
                            b, h = 1 + n // H_I, n % H_I
                            w = P * (b + 1)
                            dve.wait_ge(S["relu_done"], n + 1)
                            if h == 0:
                                ins = dve.tensor_scalar(acc[b][:, :], rl[n % 2][:, 0:w], wI[:, b, h:h + 1], None,
                                                        ALU.mult)
                            else:
                                dve.wait_ge(S["acc_done"], n)
                                ins = dve.scalar_tensor_tensor(acc[b][:, :], rl[n % 2][:, 0:w], wI[:, b, h:h + 1],
                                                               acc[b][:, :], ALU.mult, ALU.add)
                            ins.then_inc(S["acc_done"], 1)
                        dve.wait_ge(S["acc_done"], 3 * H_I)
                        for b in range(1, NB):
                            last = acc[b][:, P * b:P * (b + 1)]
                            chain.step(dve.tensor_tensor(last, last, const("causal"), ALU.add))

                    def selection():
                        for b in range(1, NB):
                            w = P * (b + 1)
                            for r in range(TOPK // 8):
                                src = acc[b][:, :] if r == 0 else wrk[:, 0:w]
                                chain.join()
                                chain.step(dve.max(m8[:, :], src))
                                chain.join()
                                chain.step(dve.match_replace(wrk[:, 0:w], m8[:, :], src, GONE))
                                if r == TOPK // 8 - 1:
                                    chain.join()
                                    chain.step(dve.tensor_tensor(unsel[b][:, :], wrk[:, 0:w], acc[b][:, :],
                                                                 ALU.is_equal))
                                    chain.join()
                                    chain.step(dve.tensor_scalar(unsel[b][:, :], unsel[b][:, :], NEG, None,
                                                                 ALU.mult))
                                yield

                    def conv(n):
                        dst = (gqT, gkT, gvT)[n // 3][:, n % 3, :]
                        wait_copied(FIRST_CONV + n)
                        src = cv[n % 2]
                        chain.step(dve.tensor_scalar(dst, src[:, 0:T], convw[:, 0, n:n + 1], None, ALU.mult))
                        for i in range(1, CONV):
                            chain.join()
                            ins = dve.scalar_tensor_tensor(dst, src[:, i:i + T], convw[:, i, n:n + 1], dst,
                                                           ALU.mult, ALU.add)
                            if i < CONV - 1:
                                chain.step(ins)
                        ins.then_inc(S["conv_done"], 1)

                    def wait_copied(gi):
                        sem, n = copied(gi)
                        dve.wait_ge(S[sem], n)

                    def evac(gi):
                        g = GROUPS[gi]
                        dve.wait_ge(S["pj_done"], gi + 1)
                        name, c, src = g["name"], g.get("c"), bank[gi % 2]
                        if name == "sm":
                            dve.tensor_tensor(smT[:, :], src[0:SM, :], rM[0:SM, :], ALU.mult
                                              ).then_inc(S["ev_dve"], 1)
                            return
                        if name == "ik":
                            for h in range(4):
                                ins = dve.scalar_tensor_tensor(ikz[:, h, :], src[:, :], const("quarter")[:, h:h + 1],
                                                               rM[:, :], ALU.mult, ALU.mult)
                            ins.then_inc(S["ev_dve"], 1)
                            return
                        if name in ("gq", "gk", "gv"):
                            n = gi - FIRST_CONV
                            if n == 0:
                                dve.wait_ge(S["mem_t"], 4)
                                dve.wait_ge(S["pool_chain"], 2)
                            if n >= 2:
                                dve.wait_ge(S["conv_done"], n - 1)
                            dst = cv[n % 2][:, CONV - 1:]
                        else:
                            dst = {"iq": iqT, "dq": dqT, "dk": dkT, "mq": mqT, "gz": gzT}[name][:, c, :]
                        dve.tensor_tensor(dst, src[:, :], rM[:, :], ALU.mult).then_inc(S["ev_dve"], 1)

                    def hook(gi):
                        if gi == GATE_GROUP:
                            dve.wait_ge(S["sm_t"], 1)
                            chain.step(dve.tensor_copy(sm.rearrange("p b n -> p (b n)"), bank[6][:, 0:NB * SM]))
                            chain.join()
                            chain.step(dve.tensor_scalar(wI[:, :, :], sm[:, :, 0:H_I], H_I ** -0.5, None, ALU.mult))
                            chain.join()
                            index_sum()
                            dtb = bcast(gdnp[:, 1, :], 1, NB)
                            chain.step(dve.tensor_tensor(tmpa, sm[:, :, H_I:H_I + H_B], dtb, ALU.add))
                            chain.step(dve.tensor_scalar(tmpc, sm[:, :, H_I + H_B:SM], -1.0, 85.0, ALU.mult, ALU.min))
                            chain.join()
                            chain.step(dve.tensor_scalar(tmpb, tmpa, -1.0, None, ALU.mult))
                            chain.join()
                            dve.tensor_tensor(tmpb, tmpb, tmpa, ALU.min).then_inc(S["sp_e"], 1)
                        if gi == 7:
                            dve.wait_ge(S["sp_b"], 1)
                            chain.step(dve.scalar_tensor_tensor(tmpa, tmpa, 0.0, tmpb, ALU.max, ALU.add))
                            chain.step(dve.tensor_scalar(tmpc, tmpc, 1.0, None, ALU.add))
                            chain.join()
                            chain.step(dve.reciprocal(beta, tmpc))
                            chain.step(dve.scalar_tensor_tensor(gdec, tmpa, -1.0, bcast(gdnp[:, 0, :], 1, NB),
                                                                ALU.mult, ALU.mult))
                            chain.join()
                            dve.sem_inc(S["g_ready"], 1)
                        if gi == 10:
                            dve.wait_ge(S["gc_ready"], 1)
                            chain.step(dve.tensor_tensor(bg, bg, beta, ALU.mult))
                        if gi == 12:
                            dve.wait_ge(S["mem_r"], 1)
                            for m in range(2):
                                chain.step(dve.tensor_scalar(memN[:, m, :], memN[:, m, :], memr[:, m:m + 1], None,
                                                             ALU.mult))
                            chain.join()
                            dve.sem_inc(S["mem_n"], 1)
                        if gi in (14, 16):
                            for t in range(gi - 14, gi - 12):
                                dve.wait_ge(S["mem_hi"], t + 1)
                                for k in range(2 * t, 2 * t + 2):
                                    ps = bank[6 + t % 2][:, (k % 2) * NM:(k % 2) * NM + NM]
                                    chain.step(dve.scalar_tensor_tensor(ML[:, k, :], ps, gain[:, 3, k:k + 1],
                                                                        MH[:, k, :].bitcast(F32), ALU.mult,
                                                                        ALU.subtract))
                                chain.join()
                                dve.sem_inc(S["mem_lo"], 1)

                    def gdn(b, step):
                        e_pe, e_act, e_dve, e_pool = b * N_PE, b * N_ACT, b * N_DVE, b * N_POOL
                        rows = [slice(0, DH), slice(DH, P)]
                        pc = "p (a c) -> p a c"

                        def sig(ins):
                            ins.then_inc(S["gd_dve"], 1)

                        def three_heads(t):
                            return t.rearrange("p a b c -> p (a b) c")
                        heads = [P, H_B, DH]
                        if step == S_ROWS:
                            g = gdec[:, b, :].rearrange("p (b a) -> p a b", a=2)
                            for par in range(2):
                                ins = dve.tensor_tensor(TG[:, par, :, :], bcast(const("upper64"), 1, 3),
                                                        g[:, par, :].unsqueeze(2).to_broadcast([P, 3, DH]), ALU.mult)
                                if par:
                                    sig(ins)
                            dve.wait_ge(S["gd_pe"], e_pe + 1)
                            if b:
                                dve.wait_ge(S["gd_dve"], e_dve)
                            sig(dve.tensor_tensor(kbT[:, :, :], gkT[:, :, b * P:(b + 1) * P],
                                                  bank[5][:, 0:3 * P].rearrange(pc, a=3), ALU.mult))
                            dve.wait_ge(S["gd_act"], e_act + 2)
                            sig(dve.tensor_tensor(three_heads(DT), three_heads(DT), bcast(const("upper64"), 1, H_B),
                                                  ALU.mult))
                        elif step == S_DECAY:
                            dve.wait_ge(S["gd_pe"], e_pe + 3)
                            k = bank[5][:, 0:WB].rearrange(pc, a=H_B)
                            dve.tensor_tensor(kbg[:, :, :], k, bg[:, b, :].unsqueeze(2).to_broadcast(heads), ALU.mult)
                            sig(dve.tensor_tensor(kdc[:, :, :], k, kdec[:, b, :].unsqueeze(2).to_broadcast(heads),
                                                  ALU.mult))
                        elif step in (S_KK, S_QK):
                            dve.wait_ge(S["gd_pe"], e_pe + (4 if step == S_KK else 5))
                            dve.wait_ge(S["gd_dve"], e_dve + 3)
                            dst = LT if step == S_KK else AT
                            for par in range(2):
                                ins = dve.tensor_tensor(dst[:, par], bank[6 + par][:, 0:3 * DH].rearrange(pc, a=3),
                                                        DT[:, par], ALU.mult)
                            sig(ins)
                        elif step == S_INV:
                            dve.wait_ge(S["gd_dve"], e_dve + 5)
                            for par in range(2):
                                if b and not par:
                                    dve.wait_ge(S["gd_pe"], e_pe)
                                chain.step(dve.tensor_tensor(XT[:, par].rearrange("p a (h c) -> p a h c", h=2),
                                                             bcast(LT[:, par], 2, 2),
                                                             bcast(const("level0").rearrange("p (h c) -> p h c", h=2),
                                                                   1, 3), ALU.mult))
                                chain.join()
                                dve.tensor_tensor(XT[:, par], bcast(const("ident"), 1, 3), XT[:, par], ALU.subtract
                                                  ).then_inc(S["iv_xt0"], 1)
                        elif S_LEVEL <= step < S_UW and (step - S_LEVEL) % 4 >= 2:
                            j, par = (step - S_LEVEL) // 4 + 1, (step - S_LEVEL) % 2
                            if j < LEVELS - 1:
                                dve.wait_ge(S["iv_xp"], level_count(b, j, par, levels=LEVELS - 2))
                                f = X[:, par].rearrange("p a c -> p (a c)")
                                dve.tensor_tensor(f, f, bank[6][:, 0:3 * P], ALU.subtract).then_inc(S["iv_xu"], 1)
                            dve.wait_ge(S["iv_xtp"], level_count(b, j, par))
                            f = XT[:, par].rearrange("p a c -> p (a c)")
                            dve.tensor_tensor(f, f, bank[7][:, 0:3 * P], ALU.subtract).then_inc(S["iv_xtu"], 1)
                        elif S_REC <= step < S_OUT:
                            ch, second = divmod(step - S_REC, 2)
                            r = rows[ch]
                            if not second:
                                dve.wait_ge(S["gd_pe"], e_pe + 7 + 4 * ch)
                                dve.wait_ge(S["gd_act"], e_act + 3)
                                u = U[r, :, :].rearrange("p h d -> p (h d)")
                                sig(dve.tensor_tensor(u, u, bank[6][r, 0:WB], ALU.subtract))
                            else:
                                dve.wait_ge(S["gd_pe"], e_pe + 9 + 4 * ch)
                                dve.wait_ge(S["gd_pool"], e_pool + 2 + ch)
                                s = bank[7][:, 0:3 * P].rearrange(pc, a=3)
                                for h in range(2):
                                    q = rows[h]
                                    ins = dve.tensor_tensor(Sbd[q, :, q], Sdec[q, :, q], s[q, :, q], ALU.add)
                                sig(ins)
                        elif step == S_OUT:
                            dve.wait_ge(S["gd_act"], e_act + 4)
                            sig(dve.tensor_reduce(oss[:, :], Y[:, 0].rearrange("p a (h c) -> p (a h) c", h=2), AX.X,
                                                  ALU.add))
                            dve.wait_ge(S["gd_act"], e_act + 5)
                            sig(dve.tensor_tensor(oG[:, :, :], bank[5][:, 0:WB].rearrange(pc, a=H_B),
                                                  oss[:, :].unsqueeze(2).to_broadcast(heads), ALU.mult))
                        elif step == S_OUT + 1:
                            dve.wait_ge(S["gd_pe"], e_pe + 15)
                            sig(dve.scalar_tensor_tensor(kbT[:, :, :], bank[6][:, 0:3 * P].rearrange(pc, a=3),
                                                         hgain[:, 4:5], gzT[:, :, b * P:(b + 1) * P],
                                                         ALU.mult, ALU.mult))
                        elif step == S_OUT + 2:
                            dve.wait_ge(S["gd_act"], e_act + 6)
                            sl = (slice(None), slice(3, 6), slice(b * P, (b + 1) * P))
                            sig(dve.tensor_tensor(XL[sl], kbT[:, :, :], XH[sl].bitcast(F32), ALU.subtract))

                    def attention(slot):
                        n = slot - 4
                        if 0 <= n < N_JOBS and n % JOBS in (H_A - 1, JOBS - 1):
                            b, ph = n // JOBS, int(n % JOBS == JOBS - 1)
                            c0, c1 = (6, 8) if ph else (0, 3)
                            dve.wait_ge(S["o_hi"], 2 * b + ph + 1)
                            sl = (slice(None), slice(c0, c1), slice(b * P, (b + 1) * P))
                            dve.tensor_tensor(XL[sl], bank[4][:, 0:P * (c1 - c0)].rearrange("p (c t) -> p c t", t=P),
                                              XH[sl].bitcast(F32), ALU.subtract).then_inc(S["o_lo"], 1)
                        n = slot - 2
                        if 0 <= n < N_JOBS:
                            b, j = divmod(n, JOBS)
                            w = P * (b + 1) if j < H_A else NM
                            dve.wait_ge(S["jtr_done"], n + 1)
                            if n >= 2:
                                dve.wait_ge(S["jv_done"], n - 1)
                            dve.tensor_copy(pT[n % 2][:, 0:w], bank[2 + n % 2][:, 0:w]).then_inc(S["jp_done"], 1)
                        n = slot
                        if n < N_JOBS:
                            b, j = divmod(n, JOBS)
                            w = P * (b + 1) if j < H_A else NM
                            t = at[n % 2]
                            m = mxs[:, n % 2, 0:1]
                            dve.wait_ge(S["jt_done"], n + 1)
                            if j < H_A:
                                near = min(w, 256)
                                chain.step(dve.tensor_tensor(t[:, w - near:w], t[:, w - near:w],
                                                             strips[:, j, 256 - near:256], ALU.add))
                                chain.join()
                                mask = unsel[b][:, :] if b else const("causal")
                                chain.step(dve.tensor_tensor_reduce(out=t[:, 0:w], in0=t[:, 0:w], in1=mask,
                                                                    scale=1.0, scalar=GONE, op0=ALU.add,
                                                                    op1=ALU.max, accum_out=m))
                            else:
                                chain.step(dve.tensor_reduce(m, t[:, 0:w], AX.X, ALU.max))
                            chain.join()
                            dve.tensor_scalar(mxs[:, n % 2, 1:2], m, -1.0, None, ALU.mult).then_inc(S["jm_done"], 1)
                        n = slot - 3
                        if 0 <= n < N_JOBS and n % JOBS in (H_A - 1, JOBS - 1):
                            b, ph = n // JOBS, int(n % JOBS == JOBS - 1)
                            j0, nh = (H_A, H_M) if ph else (0, H_A)
                            dve.wait_ge(S["je_done"], n + 1)
                            chain.step(dve.reciprocal(rrec[:, j0:j0 + nh], rsum[:, j0:j0 + nh]))
                            chain.join()
                            dve.wait_ge(S["jv_done"], n + 1)
                            r = rrec[:, j0:j0 + nh].unsqueeze(2).to_broadcast([P, nh, DH])
                            dve.tensor_tensor(oA[:, 0:nh * DH].rearrange("p (h d) -> p h d", h=nh),
                                              bank[4][:, 0:nh * DH].rearrange("p (h d) -> p h d", h=nh), r,
                                              ALU.mult).then_inc(S["o_ev"], 1)

                    dve.sem_inc(S["w_lo"], 2)
                    dve.sem_inc(S["u_free"], 2)
                    dve.sem_inc(S["g_free"], 2)
                    dve.sem_inc(S["x_up"], 4)
                    ffn(0)
                    dve.wait_ge(S["r_done"], 2)
                    rounds = selection()
                    gcols = {"dq": 0, "dk": 1, "mq": 2, "mk": 3}
                    for gi in range(N_GROUPS):
                        if copied(gi)[0] == "ev_dve":
                            evac(gi)
                        if gi - 1 in GNORM_AT:
                            for i in range(2):
                                n = 2 * GNORM_AT.index(gi - 1) + i
                                norm_apply(N_NORM_A + n, (gqT if n < 3 else gkT)[:, n % 3, :], T,
                                           DH ** -0.5 if n < 3 else 1.0)
                        if gi - 1 in NORM_OF:
                            g = GROUPS[gi - 1]
                            name, c = g["name"], g["c"]
                            ap = {"dq": dqT, "dk": dkT, "mq": mqT, "mk": mkT}[name][:, c, :]
                            norm_apply(NORM_OF[gi - 1], ap, NM if name == "mk" else T,
                                       hgain[:, gcols[name]:gcols[name] + 1])
                        hook(gi)
                        if GATE_GROUP < gi:
                            for _ in range(2 if gi < FIRST_CONV else 1):
                                next(rounds, None)
                        if FIRST_CONV <= gi < FIRST_CONV + 9:
                            conv(gi - FIRST_CONV)
                        u = GROUPS[gi]["unit"]
                        if LAST_OF_UNIT[u] == gi:
                            split_lo(u + 2, u % 2, LO_DVE)
                    for b in range(NB):
                        dve.wait_ge(S["v_t"], b + 1)
                        dve.tensor_tensor(gvN[:, b, :].rearrange("p (h d) -> p h d", h=H_B),
                                          bank[b % 2][:, 0:WB].rearrange("p (h d) -> p h d", h=H_B),
                                          beta[:, b, :].unsqueeze(2).to_broadcast([P, H_B, DH]), ALU.mult
                                          ).then_inc(S["v_done"], 1)
                    dve.wait_ge(S["nq_done"], N_NORM_A + 6)
                    dve.wait_ge(S["strip_in"], 16)
                    for b in range(NB):
                        for step in range(N_STEPS):
                            gdn(b, step)
                            if step in JOB_SLOT:
                                attention(len(SLOT_STEPS) * b + JOB_SLOT[step])
                    for c in range(KD):
                        dve.wait_ge(S["dn_done"], KD + c + 1)
                        dve.tensor_tensor(xT[:, c, :], bank[4 + c % 4][:, :], xT[:, c, :], ALU.add
                                          ).then_inc(S["x_up"], 1)
                        if c % 2:
                            split_lo(U_MIX + 18 + c // 2, (c // 2) % 2)
                    for k in range(KD):
                        lo_of_x(2, k, slice(k, k + 1), KD + k + 1)
                    ffn(1)

            first = min(S[n].num for n in SEMAPHORES)
            nc.all_engine_barrier(sems_to_clear=range(first, first + len(SEMAPHORES)))

        fin = [ctx.enter_context(nc.semaphore(n)) for n in ("fin_t", "fin_cp", "fin_out")]
        with nc.Block() as block:
            @block.tensor
            def _(pe):
                for n in range(2 * NB):
                    b, half = divmod(n, 2)
                    if n >= 2:
                        pe.wait_ge(fin[1], n - 1)
                    for c in range(4):
                        mm = pe.transpose(bank[n % 2][:, c * P:(c + 1) * P],
                                          xT[:, 4 * half + c, b * P:(b + 1) * P], const("ident"))
                    mm.then_inc(fin[0], 1)

            @block.vector
            def _(dve):
                for n in range(2 * NB):
                    b, half = divmod(n, 2)
                    dve.wait_ge(fin[0], n + 1)
                    dve.tensor_copy(xnat[:, b, 512 * half:512 * half + 512], bank[n % 2][:, :]
                                    ).then_inc(fin[1], 1)

            @block.sync
            def _(sp):
                for b in range(NB):
                    sp.wait_ge(fin[1], 2 * b + 2)
                    sp.dma_start(out[0, b * P:(b + 1) * P, :], xnat[:, b, :]).then_inc(fin[2], 16)
                sp.wait_ge(fin[2], 16 * NB)


INPUTS = ["x", "mem", "ffn1_norm", "ffn1_w_gate", "ffn1_w_up", "ffn1_w_down", "mix_norm", "w_in",
          "dsa_q_norm", "dsa_k_norm", "rel_bias", "gdn_conv", "gdn_A_log", "gdn_dt_bias",
          "gdn_out_norm", "mem_norm", "w_mem_kv", "mem_q_norm", "mem_k_norm", "w_out",
          "ffn2_norm", "ffn2_w_gate", "ffn2_w_up", "ffn2_w_down"]


def kernel(**inputs):
    import concourse.bacc as bacc
    from concourse.bass_utils import run_bass_kernel_spmd

    nc = bacc.Bacc("TRN2", target_bir_lowering=False, num_devices=1)
    arrays = {f"in_{n}": np.ascontiguousarray(inputs[n]) for n in INPUTS}
    arrays["masks"] = np.ascontiguousarray(np.concatenate(list(CONSTS.values()), axis=1))
    arrays["hot_rows"] = bucket_rows()
    args = [nc.dram_tensor(n, a.shape, mybir.dt.from_np(a.dtype), kind="ExternalInput").ap()
            for n, a in arrays.items()]
    args.append(nc.dram_tensor("out", inputs["x"].shape, F32, kind="ExternalOutput").ap())
    hybrid_trunk(nc, *args)
    got = run_bass_kernel_spmd(nc, [arrays], core_ids=[0])
    return got.results[0]["out"]
```
